# Optimizing a Trainium2 kernel written in Bass

```python
import jax
import jax.numpy as jnp
from jax import lax
import numpy as np

D_MODEL = 1024
BATCH = 1
SEQ = 512
DEPTH = 1

N_HEADS = 8
HEAD_DIM = 64
ATTN_WIDTH = N_HEADS * HEAD_DIM
MOBA_BLOCK = 256
MOBA_TOPK = 3
Q_CHUNK = 32
SGU_CHUNK = 128
SGU_GROUPS = 8
SGU_WIDTH = D_MODEL // 2
SGU_GROUP_DIM = SGU_WIDTH // SGU_GROUPS
N_BRANCHES = 2
IN_WIDTH = 3 * ATTN_WIDTH + 2 * SGU_WIDTH + N_BRANCHES * D_MODEL
N_EXPERTS = 32
EXPERT_TOPK = 4
D_EXPERT = D_MODEL
SWIGLU_LIMIT = 7.0
SWIGLU_ALPHA = 1.702
ROW_BLOCK = 128
NORM_EPS = 1e-5

kernel_name = "hybrid_moba_gmlp_moe_layer"

def rms_norm(x, g):
    xf = x.astype(jnp.float32)
    y = xf * lax.rsqrt(jnp.mean(xf * xf, axis=-1, keepdims=True) + NORM_EPS)
    return (y * g.astype(jnp.float32)).astype(x.dtype)

def layer_norm(x, g, b):
    xf = x.astype(jnp.float32)
    mu = jnp.mean(xf, axis=-1, keepdims=True)
    var = jnp.mean(jnp.square(xf - mu), axis=-1, keepdims=True)
    y = (xf - mu) * lax.rsqrt(var + NORM_EPS) * g.astype(jnp.float32) + b.astype(jnp.float32)
    return y.astype(x.dtype)

def alibi_slopes(n_heads):
    return 2.0 ** (-8.0 * jnp.arange(1, n_heads + 1, dtype=jnp.float32) / n_heads)

def moba_attention(q, k, v):
    b, s, h, dh = q.shape
    nb = -(-s // MOBA_BLOCK)
    s_pad = nb * MOBA_BLOCK
    pad = [(0, 0), (0, s_pad - s), (0, 0), (0, 0)]
    q, k, v = [jnp.pad(t, pad).transpose(0, 2, 1, 3) for t in (q, k, v)]
    k_blk = k.reshape(b, h, nb, MOBA_BLOCK, dh)
    v_blk = v.reshape(b, h, nb, MOBA_BLOCK, dh)
    k_mean = jnp.mean(k_blk.astype(jnp.float32), axis=3)
    pos = jnp.arange(s_pad, dtype=jnp.int32)
    q_blk_id = pos // MOBA_BLOCK
    gate = jnp.einsum('bhtd,bhnd->bhtn', q.astype(jnp.float32), k_mean)
    past = jnp.arange(nb, dtype=jnp.int32)[None, :] < q_blk_id[:, None]
    gate = jnp.where(past, gate, -jnp.inf)
    n_sel = min(MOBA_TOPK, nb)
    _, sel_idx = lax.top_k(gate, n_sel)
    sel_valid = jnp.arange(n_sel, dtype=jnp.int32)[None, :] < q_blk_id[:, None]

    n_chunks = s_pad // Q_CHUNK
    slopes = alibi_slopes(h)
    scale = dh ** -0.5
    q_c = q.reshape(b, h, n_chunks, Q_CHUNK, dh).transpose(2, 0, 1, 3, 4)
    idx_c = sel_idx.reshape(b, h, n_chunks, Q_CHUNK, n_sel).transpose(2, 0, 1, 3, 4)
    valid_c = sel_valid.reshape(n_chunks, Q_CHUNK, n_sel)
    b_ix = jnp.arange(b)[:, None, None, None]
    h_ix = jnp.arange(h)[None, :, None, None]
    offs = jnp.arange(MOBA_BLOCK, dtype=jnp.int32)

    def one_chunk(args):
        c, qc, ic, vc = args
        t = c * Q_CHUNK + jnp.arange(Q_CHUNK, dtype=jnp.int32)
        own = (c * Q_CHUNK) // MOBA_BLOCK
        k_sel = k_blk[b_ix, h_ix, ic]
        v_sel = v_blk[b_ix, h_ix, ic]
        k_own = lax.dynamic_index_in_dim(k_blk, own, axis=2, keepdims=False)
        v_own = lax.dynamic_index_in_dim(v_blk, own, axis=2, keepdims=False)
        s_sel = jnp.einsum('bhqd,bhqnld->bhqnl', qc, k_sel, preferred_element_type=jnp.float32) * scale
        s_own = jnp.einsum('bhqd,bhld->bhql', qc, k_own, preferred_element_type=jnp.float32) * scale
        sel_pos = ic[..., None] * MOBA_BLOCK + offs
        own_pos = own * MOBA_BLOCK + offs
        s_sel = s_sel - slopes[:, None, None, None] * (t[:, None, None] - sel_pos).astype(jnp.float32)
        s_sel = jnp.where(vc[None, None, :, :, None], s_sel, -jnp.inf)
        s_own = s_own - slopes[:, None, None] * (t[:, None] - own_pos[None, :]).astype(jnp.float32)
        s_own = jnp.where(own_pos[None, :] <= t[:, None], s_own, -jnp.inf)
        scores = jnp.concatenate([s_sel.reshape(b, h, Q_CHUNK, n_sel * MOBA_BLOCK), s_own], axis=-1)
        p = jax.nn.softmax(scores, axis=-1).astype(v.dtype)
        p_sel = p[..., :n_sel * MOBA_BLOCK].reshape(b, h, Q_CHUNK, n_sel, MOBA_BLOCK)
        p_own = p[..., n_sel * MOBA_BLOCK:]
        return (jnp.einsum('bhqnl,bhqnld->bhqd', p_sel, v_sel)
                + jnp.einsum('bhql,bhld->bhqd', p_own, v_own))

    out = lax.map(one_chunk, (jnp.arange(n_chunks, dtype=jnp.int32), q_c, idx_c, valid_c))
    out = out.transpose(1, 0, 3, 2, 4).reshape(b, s_pad, h * dh)
    return out[:, :s]

def spatial_gating(z, ln_g, ln_b, w_s, b_s):
    u, vv = jnp.split(z, 2, axis=-1)
    vv = layer_norm(vv, ln_g, ln_b)
    b, s, _ = vv.shape
    nc = s // SGU_CHUNK
    vv = vv.reshape(b, nc, SGU_CHUNK, SGU_GROUPS, SGU_GROUP_DIM)
    causal = jnp.tril(jnp.ones((SGU_CHUNK, SGU_CHUNK), dtype=bool))
    w = jnp.where(causal[None], w_s, jnp.zeros_like(w_s))
    mixed = jnp.einsum('gts,bcsgd->bctgd', w, vv) + b_s.T[None, None, :, :, None]
    return u * mixed.reshape(b, s, SGU_WIDTH)

def clamped_swiglu(gu):
    gate, up = gu[..., 0::2], gu[..., 1::2]
    gate = jnp.minimum(gate, SWIGLU_LIMIT)
    up = jnp.clip(up, -SWIGLU_LIMIT, SWIGLU_LIMIT)
    return gate * jax.nn.sigmoid(SWIGLU_ALPHA * gate) * (up + 1.0)

def moe_ffn(x, w_router, b_router, w_gate_up, b_gate_up, w_down, b_down):
    b, s, d = x.shape
    n_tok = b * s
    xt = x.reshape(n_tok, d)
    logits = (xt @ w_router + b_router).astype(jnp.float32)
    top_val, top_idx = lax.top_k(logits, EXPERT_TOPK)
    top_w = jax.nn.softmax(top_val, axis=-1)
    n_assign = n_tok * EXPERT_TOPK
    flat_e = top_idx.reshape(n_assign).astype(jnp.int32)
    flat_tok = jnp.repeat(jnp.arange(n_tok, dtype=jnp.int32), EXPERT_TOPK)
    flat_w = top_w.reshape(n_assign)
    order = jnp.argsort(flat_e)
    e_sorted = flat_e[order]
    counts = jnp.bincount(flat_e, length=N_EXPERTS).astype(jnp.int32)
    padded = (counts + ROW_BLOCK - 1) // ROW_BLOCK * ROW_BLOCK
    pad_end = jnp.cumsum(padded)
    pad_start = pad_end - padded
    grp_start = jnp.cumsum(counts) - counts
    dest = pad_start[e_sorted] + jnp.arange(n_assign, dtype=jnp.int32) - grp_start[e_sorted]
    n_blocks = -(-(n_assign + N_EXPERTS * (ROW_BLOCK - 1)) // ROW_BLOCK)
    n_rows = n_blocks * ROW_BLOCK
    row_tok = jnp.zeros((n_rows,), jnp.int32).at[dest].set(flat_tok[order])
    row_w = jnp.zeros((n_rows,), jnp.float32).at[dest].set(flat_w[order])
    block_start = jnp.arange(n_blocks, dtype=jnp.int32) * ROW_BLOCK
    block_expert = jnp.minimum(jnp.searchsorted(pad_end, block_start, side='right'), N_EXPERTS - 1)
    x_rows = xt[row_tok].reshape(n_blocks, ROW_BLOCK, d)

    def expert_block(args):
        e, xb = args
        hid = clamped_swiglu(xb @ w_gate_up[e] + b_gate_up[e])
        return hid @ w_down[e] + b_down[e]

    y_rows = lax.map(expert_block, (block_expert, x_rows)).reshape(n_rows, d)
    out = jax.ops.segment_sum(y_rows.astype(jnp.float32) * row_w[:, None], row_tok, num_segments=n_tok)
    return out.astype(x.dtype).reshape(b, s, d)

def setup_inputs(seed: int = 0) -> dict:
    key = jax.random.key(seed)
    ks = jax.random.split(key, 20)
    f32 = jnp.float32
    nrm = lambda k, shape, fan_in: jax.random.normal(k, shape, f32) * (fan_in ** -0.5)
    L = DEPTH
    return {
        "x": jax.random.normal(ks[0], (BATCH, SEQ, D_MODEL), f32),
        "mix_norm_g": 1.0 + 0.05 * jax.random.normal(ks[1], (L, D_MODEL), f32),
        "w_in": nrm(ks[2], (L, D_MODEL, IN_WIDTH), D_MODEL),
        "w_attn_out": nrm(ks[3], (L, ATTN_WIDTH, D_MODEL), ATTN_WIDTH),
        "sgu_ln_g": 1.0 + 0.05 * jax.random.normal(ks[4], (L, SGU_WIDTH), f32),
        "sgu_ln_b": 0.01 * jax.random.normal(ks[5], (L, SGU_WIDTH), f32),
        "w_spatial": nrm(ks[6], (L, SGU_GROUPS, SGU_CHUNK, SGU_CHUNK), SGU_CHUNK),
        "b_spatial": 1.0 + 0.01 * jax.random.normal(ks[7], (L, SGU_GROUPS, SGU_CHUNK), f32),
        "w_sgu_out": nrm(ks[8], (L, SGU_WIDTH, D_MODEL), SGU_WIDTH),
        "w_mix_out": nrm(ks[9], (L, D_MODEL, D_MODEL), D_MODEL),
        "ffn_norm_g": 1.0 + 0.05 * jax.random.normal(ks[10], (L, D_MODEL), f32),
        "w_router": nrm(ks[11], (L, D_MODEL, N_EXPERTS), D_MODEL),
        "b_router": 0.01 * jax.random.normal(ks[12], (L, N_EXPERTS), f32),
        "w_gate_up": nrm(ks[13], (L, N_EXPERTS, D_MODEL, 2 * D_EXPERT), D_MODEL),
        "b_gate_up": 0.01 * jax.random.normal(ks[14], (L, N_EXPERTS, 2 * D_EXPERT), f32),
        "w_down": nrm(ks[15], (L, N_EXPERTS, D_EXPERT, D_MODEL), D_EXPERT),
        "b_down": 0.01 * jax.random.normal(ks[16], (L, N_EXPERTS, D_MODEL), f32),
        "final_norm_g": 1.0 + 0.05 * jax.random.normal(ks[17], (D_MODEL,), f32),
    }

def reference(x, mix_norm_g, w_in, w_attn_out, sgu_ln_g, sgu_ln_b, w_spatial, b_spatial, w_sgu_out,
              w_mix_out, ffn_norm_g, w_router, b_router, w_gate_up, b_gate_up, w_down, b_down,
              final_norm_g):
    b, s, _ = x.shape
    h = x
    splits = [ATTN_WIDTH, 2 * ATTN_WIDTH, 3 * ATTN_WIDTH, 3 * ATTN_WIDTH + 2 * SGU_WIDTH]
    for layer in range(DEPTH):
        xn = rms_norm(h, mix_norm_g[layer])
        proj = xn @ w_in[layer]
        q, k, v, z, gates = jnp.split(proj, splits, axis=-1)
        q = q.reshape(b, s, N_HEADS, HEAD_DIM)
        k = k.reshape(b, s, N_HEADS, HEAD_DIM)
        v = v.reshape(b, s, N_HEADS, HEAD_DIM)
        y_attn = moba_attention(q, k, v) @ w_attn_out[layer]
        y_sgu = spatial_gating(jax.nn.gelu(z, approximate=False), sgu_ln_g[layer], sgu_ln_b[layer],
                               w_spatial[layer], b_spatial[layer]) @ w_sgu_out[layer]
        g_attn, g_sgu = jnp.split(jax.nn.sigmoid(gates), 2, axis=-1)
        h = h + (g_attn * y_attn + g_sgu * y_sgu) @ w_mix_out[layer]
        h = h + moe_ffn(rms_norm(h, ffn_norm_g[layer]), w_router[layer], b_router[layer],
                        w_gate_up[layer], b_gate_up[layer], w_down[layer], b_down[layer])
    return rms_norm(h, final_norm_g)


_drawn_inputs = setup_inputs


def setup_inputs(seed=0):
    import zlib

    import numpy as np

    out = dict(_drawn_inputs(seed))
    spreads = {}
    factors = {'sgu_ln_b': 3.551, 'b_spatial': 3.743, 'b_gate_up': 8.0, 'b_down': 8.0}
    for name, (base, spread) in spreads.items():
        noise = np.random.default_rng([zlib.crc32(name.encode()), seed]).standard_normal(out[name].shape)
        drawn = base * np.exp(spread * noise) if base else spread * noise
        out[name] = jnp.asarray(drawn.astype(out[name].dtype))
    for name, factor in factors.items():
        out[name] = (out[name] * factor).astype(out[name].dtype)
    return out
```

```python
from contextlib import ExitStack

import concourse.bass as bass
from concourse import mybir

F32 = mybir.dt.float32
F32R = mybir.dt.float32r
BF16 = mybir.dt.bfloat16
I32 = mybir.dt.int32
U32 = mybir.dt.uint32
ALU = mybir.AluOpType
ACT = mybir.ActivationFunctionType
AX_X = mybir.AxisListType.X

P = 128
D = 1024
KD = D // P
SEQ = 512
TT = SEQ // P
HEADS, HD = 8, 64
ATTN_W = HEADS * HD
SGU_W = D // 2
GROUPS = 8
E = 32
TOPK = 4
EPS = 1e-5
LIMIT, ALPHA = 7.0, 1.702
FAR = -1.0e30
SKIP = 65536.0

PIECE = 2048
N_IN = (3 * ATTN_W + 2 * SGU_W + 2 * D) // 256
N_MIX = N_IN + 2 + 2 + D // 256
RAW_A, SPLIT_A = 3, 2
RAW_B, SPLIT_B = 6, 4
PER_E = 12
GU_P = 8
MAX_OVER = (SEQ * TOPK) // (P + 1)
BLOCKS = 48
IDENT, DIST, ONES1, ROUTE_CONSTS = 2, 4, 5, 13
assert E + MAX_OVER < BLOCKS and PER_E % RAW_B == 0 and PER_E % SPLIT_B == 0


def build(nc, x, mix_norm_g, w_in, w_attn_out, sgu_ln_g, sgu_ln_b, w_spatial, b_spatial, w_sgu_out, w_mix_out,
          ffn_norm_g, w_router, b_router, w_gate_up, b_gate_up, w_down, b_down, final_norm_g, out):
    ctx = ExitStack()
    with ctx:
        base = -(-nc.sbuf_base // 64) * 64
        count = [0]

        def at(offset, shape, dt, name):
            count[0] += 1
            return nc.alloc_sbuf_tensor_at(name, shape, dt, offset=base + offset)

        K = 1024
        raw = [at(8 * K * s, [P, PIECE], F32, f"raw{s}") for s in range(RAW_A)]
        whi = [at(24 * K + 8 * K * s, [P, PIECE], F32R, f"whi{s}") for s in range(SPLIT_A)]
        wlo = [at(40 * K + 8 * K * s, [P, PIECE], F32R, f"wlo{s}") for s in range(SPLIT_A)]
        h2 = at(56 * K, [P, TT, D], F32, "h2")
        qT = at(56 * K, [P, HEADS // 2, SEQ], F32, "qT")
        kT = at(64 * K, [P, HEADS // 2, SEQ], F32, "kT")
        S0 = 72 * K
        small_at = [S0]

        def small(shape, dt, name):
            n = 1
            for v in shape[1:]:
                n *= v
            size = -(-n * (2 if dt == BF16 else 4) // 64) * 64
            t = at(small_at[0], shape, dt, name)
            small_at[0] += size
            return t

        ident = small([P, P], F32, "ident")
        gcol = small([P, KD], F32, "gcol")
        fcol = small([P, KD], F32, "fcol")
        stat = small([P, 4, 8], F32, "stat")
        bn = small([P, TT, 6], F32, "bn")
        mv = small([P, TT, 2], F32, "mv")
        negmax = small([P, 2, 4], F32, "negmax")
        rowsum = small([P, 2, 4], F32, "rowsum")
        rinv = small([P, 2, 4], F32, "rinv")
        top8 = small([P, TT, 8], F32, "top8")
        idx8 = small([P, TT, 8], U32, "idx8")
        topw = small([P, TT, TOPK], F32, "topw")
        wsum = small([P, TT], F32, "wsum")
        xidx = small([P, BLOCKS], I32, "xidx")
        yidx = small([P, BLOCKS], I32, "yidx")
        expert_of = small([P, BLOCKS], I32, "expert_of")
        n_blocks = small([P, 1], I32, "n_blocks")
        cur_x = small([P, 1], I32, "cur_x")
        cur_y = small([P, 1], I32, "cur_y")
        brow = small([1, E], F32, "brow")
        ones1 = small([1, P], F32, "ones1")
        assert small_at[0] <= 76 * K, small_at[0]

        A0 = 76 * K
        xnh = at(A0, [P, KD, SEQ], F32R, "xnh")
        xnl = at(A0 + 16 * K, [P, KD, SEQ], F32R, "xnl")
        gates = at(A0 + 32 * K, [P, 2 * KD, SEQ], F32, "gates")
        x_in = at(A0 + 32 * K, [P, TT, D], F32, "x_in")
        xn = at(A0 + 48 * K, [P, TT, D], F32, "xn")
        v = at(A0 + 64 * K, [P, TT, ATTN_W], F32, "v")
        sgh = at(A0 + 64 * K, [P, 4, SEQ], F32R, "sgh")
        prob = at(A0 + 72 * K, [P, 1280], F32, "prob")
        probT = at(A0 + 77 * K, [P, 1280], F32, "probT")
        sgl = at(A0 + 72 * K, [P, 4, SEQ], F32R, "sgl")
        u = at(A0 + 82 * K, [P, 4, SEQ], F32, "u")
        vv = at(A0 + 90 * K, [P, TT, SGU_W], F32, "vv")
        wsp = at(A0 + 90 * K, [P, GROUPS, P], F32, "wsp")
        ah = at(A0 + 98 * K, [P, HEADS // 2, SEQ], F32R, "ah")
        al = at(A0 + 106 * K, [P, HEADS // 2, SEQ], F32R, "al")
        wspT = at(A0 + 114 * K, [P, GROUPS, P], F32, "wspT")
        dist = at(A0 + 118 * K, [P, SEQ], F32, "dist")
        lng = at(A0 + 120 * K, [P, SGU_W], F32, "lng")
        lnb = at(A0 + 122 * K, [P, SGU_W], F32, "lnb")
        bsp = at(A0 + 124 * K, [P, 4, P], F32, "bsp")
        assert 76 + 126 <= 207

        R0 = A0 + 64 * K
        hn = at(R0, [P, TT, D], F32, "hn")
        hnT = at(R0 + 16 * K, [P, KD, SEQ], F32, "hnT")
        wr = at(R0 + 32 * K, [P, KD, E], F32, "wr")
        rt_at = [R0 + 33 * K]

        def rt(shape, dt, name):
            n = 1
            for w in shape[1:]:
                n *= w
            t = at(rt_at[0], shape, dt, name)
            rt_at[0] += -(-n * (2 if dt == BF16 else 4) // 64) * 64
            return t

        logits = rt([P, TT, E], F32, "logits")
        idxf = rt([P, TT, TOPK], F32, "idxf")
        iota_e = rt([P, 48], F32, "iota_e")
        iota_s = rt([P, P], F32, "iota_s")
        pcol = rt([P, 1], F32, "pcol")
        kcol = rt([P, 16], F32, "kcol")
        pick = rt([P, 16, E], F32, "pick")
        prod = rt([P, 16, E], F32, "prod")
        chosen = rt([P, TT, E], BF16, "chosen")
        before = rt([P, P], BF16, "before")
        onesb = rt([P, P], BF16, "onesb")
        cnt = rt([P, E], F32, "cnt")
        ones_e = rt([P, E], F32, "ones_e")
        spill = rt([P, E], F32, "spill")
        incl = rt([P, E], F32, "incl")
        first = rt([P, E], F32, "first")
        pos = rt([P, TT, E], F32, "pos")
        lap = rt([P, TT, E], F32, "lap")
        blk = rt([P, TT, E], F32, "blk")
        tmp1 = rt([P, TT, E], F32, "tmp1")
        rslot = rt([P, 16], F32, "rslot")
        rblk = rt([P, 16], F32, "rblk")
        hot_s = rt([P, 16, P], BF16, "hot_s")
        hot_b = rt([P, 16, 48], F32, "hot_b")
        hot_v = rt([P, 16, 96], BF16, "hot_v")
        tab = rt([P, 96], F32, "tab")
        row = rt([P, 48], F32, "row")
        rnk = rt([P, 48], F32, "rnk")
        skp = rt([P, 48], F32, "skp")
        own = rt([P, BLOCKS], F32, "own")
        ended = at(R0 + 16 * K, [P, BLOCKS, E], F32, "ended")
        exf = rt([P, BLOCKS], F32, "exf")
        nbf = rt([P, 1], F32, "nbf")
        assert rt_at[0] <= A0 + 119 * K, rt_at[0] - A0

        raw_b = raw + [at(A0 + 32 * K + 8 * K * s, [P, PIECE], F32, f"raw{3 + s}") for s in range(RAW_B - RAW_A)]
        whi_b = whi + [at(A0 + 8 * K * s, [P, PIECE], F32R, f"whi{2 + s}") for s in range(SPLIT_B - SPLIT_A)]
        wlo_b = wlo + [at(A0 + 16 * K + 8 * K * s, [P, PIECE], F32R, f"wlo{2 + s}") for s in range(SPLIT_B - SPLIT_A)]
        biasr = at(A0 + 119 * K, [2 * E, 3 * D], F32, "biasr")
        selh = at(A0 + 56 * K, [2 * E, P], F32R, "selh")
        seld = at(A0 + 56 * K + 512, [2 * E, P], F32R, "seld")
        selt = at(A0 + 57 * K, [2 * E, BLOCKS], F32, "selt")
        xgat = at(A0 + 60 * K, [P, D], F32, "xgat")
        B0 = A0 + 64 * K
        xth = at(B0, [P, KD, P], F32R, "xth")
        xtl = at(B0 + 4 * K, [P, KD, P], F32R, "xtl")
        hth = at(B0 + 8 * K, [P, KD, P], F32R, "hth")
        htl = at(B0 + 12 * K, [P, KD, P], F32R, "htl")
        hid = at(B0 + 16 * K, [P, D], F32, "hid")
        gm = at(B0 + 20 * K, [P, D], F32, "gm")
        um = at(B0 + 24 * K, [P, D], F32, "um")
        sg = at(B0 + 28 * K, [P, D], F32, "sg")
        yb = at(B0 + 32 * K, [P, D], F32, "yb")
        bias = at(B0 + 36 * K, [2 * E, 3 * D], F32R, "bias")
        gfin = at(A0 + 124 * K, [P, D], F32, "gfin")

        ps = ctx.enter_context(nc.psum_tensor("ps", [P, 8, 512], F32))
        hn_dram = nc.dram_tensor("hn_dram", (SEQ, D), F32).ap()
        y_dram = nc.dram_tensor("y_dram", (SEQ * TOPK, D), F32).ap()

        def sem(name):
            return ctx.enter_context(nc.semaphore(name))

        raw_landed = [sem(f"raw_landed{s}") for s in range(RAW_B)]
        x_loaded = [sem(f"x_loaded{t}") for t in range(TT)]
        consts_loaded = sem("consts_loaded")
        wsp_loaded = sem("wsp_loaded")
        x_again = sem("x_again")
        bias_loaded = sem("bias_loaded")
        wr_loaded = sem("wr_loaded")
        high_made, low_made, piece_used = sem("high_made"), sem("low_made"), sem("piece_used")
        pool_made = sem("pool_made")
        dve_step = sem("dve_step")
        sum_made, root_made, xn_made = sem("sum_made"), sem("root_made"), sem("xn_made")
        xT_turned, xnh_made, xnl_made = sem("xT_turned"), sem("xnh_made"), sem("xnl_made")
        wsp_turned, wspT_made, wsp_masked = sem("wsp_turned"), sem("wspT_made"), sem("wsp_masked")
        task_done, act_evac, dve_evac = sem("task_done"), sem("act_evac"), sem("dve_evac")
        scores_ready, max_made, exp_made, prob_made = sem("scores_ready"), sem("max_made"), sem("exp_made"), sem("prob_made")
        prob_turned, probT_made, head_done, ah_made, al_made = (sem("prob_turned"), sem("probT_made"),
                                                                sem("head_done"), sem("ah_made"), sem("al_made"))
        ln_var, ln_root, ln_made = sem("ln_var"), sem("ln_root"), sem("ln_made")
        sg_sum, sgh_made, sgl_made = sem("sg_sum"), sem("sgh_made"), sem("sgl_made")
        sigm_made, merged, mh_made, ml_made = sem("sigm_made"), sem("merged"), sem("mh_made"), sem("ml_made")
        h2_sum, h2_root, hn_made, hn_stored = sem("h2_sum"), sem("h2_root"), sem("hn_made"), sem("hn_stored")
        hn_turned, hnT_made, logits_done, chosen_made = (sem("hn_turned"), sem("hnT_made"), sem("logits_done"),
                                                         sem("chosen_made"))
        counted, hot_made, table_done, tables_ready = sem("counted"), sem("hot_made"), sem("table_done"), sem("tables_ready")
        exps_in, exps_out = sem("exps_in"), sem("exps_out")
        bias_made = sem("bias_made")
        idx_copied, idx_seen, x_landed, y_stored = sem("idx_copied"), sem("idx_seen"), sem("x_landed"), sem("y_stored")
        selh_made, seld_made = sem("selh_made"), sem("seld_made")
        x_turned, xth_made, xtl_made = sem("x_turned"), sem("xth_made"), sem("xtl_made")
        gu_done, gate_made, up_made, sig_made, gu_mult, hid_made = (
            sem("gu_done"), sem("gate_made"), sem("up_made"), sem("sig_made"), sem("gu_mult"), sem("hid_made"))
        hid_turned, hth_made, htl_made = sem("hid_turned"), sem("hth_made"), sem("htl_made")
        y_done, y_made, yb_free = sem("y_done"), sem("y_made"), sem("yb_free")
        y_loaded = [sem(f"y_loaded{s}") for s in range(RAW_B)]
        acc_made, fin_sum, fin_root, fin_made, out_stored = (sem("acc_made"), sem("fin_sum"), sem("fin_root"),
                                                             sem("fin_made"), sem("out_stored"))

        x2 = x[0].rearrange("(t p) d -> t p d", p=P)
        out2 = out[0].rearrange("(t p) d -> t p d", p=P)
        win = w_in[0].rearrange("(k p) (n c) -> n p k c", p=P, c=256)
        wao = w_attn_out[0].rearrange("(k p) (n c) -> n p k c", p=P, c=512)
        wso = w_sgu_out[0].rearrange("(k p) (n c) -> n p k c", p=P, c=512)
        wmo = w_mix_out[0].rearrange("(k p) (n c) -> n p k c", p=P, c=256)
        hn_d = hn_dram.rearrange("(t p) d -> t p d", p=P)
        y_d = y_dram.rearrange("(r t p) d -> t p r d", r=TOPK, p=P)
        slope = [2.0 ** (-8.0 * (h + 1) / HEADS) for h in range(HEADS)]

        def piece_source(n):
            if n < N_IN:
                return win[n], 8
            if n < N_IN + 2:
                return wao[n - N_IN], 4
            if n < N_IN + 4:
                return wso[n - N_IN - 2], 4
            return wmo[n - N_IN - 4], 8

        def mix_slot(n):
            k = piece_source(n)[1]
            return (whi[n % SPLIT_A][:].rearrange("p (k c) -> p k c", k=k),
                    wlo[n % SPLIT_A][:].rearrange("p (k c) -> p k c", k=k))

        M0 = N_MIX
        task_piece = ([n for n in range(N_IN) for _ in range(2)] + [None] * 4
                      + [n for n in range(N_IN, N_IN + 4) for _ in range(4)] + [n for n in range(N_IN + 4, N_MIX) for _ in range(2)])
        ends_piece = [p is not None and (i + 1 == len(task_piece) or task_piece[i + 1] != p) for i, p in enumerate(task_piece)]

        def wait_task(eng, task):
            if ends_piece[task]:
                eng.wait_ge(piece_used, task_piece[task] + 1)
            else:
                eng.wait_ge(task_done, sum(not x for x in ends_piece[:task + 1]))

        sc_ps = {3: (4, 0), 2: (5, 0), 0: (5, 384), 1: (6, 0)}
        sc_sb = {0: 0, 1: 128, 2: 384, 3: 768}
        pt_at = {0: 0, 1: 512, 3: 896, 2: 1024}
        ps46 = ps[:, 4:7, :].rearrange("p b c -> p (b c)")
        gu_ps = ps[:, 0:4, :].rearrange("p b c -> p (b c)").rearrange("p (c two) -> p two c", two=2)
        t_ps = ps[:, 4:6, :].rearrange("p b c -> p (b c)")
        y_ps = ps[:, 6:8, :].rearrange("p b c -> p (b c)")

        block = ctx.enter_context(nc.Block())

        @block.sync
        def _(sp):
            def expert_source(e, j):
                if j < GU_P:
                    return w_gate_up[0][e, j * P:(j + 1) * P, :]
                return w_down[0][e, (j - GU_P) * 256:(j - GU_P + 1) * 256, :].rearrange("(p two) c -> p (two c)", two=2)

            for t in range(TT):
                sp.dma_start(x_in[:, t, :], x2[t]).then_inc(x_loaded[t], 16)
            for n in range(N_MIX):
                src, k = piece_source(n)
                if n >= RAW_A:
                    sp.wait_ge(low_made, n - RAW_A + 1)
                sp.dma_start(raw[n % RAW_A][:].rearrange("p (k c) -> p k c", k=k), src).then_inc(raw_landed[n % RAW_A], 16)
                if n == 2:
                    sp.dma_start(gcol[:], mix_norm_g[0].rearrange("(k p) -> p k", p=P),
                                 allow_slow_non_contiguous=True).then_inc(consts_loaded, 16)
                    sp.dma_start(fcol[:], ffn_norm_g[0].rearrange("(k p) -> p k", p=P),
                                 allow_slow_non_contiguous=True).then_inc(consts_loaded, 16)
                    sp.dma_start(wsp[:], w_spatial[0].rearrange("g t s -> t g s")).then_inc(wsp_loaded, 16)
                    sp.dma_start(lng[:], sgu_ln_g[0].rearrange("(o c) -> o c", o=1).broadcast_to((P, SGU_W))).then_inc(consts_loaded, 16)
                    sp.dma_start(lnb[:], sgu_ln_b[0].rearrange("(o c) -> o c", o=1).broadcast_to((P, SGU_W))).then_inc(consts_loaded, 16)
                    for g in range(GROUPS):
                        q = (g % 2) * 64
                        sp.dma_start(bsp[q:q + 64, g // 2, :], b_spatial[0][g:g + 1, :].broadcast_to((64, P))).then_inc(consts_loaded, 16)
                    sp.dma_start(brow[:], b_router[0].rearrange("(o c) -> o c", o=1)).then_inc(consts_loaded, 16)
                if n == N_IN + 3:
                    sp.wait_ge(head_done, HEADS)
                    sp.dma_start(h2[:], x[0].rearrange("(t p) d -> p t d", p=P)).then_inc(x_again, 16)

            def expert_piece(n, e, j, m):
                s = j_slot(m)
                if m is not None and m < RAW_B:
                    if m < RAW_A:
                        last = max(i for i in range(N_MIX) if i % RAW_A == m)
                        sp.wait_ge(low_made, last + 1)
                    else:
                        sp.wait_ge(ml_made, KD)
                    s = m
                else:
                    sp.wait_ge(low_made, n - RAW_B + 1)
                sp.dma_start(raw_b[s][:], expert_source(e, j)).then_inc(raw_landed[s], 16)

            def j_slot(m):
                return m % RAW_B

            for m in range(GU_P):
                expert_piece(M0 + m, 0, m, m)
            sp.wait_ge(tables_ready, 1)
            nb = sp.value_load(n_blocks[0:1, 0:1], min_val=E, max_val=E + MAX_OVER)
            with sp.Fori(1, nb) as e:
                now = sp.value_load(expert_of[0:1, bass.ds(e, 1)], min_val=0, max_val=E - 1)
                past = sp.value_load(expert_of[0:1, bass.ds(e - 1, 1)], min_val=0, max_val=E - 1)
                for j in range(PER_E):
                    sp.wait_ge(low_made, M0 + GU_P + (e - 1) * PER_E + j - RAW_B + 1)
                    s = (GU_P + j) % RAW_B
                    sp.dma_start(raw_b[s][:], expert_source(now if j < GU_P else past, j)).then_inc(raw_landed[s], 16)
            last = sp.value_load(expert_of[0:1, bass.ds(nb - 1, 1)], min_val=0, max_val=E - 1)
            for j in range(GU_P, PER_E):
                sp.wait_ge(low_made, nb * PER_E + (M0 + j - PER_E - RAW_B + 1))
                sp.dma_start(raw_b[j % RAW_B][:], expert_source(last, j)).then_inc(raw_landed[j % RAW_B], 16)
            sp.wait_ge(y_stored, nb * 16)
            for i in range(2 * TT):
                t, half = i // 2, i % 2
                if i >= RAW_B:
                    sp.wait_ge(acc_made, 2 * (i - RAW_B) + 2)
                sp.dma_start(raw_b[i % RAW_B][:].rearrange("p (r d) -> p r d", r=2),
                             y_d[t][:, 2 * half:2 * half + 2, :]).then_inc(y_loaded[i % RAW_B], 16)
            for t in range(TT):
                sp.wait_ge(fin_made, t + 1)
                sp.dma_start(out2[t], h2[:, t, :]).then_inc(out_stored, 16)
            sp.wait_ge(out_stored, 16 * TT)

        @block.gpsimd
        def _(pool):
            made = [0]

            def step(ins, wait=True):
                made[0] += 1
                ins.then_inc(pool_made, 1)
                if wait:
                    pool.wait_ge(pool_made, made[0])

            step(nc.gpsimd.memset(ident[:], 0.0))
            step(nc.gpsimd.affine_select(out=ident[:], in_=ident[:], compare_op=ALU.not_equal, fill=1.0, base=0,
                                         pattern=[[-1, P]], channel_multiplier=1))
            step(nc.gpsimd.iota(dist[:], pattern=[[1, SEQ]], base=-(SEQ - P), channel_multiplier=-1,
                                allow_small_or_imprecise_dtypes=True))
            step(nc.gpsimd.affine_select(out=dist[:], in_=dist[:], compare_op=ALU.is_ge, fill=FAR, base=SEQ - P,
                                         pattern=[[-1, SEQ]], channel_multiplier=1))
            step(nc.gpsimd.memset(ones1[:], 1.0))
            pool.wait_ge(wspT_made, 2)
            nc.gpsimd.affine_select(out=wspT[:], in_=wspT[:], compare_op=ALU.is_ge, fill=0.0, base=0,
                                    pattern=[[0, GROUPS], [1, P]], channel_multiplier=-1).then_inc(wsp_masked, 1)
            pool.wait_ge(piece_used, N_IN + 4)
            pool.dma_start(wr[:], w_router[0].rearrange("(k p) e -> p k e", p=P)).then_inc(wr_loaded, 16)
            for half in range(2):
                pool.dma_start(biasr[half * E:(half + 1) * E, 0:2 * D], b_gate_up[0]).then_inc(bias_loaded, 16)
                pool.dma_start(biasr[half * E:(half + 1) * E, 2 * D:3 * D], b_down[0]).then_inc(bias_loaded, 16)
            pool.wait_ge(ml_made, KD)
            step(nc.gpsimd.iota(iota_e[:], pattern=[[1, 48]], base=0, channel_multiplier=0,
                                allow_small_or_imprecise_dtypes=True))
            step(nc.gpsimd.iota(iota_s[:], pattern=[[1, P]], base=0, channel_multiplier=0,
                                allow_small_or_imprecise_dtypes=True))
            step(nc.gpsimd.iota(pcol[:], pattern=[[1, 1]], base=0, channel_multiplier=1,
                                allow_small_or_imprecise_dtypes=True))
            step(nc.gpsimd.affine_select(out=own[:], in_=iota_e[:], compare_op=ALU.is_ge, fill=0.0, base=E - 1,
                                         pattern=[[-1, BLOCKS]], channel_multiplier=0))
            step(nc.gpsimd.iota(kcol[:], pattern=[[1, TT], [TT, TOPK]], base=1, channel_multiplier=0,
                                allow_small_or_imprecise_dtypes=True))
            step(nc.gpsimd.memset(onesb[:], 1.0))
            step(nc.gpsimd.memset(ones_e[:], 1.0))
            step(nc.gpsimd.affine_select(out=before[:], in_=onesb[:], compare_op=ALU.is_gt, fill=0.0, base=0,
                                         pattern=[[1, P]], channel_multiplier=-1))
            step(nc.gpsimd.memset(selt[:], 0.0))
            step(nc.gpsimd.affine_select(out=selt[:], in_=selt[:], compare_op=ALU.not_equal, fill=1.0, base=0,
                                         pattern=[[-1, BLOCKS]], channel_multiplier=1))
            step(nc.gpsimd.affine_select(out=selt[:], in_=selt[:], compare_op=ALU.not_equal, fill=1.0, base=-E,
                                         pattern=[[-1, BLOCKS]], channel_multiplier=1))
            step(nc.gpsimd.memset(xgat[:], 0.0))

            last_token = nc.gpsimd.to_reg(SEQ - 1)
            last_row = nc.gpsimd.to_reg(SEQ * TOPK - 1)

            def gather(b, copies):
                nc.gpsimd.tensor_copy(cur_x[:], xidx[:, bass.ds(b, 1)]).then_inc(idx_copied, 1)
                pool.wait_ge(idx_copied, copies)
                pool.sem_inc(idx_seen, 1)
                pool.indirect_dma_start(out=xgat[:], out_offset=None, in_=hn_dram,
                                        in_offset=bass.IndirectOffsetOnAxis(ap=cur_x[:, 0:1].bitcast(U32), axis=0),
                                        bounds_check=last_token, oob_is_err=False).then_inc(x_landed, 16)

            def scatter(b, copies):
                nc.gpsimd.tensor_copy(cur_y[:], yidx[:, bass.ds(b, 1)]).then_inc(idx_copied, 1)
                pool.wait_ge(idx_copied, copies)
                pool.sem_inc(idx_seen, 1)
                pool.indirect_dma_start(out=y_dram, out_offset=bass.IndirectOffsetOnAxis(ap=cur_y[:, 0:1].bitcast(U32), axis=0),
                                        in_=yb[:], in_offset=None,
                                        bounds_check=last_row, oob_is_err=False).then_inc(y_stored, 16)

            def select(dst, e, signal):
                nc.gpsimd.tensor_copy(dst[:], selt[:, bass.ds(e, 1)].broadcast_to((2 * E, P))).then_inc(signal, 1)

            for t in range(TT):
                pool.wait_ge(hn_made, t + 1)
                pool.dma_start(hn_d[t], hn[:, t, :]).then_inc(hn_stored, 16)
            select(selh, 0, selh_made)
            select(seld, 0, seld_made)
            pool.wait_ge(bias_made, 2)
            pool.dma_start(gfin[:], final_norm_g.rearrange("(o c) -> o c", o=1).broadcast_to((P, D))).then_inc(bias_loaded, 16)
            pool.wait_ge(tables_ready, 1)
            pool.wait_ge(hn_stored, 16 * TT)
            gather(0, 1)
            pool.wait_ge(x_turned, 1)
            gather(1, 2)
            pool.wait_ge(gu_done, 1)
            select(selh, 1, selh_made)
            nb = pool.value_load(n_blocks[0:1, 0:1], min_val=E, max_val=E + MAX_OVER)
            with pool.Fori(1, nb) as e:
                now = pool.value_load(expert_of[0:1, bass.ds(e, 1)], min_val=0, max_val=E - 1)
                after = pool.value_load(expert_of[0:1, bass.ds(e + 1, 1)], min_val=0, max_val=E - 1)
                pool.wait_ge(x_turned, e + 1)
                pool.wait_ge(x_landed, e * 16 + 16)
                gather(e + 1, e * 2 + 1)
                pool.wait_ge(gu_done, e + 1)
                select(selh, after, selh_made)
                pool.wait_ge(y_made, e)
                scatter(e - 1, e * 2 + 2)
                select(seld, now, seld_made)
                pool.wait_ge(y_stored, e * 16)
            pool.sem_inc(yb_free, 1)
            pool.wait_ge(y_made, nb)
            scatter(nb - 1, nb * 2 + 1)
            pool.wait_ge(x_landed, nb * 16 + 16)
            pool.wait_ge(y_stored, nb * 16)

        @block.scalar
        def _(act):
            def mix_high(n):
                act.wait_ge(raw_landed[n % RAW_A], 16 * (n // RAW_A + 1))
                if n >= SPLIT_A:
                    act.wait_ge(piece_used, n - SPLIT_A + 1)
                nc.scalar.activation(whi[n % SPLIT_A][:], raw[n % RAW_A][:], ACT.Copy).then_inc(high_made, 1)

            mix_high(0)
            mix_high(1)
            for t in range(TT):
                act.wait_ge(x_loaded[t], 16)
                nc.scalar.activation(xn[:, t, :], x_in[:, t, :], ACT.Square, accum_out=stat[:, t, 0:1]).then_inc(sum_made, 1)
            act.wait_ge(sum_made, 2 * TT)
            nc.scalar.activation(stat[:, :, 2:3], stat[:, :, 1:2], ACT.Sqrt).then_inc(root_made, 1)
            act.wait_ge(consts_loaded, 16 * (4 + GROUPS + 1))
            for k in range(KD):
                act.wait_ge(xT_turned, k + 1)
                nc.scalar.activation(xnh[:, k, :], ps[:, k, :], ACT.Copy, scale=gcol[:, k:k + 1]).then_inc(xnh_made, 1)
            for c in range(2):
                act.wait_ge(wsp_turned, c + 1)
                nc.scalar.activation(wspT[:, 4 * c:4 * c + 4, :], ps[:, 4 + c, :].rearrange("p (g t) -> p g t", g=4),
                                     ACT.Copy).then_inc(wspT_made, 1)

            def evac(task):
                wait_task(act, task)
                n, c = task // 2, task % 2
                src = ps[:, task % 4, :]
                if n < 2:
                    nc.scalar.activation(qT[:, task, :], src, ACT.Copy, scale=HD ** -0.5).then_inc(act_evac, 1)
                elif n < 4:
                    nc.scalar.activation(kT[:, task - 4, :], src, ACT.Copy).then_inc(act_evac, 1)
                elif n < 6:
                    nc.scalar.activation(v[:, 2 * c:2 * c + 2, (n - 4) * 256:(n - 3) * 256],
                                         src.rearrange("p (t d) -> p t d", t=2), ACT.Copy).then_inc(act_evac, 1)
                elif n < 8:
                    nc.scalar.activation(u[:, task - 12, :], src, ACT.Gelu).then_inc(act_evac, 1)
                elif n < 10:
                    nc.scalar.activation(vv[:, 2 * c:2 * c + 2, (n - 8) * 256:(n - 7) * 256],
                                         src.rearrange("p (t d) -> p t d", t=2), ACT.Gelu).then_inc(act_evac, 1)
                else:
                    nc.scalar.activation(gates[:, task - 20, :], src, ACT.Copy).then_inc(act_evac, 1)

            for n in range(N_IN):
                if n >= 1:
                    mix_high(n + 1)
                evac(2 * n)
                ht, hs = n - 10, n - 9
                if ht >= 0:
                    act.wait_ge(prob_turned, ht + 1)
                    if ht >= 1:
                        act.wait_ge(head_done, ht)
                    nc.scalar.activation(probT[:], ps46[:, 0:1280], ACT.Copy).then_inc(probT_made, 1)
                evac(2 * n + 1)
                if n == 10:
                    act.wait_ge(ln_var, TT)
                    nc.scalar.activation(stat[:, :, 5:6], stat[:, :, 4:5], ACT.Sqrt).then_inc(ln_root, 1)
                if ht >= 0:
                    act.wait_ge(head_done, ht + 1)
                    q = (ht % 2) * 64
                    nc.scalar.activation(ah[q:q + 64, ht // 2, :], ps[q:q + 64, 7, :], ACT.Copy).then_inc(ah_made, 1)
                if 0 <= hs < HEADS:
                    for i in range(TT):
                        act.wait_ge(max_made, 4 * hs + i + 1)
                        a = sc_sb[i]
                        nc.scalar.activation(prob[:, a:a + P * (i + 1)], prob[:, a:a + P * (i + 1)], ACT.Exp,
                                             bias=negmax[:, hs % 2, i:i + 1],
                                             accum_out=rowsum[:, hs % 2, i:i + 1]).then_inc(exp_made, 1)
            act.wait_ge(act_evac, 2 * N_IN)
            for c in range(4):
                nc.scalar.activation(gates[:, 4 * c:4 * c + 4, :], gates[:, 4 * c:4 * c + 4, :], ACT.Sigmoid).then_inc(sigm_made, 1)
            mix_high(N_IN + 1)
            for g in range(4):
                act.wait_ge(sg_sum, g + 1)
                nc.scalar.activation(sgh[:, g, :], u[:, g, :], ACT.Copy).then_inc(sgh_made, 1)
            mix_high(N_IN + 2)
            mix_high(N_IN + 3)
            for d in range(KD):
                if d == 4:
                    mix_high(N_IN + 4)
                act.wait_ge(merged, d + 1)
                nc.scalar.activation(xnh[:, d, :], gates[:, d, :], ACT.Copy).then_inc(mh_made, 1)
            mix_high(N_IN + 5)
            mix_high(N_IN + 6)
            mix_high(N_IN + 7)

            def high(j, m_or_expr, s_raw, turns, free):
                act.wait_ge(raw_landed[s_raw], turns)
                act.wait_ge(piece_used, free)
                nc.scalar.activation(whi_b[j][:], raw_b[s_raw][:], ACT.Copy).then_inc(high_made, 1)

            mix_turns = [16 * len([i for i in range(N_MIX) if i % RAW_A == s]) if s < RAW_A else 0 for s in range(RAW_B)]

            def first_high(m):
                high(m % SPLIT_B, m, m % RAW_B, mix_turns[m % RAW_B] + 16 * (m // RAW_B + 1),
                     max(M0 - 2 + m + 1 if m < 2 else M0, M0 + m - SPLIT_B + 1))

            first_high(0)
            first_high(1)
            for t in range(TT):
                act.wait_ge(dve_evac, 28)
                nc.scalar.activation(hn[:, t, :], h2[:, t, :], ACT.Square, accum_out=stat[:, t, 0:1]).then_inc(h2_sum, 1)
            act.wait_ge(h2_sum, 2 * TT)
            nc.scalar.activation(stat[:, :, 2:3], stat[:, :, 1:2], ACT.Sqrt).then_inc(h2_root, 1)
            first_high(2)
            first_high(3)
            for k in range(KD):
                act.wait_ge(hn_turned, k + 1)
                nc.scalar.activation(hnT[:, k, :], ps[:, k, :], ACT.Copy, scale=fcol[:, k:k + 1]).then_inc(hnT_made, 1)
            act.wait_ge(exps_in, 1)
            nc.scalar.activation(topw[:], topw[:], ACT.Exp).then_inc(exps_out, 1)
            act.wait_ge(bias_loaded, 16 * 4)
            act.wait_ge(tables_ready, 1)
            nc.scalar.activation(bias[:], biasr[:], ACT.Copy).then_inc(bias_made, 1)

            def tokens_high(e):
                act.wait_ge(x_turned, e + 1)
                for k in range(KD):
                    ins = nc.scalar.activation(xth[:, k, :], t_ps[:, k * P:(k + 1) * P], ACT.Copy, scale=fcol[:, k:k + 1])
                ins.then_inc(xth_made, 1)

            def hidden_high(e):
                act.wait_ge(hid_turned, e + 1)
                nc.scalar.activation(hth[:], t_ps.rearrange("p (k s) -> p k s", k=KD), ACT.Copy).then_inc(hth_made, 1)

            def sigmoid(e):
                act.wait_ge(gate_made, e + 1)
                nc.scalar.activation(sg[:], gm[:], ACT.Sigmoid, scale=ALPHA).then_inc(sig_made, 1)

            def rows(e):
                act.wait_ge(y_done, e + 1)
                nc.scalar.activation(yb[:], y_ps, ACT.Copy).then_inc(y_made, 1)

            tokens_high(0)
            for m in range(4, GU_P):
                first_high(m)
            def loop_high(e, j):
                s_raw = (GU_P + j) % RAW_B
                m0 = GU_P + j
                turns = mix_turns[s_raw] + 16 * (m0 // RAW_B + 1)
                act.wait_ge(raw_landed[s_raw], (e - 1) * (16 * PER_E // RAW_B) + turns)
                act.wait_ge(piece_used, (e - 1) * PER_E + (M0 + m0 - SPLIT_B + 1))
                nc.scalar.activation(whi_b[(GU_P + j) % SPLIT_B][:], raw_b[s_raw][:], ACT.Copy).then_inc(high_made, 1)

            loop_high(1, 0)
            loop_high(1, 1)
            tokens_high(1)
            sigmoid(0)
            nb = act.value_load(n_blocks[0:1, 0:1], min_val=E, max_val=E + MAX_OVER)
            with act.Fori(1, nb) as e:
                for j in range(PER_E):
                    loop_high(e, j + 2)
                    if j == 4:
                        hidden_high(e - 1)
                    if j == 8:
                        tokens_high(e + 1)
                    if j == 10:
                        sigmoid(e)
                rows(e - 1)
            loop_high(nb, 2)
            loop_high(nb, 3)
            hidden_high(nb - 1)
            act.wait_ge(yb_free, 1)
            rows(nb - 1)
            for t in range(TT):
                act.wait_ge(acc_made, 4 * t + 4)
                nc.scalar.activation(gm[:], h2[:, t, :], ACT.Square, accum_out=stat[:, t, 0:1]).then_inc(fin_sum, 1)
                act.wait_ge(fin_sum, 2 * t + 2)
                nc.scalar.activation(stat[:, t, 2:3], stat[:, t, 1:2], ACT.Sqrt).then_inc(fin_root, 1)

        @block.vector
        def _(dve):
            steps = [0]

            def link(ins):
                steps[0] += 1
                ins.then_inc(dve_step, 1)
                dve.wait_ge(dve_step, steps[0])

            def mix_low(n):
                dve.wait_ge(high_made, n + 1)
                nc.vector.tensor_tensor(wlo[n % SPLIT_A][:], raw[n % RAW_A][:], whi[n % SPLIT_A][:].bitcast(F32),
                                        ALU.subtract).then_inc(low_made, 1)

            mix_low(0)
            mix_low(1)
            dve.wait_ge(pool_made, DIST)
            dve.wait_ge(consts_loaded, 16 * (4 + GROUPS + 1))
            for t in range(TT):
                dve.wait_ge(sum_made, TT + t)
                nc.vector.tensor_scalar(stat[:, t, 1:2], stat[:, t, 0:1], 1.0 / D, EPS, ALU.mult, ALU.add).then_inc(sum_made, 1)
            dve.wait_ge(root_made, 1)
            link(nc.vector.reciprocal(stat[:, :, 3:4], stat[:, :, 2:3]))
            for t in range(TT):
                nc.vector.tensor_scalar(xn[:, t, :], x_in[:, t, :], stat[:, t, 3:4], None, ALU.mult).then_inc(xn_made, 1)
            for k in range(KD):
                dve.wait_ge(xnh_made, k + 1)
                nc.vector.scalar_tensor_tensor(out=xnl[:, k, :], in0=ps[:, k, :], scalar=gcol[:, k:k + 1],
                                               in1=xnh[:, k, :].bitcast(F32), op0=ALU.mult, op1=ALU.subtract).then_inc(xnl_made, 1)
            for n in range(N_IN):
                if n >= 1:
                    mix_low(n + 1)
                ht, hs = n - 10, n - 9
                if n == 10:
                    dve.wait_ge(act_evac, 20)
                    for t in range(TT):
                        link(nc.vector.bn_stats(bn[:, t, :], vv[:, t, :]))
                        link(nc.vector.bn_aggr(mv[:, t, :], bn[:, t, :]))
                        nc.vector.tensor_scalar(stat[:, t, 4:5], mv[:, t, 1:2], EPS, None, ALU.add).then_inc(ln_var, 1)
                if n == 11:
                    dve.wait_ge(ln_root, 1)
                    link(nc.vector.reciprocal(stat[:, :, 6:7], stat[:, :, 5:6]))
                    for t in range(TT):
                        link(nc.vector.tensor_scalar(vv[:, t, :], vv[:, t, :], mv[:, t, 0:1], stat[:, t, 6:7],
                                                     ALU.subtract, ALU.mult))
                        link(nc.vector.tensor_tensor(vv[:, t, :], vv[:, t, :], lng[:], ALU.mult))
                        nc.vector.tensor_tensor(vv[:, t, :], vv[:, t, :], lnb[:], ALU.add).then_inc(ln_made, 1)
                if 0 <= hs < HEADS:
                    dve.wait_ge(scores_ready, hs + 1)
                    for i in range(TT):
                        w, a = P * (i + 1), sc_sb[i]
                        bank, col = sc_ps[i]
                        link(nc.vector.scalar_tensor_tensor(out=prob[:, a:a + w], in0=dist[:, SEQ - w:SEQ], scalar=slope[hs],
                                                            in1=ps[:, bank, col:col + w], op0=ALU.mult, op1=ALU.add))
                        nc.vector.tensor_reduce(negmax[:, hs % 2, i:i + 1], prob[:, a:a + w], AX_X, ALU.max,
                                                negate=True).then_inc(max_made, 1)
                if ht >= 0:
                    dve.wait_ge(ah_made, ht + 1)
                    q = (ht % 2) * 64
                    nc.vector.tensor_tensor(al[q:q + 64, ht // 2, :], ps[q:q + 64, 7, :],
                                            ah[q:q + 64, ht // 2, :].bitcast(F32), ALU.subtract).then_inc(al_made, 1)
                if 0 <= hs < HEADS:
                    dve.wait_ge(exp_made, 4 * hs + 4)
                    link(nc.vector.reciprocal(rinv[:, hs % 2, :], rowsum[:, hs % 2, :]))
                    for i in range(TT):
                        w, a = P * (i + 1), sc_sb[i]
                        nc.vector.tensor_scalar(prob[:, a:a + w], prob[:, a:a + w], rinv[:, hs % 2, i:i + 1], None,
                                                ALU.mult).then_inc(prob_made, 1)
            mix_low(N_IN + 1)
            for g in range(4):
                task = 2 * N_IN + g
                wait_task(dve, task)
                m4 = ps[:, task % 4, :].rearrange("p (c t) -> p c t", c=TT)
                nc.vector.tensor_tensor(lng[:].rearrange("p (c t) -> p c t", c=TT), m4, bsp[:, g:g + 1, :].broadcast_to((P, TT, P)),
                                        ALU.add).then_inc(dve_evac, 1)
                dve.wait_ge(dve_evac, g + 1)
                nc.vector.tensor_tensor(u[:, g, :], u[:, g, :], lng[:], ALU.mult).then_inc(sg_sum, 1)
                dve.wait_ge(sgh_made, g + 1)
                nc.vector.tensor_tensor(sgl[:, g, :], u[:, g, :], sgh[:, g, :].bitcast(F32), ALU.subtract).then_inc(sgl_made, 1)
            dve.wait_ge(sigm_made, 4)
            for d in range(KD):
                task = 2 * N_IN + 4 + d
                wait_task(dve, task)
                nc.vector.tensor_tensor(gates[:, d, :], gates[:, d, :], ps[:, task % 4, :], ALU.mult).then_inc(dve_evac, 1)
                if d % 4 == 3:
                    mix_low(N_IN + 2 + d // 4)
            for d in range(KD):
                if d == 4:
                    mix_low(N_IN + 4)
                task = 2 * N_IN + 12 + d
                wait_task(dve, task)
                nc.vector.tensor_tensor(gates[:, KD + d, :], gates[:, KD + d, :], ps[:, task % 4, :], ALU.mult).then_inc(dve_evac, 1)
                dve.wait_ge(dve_evac, 4 + KD + d + 1)
                nc.vector.tensor_tensor(gates[:, d, :], gates[:, d, :], gates[:, KD + d, :], ALU.add).then_inc(merged, 1)
                dve.wait_ge(mh_made, d + 1)
                nc.vector.tensor_tensor(xnl[:, d, :], gates[:, d, :], xnh[:, d, :].bitcast(F32), ALU.subtract).then_inc(ml_made, 1)
            mix_low(N_IN + 5)
            dve.wait_ge(x_again, 16)
            for n in range(4):
                for c in range(2):
                    task = 2 * N_IN + 20 + 2 * n + c
                    wait_task(dve, task)
                    part = h2[:, 2 * c:2 * c + 2, n * 256:(n + 1) * 256]
                    nc.vector.tensor_tensor(part, part, ps[:, task % 4, :].rearrange("p (t d) -> p t d", t=2),
                                            ALU.add).then_inc(dve_evac, 1)
                if n < 2:
                    mix_low(N_IN + 6 + n)

            def low(s, s_raw, number):
                dve.wait_ge(high_made, number)
                nc.vector.tensor_tensor(wlo_b[s][:], raw_b[s_raw][:], whi_b[s][:].bitcast(F32), ALU.subtract).then_inc(low_made, 1)

            def first_low(m):
                low(m % SPLIT_B, m % RAW_B, M0 + m + 1)

            first_low(0)
            first_low(1)
            for t in range(TT):
                dve.wait_ge(h2_sum, TT + t)
                nc.vector.tensor_scalar(stat[:, t, 1:2], stat[:, t, 0:1], 1.0 / D, EPS, ALU.mult, ALU.add).then_inc(h2_sum, 1)
            dve.wait_ge(h2_root, 1)
            link(nc.vector.reciprocal(stat[:, :, 3:4], stat[:, :, 2:3]))
            for t in range(TT):
                nc.vector.tensor_scalar(hn[:, t, :], h2[:, t, :], stat[:, t, 3:4], None, ALU.mult).then_inc(hn_made, 1)
            first_low(2)
            first_low(3)

            dve.wait_ge(logits_done, 1)
            dve.wait_ge(pool_made, ROUTE_CONSTS)
            link(nc.vector.tensor_copy(logits[:], ps[:, 0, 0:TT * E].rearrange("p (t e) -> p t e", t=TT)))
            for t in range(TT):
                link(nc.vector.max(top8[:, t, :], logits[:, t, :]))
                link(nc.vector.max_index(idx8[:, t, :], top8[:, t, :], logits[:, t, :]))
            link(nc.vector.tensor_copy(idxf[:], idx8[:, :, 0:TOPK]))
            nc.vector.tensor_tensor(topw[:], top8[:, :, 0:TOPK], top8[:, :, 0:1].broadcast_to((P, TT, TOPK)),
                                    ALU.subtract).then_inc(exps_in, 1)
            link(nc.vector.tensor_tensor(pick[:], idxf[:].rearrange("p t r -> p (t r)").unsqueeze(2).broadcast_to((P, 16, E)),
                                         iota_e[:, 0:E].unsqueeze(1).broadcast_to((P, 16, E)), ALU.is_equal))
            with nc.allow_low_precision("zeros and ones are exact in bfloat16"):
                nc.vector.tensor_reduce(chosen[:], pick[:].rearrange("p (t r) e -> p t e r", t=TT), AX_X, ALU.add).then_inc(chosen_made, 1)
            dve.wait_ge(counted, 1)
            link(nc.vector.tensor_copy(pos[:], ps[:, 1, 0:TT * E].rearrange("p (t e) -> p t e", t=TT)))
            link(nc.vector.tensor_copy(cnt[:], ps[:, 1, TT * E:TT * E + E]))
            link(nc.vector.tensor_scalar(spill[:], cnt[:], float(P), None, ALU.is_gt))
            for q in (2, 3):
                link(nc.vector.scalar_tensor_tensor(out=spill[:], in0=cnt[:], scalar=float(P * q), in1=spill[:],
                                                    op0=ALU.is_gt, op1=ALU.add))
            link(nc.vector.tensor_tensor_scan(incl[:], ones_e[:], spill[:], 0.0, ALU.mult, ALU.add))
            link(nc.vector.tensor_tensor(first[:], incl[:], spill[:], ALU.subtract))
            link(nc.vector.scalar_tensor_tensor(out=first[:], in0=first[:], scalar=float(E - 1), in1=iota_e[:, 0:E],
                                                op0=ALU.add, op1=ALU.subtract))
            link(nc.vector.tensor_scalar(lap[:], pos[:], float(P), None, ALU.is_ge))
            link(nc.vector.tensor_copy(tmp1[:], lap[:]))
            for q in (2, 3):
                link(nc.vector.scalar_tensor_tensor(out=lap[:].rearrange("p t e -> p (t e)"), in0=pos[:].rearrange("p t e -> p (t e)"), scalar=float(P * q), in1=lap[:].rearrange("p t e -> p (t e)"),
                                                    op0=ALU.is_ge, op1=ALU.add))
            link(nc.vector.tensor_tensor(blk[:], lap[:], first[:].unsqueeze(1).broadcast_to((P, TT, E)), ALU.add))
            link(nc.vector.tensor_tensor(blk[:], blk[:], tmp1[:], ALU.mult))
            link(nc.vector.tensor_tensor(blk[:], blk[:], iota_e[:, 0:E].unsqueeze(1).broadcast_to((P, TT, E)), ALU.add))
            link(nc.vector.scalar_tensor_tensor(out=pos[:].rearrange("p t e -> p (t e)"), in0=lap[:].rearrange("p t e -> p (t e)"), scalar=-float(P), in1=pos[:].rearrange("p t e -> p (t e)"),
                                                op0=ALU.mult, op1=ALU.add))
            for src, dst in ((pos, rslot), (blk, rblk)):
                for t in range(TT):
                    link(nc.vector.tensor_tensor(prod[:, 4 * t:4 * t + 4, :], pick[:, 4 * t:4 * t + 4, :],
                                                 src[:, t:t + 1, :].broadcast_to((P, TOPK, E)), ALU.mult))
                link(nc.vector.tensor_reduce(dst[:], prod[:], AX_X, ALU.add))
            link(nc.vector.tensor_tensor(hot_s[:], rslot[:].unsqueeze(2).broadcast_to((P, 16, P)),
                                         iota_s[:].unsqueeze(1).broadcast_to((P, 16, P)), ALU.is_equal))
            link(nc.vector.tensor_tensor(hot_b[:], rblk[:].unsqueeze(2).broadcast_to((P, 16, 48)),
                                         iota_e[:].unsqueeze(1).broadcast_to((P, 16, 48)), ALU.is_equal))
            link(nc.vector.tensor_scalar(hot_v[:, :, 0:48], hot_b[:], pcol[:, 0:1], None, ALU.mult))
            nc.vector.tensor_tensor(hot_v[:, :, 48:96], hot_b[:], kcol[:].unsqueeze(2).broadcast_to((P, 16, 48)),
                                    ALU.mult).then_inc(hot_made, 1)
            dve.wait_ge(exps_out, 1)
            link(nc.vector.tensor_reduce(wsum[:], topw[:], AX_X, ALU.add))
            link(nc.vector.reciprocal(wsum[:], wsum[:]))
            link(nc.vector.tensor_tensor(topw[:], topw[:], wsum[:].unsqueeze(2).broadcast_to((P, TT, TOPK)), ALU.mult))
            link(nc.vector.tensor_scalar(exf[:], iota_e[:], -float(E), None, ALU.add))
            link(nc.vector.tensor_tensor(ended[:], incl[:].unsqueeze(1).broadcast_to((P, BLOCKS, E)),
                                         exf[:].unsqueeze(2).broadcast_to((P, BLOCKS, E)), ALU.is_le))
            link(nc.vector.tensor_reduce(exf[:], ended[:], AX_X, ALU.add))
            link(nc.vector.scalar_tensor_tensor(out=exf[:], in0=exf[:], scalar=float(E - 1), in1=own[:], op0=ALU.min, op1=ALU.add))
            link(nc.vector.tensor_copy(expert_of[:], exf[:]))
            link(nc.vector.tensor_scalar(nbf[:], incl[:, E - 1:E], float(E), None, ALU.add))
            link(nc.vector.tensor_copy(n_blocks[:], nbf[:]))
            dve.wait_ge(table_done, 1)
            link(nc.vector.tensor_copy(tab[:], ps[:, 2, 0:96]))
            a_, b_ = tab[:, 0:48], tab[:, 48:96]
            link(nc.vector.scalar_tensor_tensor(out=row[:], in0=b_, scalar=float(P), in1=a_, op0=ALU.mult, op1=ALU.add))
            link(nc.vector.tensor_scalar(skp[:], b_, 0.5, SKIP, ALU.is_lt, ALU.mult))
            link(nc.vector.scalar_tensor_tensor(out=row[:], in0=row[:], scalar=-float(P), in1=skp[:], op0=ALU.add, op1=ALU.add))
            link(nc.vector.tensor_copy(yidx[:], row[:]))
            link(nc.vector.tensor_scalar(rnk[:], b_, 4.5, None, ALU.is_gt))
            for q in (8.5, 12.5):
                link(nc.vector.scalar_tensor_tensor(out=rnk[:], in0=b_, scalar=q, in1=rnk[:], op0=ALU.is_gt, op1=ALU.add))
            link(nc.vector.scalar_tensor_tensor(out=row[:], in0=rnk[:], scalar=-float(SEQ), in1=row[:], op0=ALU.mult, op1=ALU.add))
            nc.vector.tensor_copy(xidx[:], row[:]).then_inc(tables_ready, 1)
            dve.wait_ge(bias_made, 1)
            nc.vector.tensor_tensor(bias[E:2 * E, :], biasr[E:2 * E, :], bias[E:2 * E, :].bitcast(F32),
                                    ALU.subtract).then_inc(bias_made, 1)

            def tokens_low(e):
                dve.wait_ge(xth_made, e + 1)
                for k in range(KD):
                    ins = nc.vector.scalar_tensor_tensor(out=xtl[:, k, :], in0=t_ps[:, k * P:(k + 1) * P],
                                                         scalar=fcol[:, k:k + 1], in1=xth[:, k, :].bitcast(F32),
                                                         op0=ALU.mult, op1=ALU.subtract)
                ins.then_inc(xtl_made, 1)

            def hidden_low(e):
                dve.wait_ge(hth_made, e + 1)
                nc.vector.tensor_tensor(htl[:], t_ps.rearrange("p (k s) -> p k s", k=KD), hth[:].bitcast(F32),
                                        ALU.subtract).then_inc(htl_made, 1)

            def gate(e):
                dve.wait_ge(gu_done, e + 1)
                nc.vector.tensor_scalar(gm[:], gu_ps[:, 0, :], LIMIT, None, ALU.min).then_inc(gate_made, 1)

            def up(e):
                nc.vector.tensor_scalar(um[:], gu_ps[:, 1, :], LIMIT, -LIMIT, ALU.min, ALU.max).then_inc(up_made, 1)

            def product(e):
                dve.wait_ge(up_made, e + 1)
                nc.vector.scalar_tensor_tensor(out=um[:], in0=um[:], scalar=1.0, in1=gm[:], op0=ALU.add,
                                               op1=ALU.mult).then_inc(gu_mult, 1)

            def hidden(e):
                dve.wait_ge(gu_mult, e + 1)
                dve.wait_ge(sig_made, e + 1)
                nc.vector.tensor_tensor(hid[:], um[:], sg[:], ALU.mult).then_inc(hid_made, 1)

            tokens_low(0)
            for m in range(4, 8):
                first_low(m)

            def loop_low(e, j):
                s, s_raw = (GU_P + j) % SPLIT_B, (GU_P + j) % RAW_B
                dve.wait_ge(high_made, (e - 1) * PER_E + (M0 + GU_P + j + 1))
                nc.vector.tensor_tensor(wlo_b[s][:], raw_b[s_raw][:], whi_b[s][:].bitcast(F32), ALU.subtract).then_inc(low_made, 1)

            loop_low(1, 0)
            loop_low(1, 1)
            tokens_low(1)
            gate(0)
            up(0)
            nb = dve.value_load(n_blocks[0:1, 0:1], min_val=E, max_val=E + MAX_OVER)
            with dve.Fori(1, nb) as e:
                for j in range(PER_E):
                    loop_low(e, j + 2)
                    if j == 0:
                        product(e - 1)
                    if j == 1:
                        hidden(e - 1)
                    if j == 4:
                        hidden_low(e - 1)
                    if j == 8:
                        tokens_low(e + 1)
                    if j == 9:
                        gate(e)
                    if j == 10:
                        up(e)
            loop_low(nb, 2)
            loop_low(nb, 3)
            product(nb - 1)
            hidden(nb - 1)
            hidden_low(nb - 1)
            for t in range(TT):
                for r in range(TOPK):
                    i = 2 * t + r // 2
                    dve.wait_ge(y_loaded[i % RAW_B], 16 * (i // RAW_B + 1))
                    if r >= 1:
                        dve.wait_ge(acc_made, 4 * t + r)
                    nc.vector.scalar_tensor_tensor(out=h2[:, t, :], in0=raw_b[i % RAW_B][:, (r % 2) * D:(r % 2 + 1) * D],
                                                   scalar=topw[:, t, r:r + 1], in1=h2[:, t, :], op0=ALU.mult,
                                                   op1=ALU.add).then_inc(acc_made, 1)
                dve.wait_ge(fin_sum, 2 * t + 1)
                nc.vector.tensor_scalar(stat[:, t, 1:2], stat[:, t, 0:1], 1.0 / D, EPS, ALU.mult, ALU.add).then_inc(fin_sum, 1)
                dve.wait_ge(fin_root, t + 1)
                link(nc.vector.reciprocal(stat[:, t, 3:4], stat[:, t, 2:3]))
                link(nc.vector.tensor_scalar(h2[:, t, :], h2[:, t, :], stat[:, t, 3:4], None, ALU.mult))
                if t == 0:
                    dve.wait_ge(bias_loaded, 16 * 5)
                nc.vector.tensor_tensor(h2[:, t, :], h2[:, t, :], gfin[:], ALU.mult).then_inc(fin_made, 1)

        @block.tensor
        def _(pe):
            def three(out_ap, sta, mov, first, last):
                nc.tensor.matmul(out_ap, sta[0], mov[0], start=first, stop=False)
                nc.tensor.matmul(out_ap, sta[0], mov[1], start=False, stop=False)
                return nc.tensor.matmul(out_ap, sta[1], mov[0], start=False, stop=last)

            def wait_bank(task):
                if task < 4:
                    return
                if task - 4 < 2 * N_IN:
                    pe.wait_ge(act_evac, task - 3)
                else:
                    pe.wait_ge(dve_evac, task - 4 - 2 * N_IN + 1)

            def turned_task(n, c, task, mov, kt, col):
                wait_bank(task)
                hi, lo = mix_slot(n)
                for k in range(kt):
                    ins = three(ps[:, task % 4, :], (hi[:, k, col:col + P], lo[:, k, col:col + P]),
                                (mov[0][:, k, :], mov[1][:, k, :]), k == 0, k == kt - 1)
                ins.then_inc(piece_used if ends_piece[task] else task_done, 1)

            def token_task(n, c, task):
                wait_bank(task)
                hi, lo = mix_slot(n)
                for i in range(2):
                    tok = slice((2 * c + i) * P, (2 * c + i + 1) * P)
                    for k in range(KD):
                        ins = three(ps[:, task % 4, i * 256:(i + 1) * 256], (xnh[:, k, tok], xnl[:, k, tok]),
                                    (hi[:, k, :], lo[:, k, :]), k == 0, k == KD - 1)
                ins.then_inc(piece_used if ends_piece[task] else task_done, 1)

            pe.wait_ge(pool_made, IDENT)
            for k in range(KD):
                for t in range(TT):
                    if k == 0:
                        pe.wait_ge(xn_made, t + 1)
                    ins = nc.tensor.transpose(ps[:, k, t * P:(t + 1) * P], xn[:, t, k * P:(k + 1) * P], ident[:])
                ins.then_inc(xT_turned, 1)
            pe.wait_ge(wsp_loaded, 16)
            pe.wait_ge(xnl_made, KD)
            for c in range(2):
                for g in range(4):
                    ins = nc.tensor.transpose(ps[:, 4 + c, g * P:(g + 1) * P], wsp[:, 4 * c + g, :], ident[:])
                ins.then_inc(wsp_turned, 1)

            def scores(h):
                pe.wait_ge(act_evac, 8)
                if h == 0:
                    pe.wait_ge(wspT_made, 2)
                else:
                    pe.wait_ge(probT_made, h)
                q, pair = (h % 2) * 64, h // 2
                for i in (3, 2, 0, 1):
                    bank, col = sc_ps[i]
                    w = P * (i + 1)
                    ins = nc.tensor.matmul(ps[:, bank, col:col + w], qT[q:q + 64, pair, i * P:(i + 1) * P],
                                           kT[q:q + 64, pair, 0:w], start=True, stop=True)
                ins.then_inc(scores_ready, 1)

            def turn_prob(h):
                pe.wait_ge(prob_made, 4 * h + 4)
                for i in range(TT):
                    for j in range(i + 1):
                        a = pt_at[j] + (i - j) * P
                        ins = nc.tensor.transpose(ps46[:, a:a + P], prob[:, sc_sb[i] + j * P:sc_sb[i] + (j + 1) * P], ident[:])
                ins.then_inc(prob_turned, 1)

            def weigh(h):
                pe.wait_ge(probT_made, h + 1)
                pe.wait_ge(act_evac, 12)
                if h >= 1:
                    pe.wait_ge(al_made, h)
                q = (h % 2) * 64
                for j in range(TT):
                    ins = nc.tensor.matmul(ps[q:q + 64, 7, j * P:SEQ], v[:, j, h * HD:(h + 1) * HD],
                                           probT[:, pt_at[j]:pt_at[j] + SEQ - j * P], start=(j == 0), stop=(j == TT - 1))
                ins.then_inc(head_done, 1)

            xT = (xnh, xnl)
            for n in range(N_IN):
                pe.wait_ge(low_made, n + 1)
                by_token = 4 <= n < 6 or 8 <= n < 10
                for c in range(2):
                    if by_token:
                        token_task(n, c, 2 * n + c)
                    else:
                        turned_task(n, c, 2 * n + c, xT, KD, c * P)
                    if c == 0 and n >= 10:
                        turn_prob(n - 10)
                if 0 <= n - 9 < HEADS:
                    scores(n - 9)
                if n >= 10:
                    weigh(n - 10)
            pe.wait_ge(ln_made, TT)
            pe.wait_ge(wsp_masked, 1)
            for g in range(4):
                task = 2 * N_IN + g
                wait_bank(task)
                for c in range(TT):
                    for half in range(2):
                        q = half * 64
                        ins = nc.tensor.matmul(ps[q:q + 64, task % 4, c * P:(c + 1) * P],
                                               vv[:, c, (2 * g + half) * 64:(2 * g + half + 1) * 64],
                                               wspT[:, 2 * g + half, :], start=True, stop=True)
                ins.then_inc(task_done, 1)
            for n in range(N_IN, N_IN + 4):
                attn = n < N_IN + 2
                pe.wait_ge(low_made, n + 1)
                if n == N_IN:
                    pe.wait_ge(al_made, HEADS)
                if n == N_IN + 2:
                    pe.wait_ge(sgl_made, 4)
                for c in range(4):
                    turned_task(n, c, 2 * N_IN + 4 + 4 * (n - N_IN) + c, (ah, al) if attn else (sgh, sgl), 4, c * P)
            for n in range(N_IN + 4, N_MIX):
                pe.wait_ge(low_made, n + 1)
                pe.wait_ge(ml_made, KD)
                for c in range(2):
                    token_task(n, c, 2 * N_IN + 20 + 2 * (n - N_IN - 4) + c)

            for k in range(KD):
                for t in range(TT):
                    if k == 0:
                        pe.wait_ge(hn_made, t + 1)
                    ins = nc.tensor.transpose(ps[:, k, t * P:(t + 1) * P], hn[:, t, k * P:(k + 1) * P], ident[:])
                ins.then_inc(hn_turned, 1)
            pe.wait_ge(hnT_made, KD)
            pe.wait_ge(wr_loaded, 16)
            pe.wait_ge(consts_loaded, 16 * (4 + GROUPS + 1))
            pe.wait_ge(pool_made, ROUTE_CONSTS)
            for t in range(TT):
                dst = ps[:, 0, t * E:(t + 1) * E]
                nc.tensor.matmul(dst, ones1[:], brow[:], start=True, stop=False)
                for k in range(KD):
                    ins = nc.tensor.matmul(dst, hnT[:, k, t * P:(t + 1) * P], wr[:, k, :], start=False, stop=(k == KD - 1))
            ins.then_inc(logits_done, 1)
            pe.wait_ge(chosen_made, 1)
            for t in range(TT):
                dst = ps[:, 1, t * E:(t + 1) * E]
                for s in range(t):
                    nc.tensor.matmul(dst, onesb[:], chosen[:, s, :], start=(s == 0), stop=False)
                nc.tensor.matmul(dst, before[:], chosen[:, t, :], start=(t == 0), stop=True)
            for s in range(TT):
                ins = nc.tensor.matmul(ps[:, 1, TT * E:TT * E + E], onesb[:], chosen[:, s, :], start=(s == 0), stop=(s == TT - 1))
            ins.then_inc(counted, 1)
            pe.wait_ge(hot_made, 1)
            for i in range(16):
                ins = nc.tensor.matmul(ps[:, 2, 0:96], hot_s[:, i, :], hot_v[:, i, :], start=(i == 0), stop=(i == 15))
            ins.then_inc(table_done, 1)

            def turn_tokens(landed, used):
                pe.wait_ge(x_landed, landed)
                pe.wait_ge(htl_made, used) if used is not None else None
                for k in range(KD):
                    ins = nc.tensor.transpose(t_ps[:, k * P:(k + 1) * P], xgat[:, k * P:(k + 1) * P], ident[:])
                ins.then_inc(x_turned, 1)

            def turn_hidden(e, tokens):
                pe.wait_ge(hid_made, e + 1)
                pe.wait_ge(xtl_made, tokens)
                for k in range(KD):
                    a = (k // 2) * 256 + k % 2
                    ins = nc.tensor.transpose(t_ps[:, k * P:(k + 1) * P], hid[:, a:a + 255:2], ident[:])
                ins.then_inc(hid_turned, 1)

            def gate_up_ready(e, tokens):
                pe.wait_ge(xtl_made, tokens)
                if e is not None:
                    pe.wait_ge(gate_made, e)
                    pe.wait_ge(up_made, e)

            def gate_up_bias(sel):
                pe.wait_ge(selh_made, sel)
                for q in range(4):
                    ins = nc.tensor.matmul(ps[:, q, :], selh[:], bias[:, q * 512:(q + 1) * 512], start=False, stop=True)
                ins.then_inc(gu_done, 1)

            def gate_up_piece(j, s, number):
                pe.wait_ge(low_made, number)
                for q in range(4):
                    cols = slice(q * 512, (q + 1) * 512)
                    ins = three(ps[:, q, :], (xth[:, j, :], xtl[:, j, :]), (whi_b[s][:, cols], wlo_b[s][:, cols]),
                                j == 0, False)
                ins.then_inc(piece_used, 1)

            def down_ready(halves):
                pe.wait_ge(htl_made, halves)

            def down_bias(sel):
                pe.wait_ge(seld_made, sel)
                for q in range(2):
                    ins = nc.tensor.matmul(ps[:, 6 + q, :], seld[:], bias[:, 2 * D + q * 512:2 * D + (q + 1) * 512],
                                           start=False, stop=True)
                ins.then_inc(y_done, 1)

            def down_piece(i, s, number):
                pe.wait_ge(low_made, number)
                for two in range(2):
                    k = 2 * i + two
                    for q in range(2):
                        cols = slice(two * D + q * 512, two * D + (q + 1) * 512)
                        ins = three(ps[:, 6 + q, :], (hth[:, k, :], htl[:, k, :]), (whi_b[s][:, cols], wlo_b[s][:, cols]),
                                    k == 0, False)
                ins.then_inc(piece_used, 1)

            pe.wait_ge(tables_ready, 1)
            pe.wait_ge(bias_made, 2)
            turn_tokens(16, None)
            gate_up_ready(None, 1)
            for j in range(GU_P):
                gate_up_piece(j, j % SPLIT_B, M0 + j + 1)
            gate_up_bias(1)
            turn_tokens(32, None)
            nb = pe.value_load(n_blocks[0:1, 0:1], min_val=E, max_val=E + MAX_OVER)
            with pe.Fori(1, nb) as e:
                gate_up_ready(e, e + 1)
                for j in range(PER_E):
                    number = (e - 1) * PER_E + (M0 + GU_P + j + 1)
                    if j == 4:
                        turn_hidden(e - 1, e + 1)
                    if j == GU_P:
                        gate_up_bias(e + 1)
                        turn_tokens(e * 16 + 32, e)
                        down_ready(e)
                    if j < GU_P:
                        gate_up_piece(j, (GU_P + j) % SPLIT_B, number)
                    else:
                        down_piece(j - GU_P, (GU_P + j) % SPLIT_B, number)
                down_bias(e)
            turn_hidden(nb - 1, nb + 1)
            down_ready(nb)
            for i in range(4):
                down_piece(i, (GU_P + i) % SPLIT_B, nb * PER_E + (M0 + GU_P - PER_E + i + 1))
            down_bias(nb)


_INS = ["x", "mix_norm_g", "w_in", "w_attn_out", "sgu_ln_g", "sgu_ln_b", "w_spatial", "b_spatial", "w_sgu_out", "w_mix_out",
        "ffn_norm_g", "w_router", "b_router", "w_gate_up", "b_gate_up", "w_down", "b_down", "final_norm_g"]


def kernel(**inputs):
    import numpy as np
    import concourse.bacc as bacc
    from concourse.bass_utils import run_bass_kernel_spmd

    nc = bacc.Bacc("TRN2", target_bir_lowering=False, num_devices=1)
    arrays, args = {}, []
    for name in _INS:
        a = np.ascontiguousarray(inputs[name])
        arrays[f"in_{name}"] = a
        args.append(nc.dram_tensor(f"in_{name}", a.shape, mybir.dt.from_np(a.dtype), kind="ExternalInput").ap())
    args.append(nc.dram_tensor("out_0", (1, SEQ, D), F32, kind="ExternalOutput").ap())
    build(nc, *args)
    r = run_bass_kernel_spmd(nc, [arrays], core_ids=[0])
    return r.results[0]["out_0"]
```

```python
from contextlib import ExitStack

import concourse.bass as bass
from concourse import mybir

F32 = mybir.dt.float32
F32R = mybir.dt.float32r
BF16 = mybir.dt.bfloat16
I32 = mybir.dt.int32
U32 = mybir.dt.uint32
ALU = mybir.AluOpType
ACT = mybir.ActivationFunctionType
AX_X = mybir.AxisListType.X

P = 128
D = 1024
KD = D // P
SEQ = 512
TT = SEQ // P
HEADS, HD = 8, 64
ATTN_W = HEADS * HD
SGU_W = D // 2
GROUPS = 8
E = 32
TOPK = 4
EPS = 1e-5
LIMIT, ALPHA = 7.0, 1.702
FAR = -1.0e30
SKIP = 65536.0

PIECE = 2048
N_IN = (3 * ATTN_W + 2 * SGU_W + 2 * D) // 256
N_MIX = N_IN + 2 + 2 + D // 256
RAW_A, SPLIT_A = 3, 2
RAW_B, SPLIT_B = 6, 4
PER_E = 12
GU_P = 8
MAX_OVER = (SEQ * TOPK) // (P + 1)
BLOCKS = 48
IDENT, DIST, ROUTE_CONSTS, LATE_CONSTS = 2, 4, 12, 19
CONSTS = 16 * (3 + GROUPS + 1)
assert E + MAX_OVER < BLOCKS and PER_E % RAW_B == 0 and PER_E % SPLIT_B == 0


def build(nc, x, mix_norm_g, w_in, w_attn_out, sgu_ln_g, sgu_ln_b, w_spatial, b_spatial, w_sgu_out, w_mix_out,
          ffn_norm_g, w_router, b_router, w_gate_up, b_gate_up, w_down, b_down, final_norm_g, out):
    ctx = ExitStack()
    with ctx:
        base = -(-nc.sbuf_base // 64) * 64
        count = [0]

        def at(offset, shape, dt, name):
            count[0] += 1
            return nc.alloc_sbuf_tensor_at(name, shape, dt, offset=base + offset)

        K = 1024
        raw = [at(8 * K * s, [P, PIECE], F32, f"raw{s}") for s in range(RAW_A)]
        whi = [at(24 * K + 8 * K * s, [P, PIECE], F32R, f"whi{s}") for s in range(SPLIT_A)]
        wlo = [at(40 * K + 8 * K * s, [P, PIECE], F32R, f"wlo{s}") for s in range(SPLIT_A)]
        h2 = at(56 * K, [P, TT, D], F32, "h2")
        qT = at(56 * K, [P, HEADS // 2, SEQ], F32, "qT")
        kT = at(64 * K, [P, HEADS // 2, SEQ], F32, "kT")
        S0 = 72 * K
        small_at = [S0]

        def small(shape, dt, name):
            n = 1
            for v in shape[1:]:
                n *= v
            size = -(-n * (2 if dt == BF16 else 4) // 64) * 64
            t = at(small_at[0], shape, dt, name)
            small_at[0] += size
            return t

        ident = small([P, P], F32, "ident")
        gcol = small([P, KD], F32, "gcol")
        fcol = small([P, KD], F32, "fcol")
        stat = small([P, 4, 8], F32, "stat")
        bn = small([P, TT, 6], F32, "bn")
        mv = small([P, TT, 2], F32, "mv")
        negmax = small([P, 2, 4], F32, "negmax")
        rowsum = small([P, 2, 4], F32, "rowsum")
        rinv = small([P, 2, 4], F32, "rinv")
        top8 = small([P, TT, 8], F32, "top8")
        idx8 = small([P, TT, 8], U32, "idx8")
        topw = small([P, TT, TOPK], F32, "topw")
        wsum = small([P, TT], F32, "wsum")
        xidx = small([P, BLOCKS], I32, "xidx")
        yidx = small([P, BLOCKS], I32, "yidx")
        expert_of = small([P, BLOCKS], I32, "expert_of")
        n_blocks = small([P, 1], I32, "n_blocks")
        cur_x = small([P, 1], I32, "cur_x")
        cur_y = small([P, 1], I32, "cur_y")
        late = small([P, 16], F32, "late")
        wlate = small([P, TT], F32, "wlate")
        xlast = small([P, 1], F32, "xlast")
        brow = small([P, E], F32, "brow")
        assert small_at[0] <= 76 * K, small_at[0]

        A0 = 76 * K
        xnh = at(A0, [P, KD, SEQ], F32R, "xnh")
        xnl = at(A0 + 16 * K, [P, KD, SEQ], F32R, "xnl")
        gates = at(A0 + 32 * K, [P, 2 * KD, SEQ], F32, "gates")
        x_in = at(A0 + 32 * K, [P, TT, D], F32, "x_in")
        xn = at(A0 + 48 * K, [P, TT, D], F32, "xn")
        v = at(A0 + 64 * K, [P, TT, ATTN_W], F32, "v")
        sgh = at(A0 + 64 * K, [P, 4, SEQ], F32R, "sgh")
        prob = at(A0 + 72 * K, [P, 1280], F32, "prob")
        probT = at(A0 + 77 * K, [P, 1280], F32, "probT")
        sgl = at(A0 + 72 * K, [P, 4, SEQ], F32R, "sgl")
        u = at(A0 + 82 * K, [P, 4, SEQ], F32, "u")
        vv = at(A0 + 90 * K, [P, TT, SGU_W], F32, "vv")
        wsp = at(A0 + 90 * K, [P, GROUPS, P], F32, "wsp")
        ah = at(A0 + 98 * K, [P, HEADS // 2, SEQ], F32R, "ah")
        al = at(A0 + 106 * K, [P, HEADS // 2, SEQ], F32R, "al")
        wspT = at(A0 + 114 * K, [P, GROUPS, P], F32, "wspT")
        dist = at(A0 + 118 * K, [P, SEQ], F32, "dist")
        lng = at(A0 + 120 * K, [P, SGU_W], F32, "lng")
        lnb = at(A0 + 122 * K, [P, SGU_W], F32, "lnb")
        bsp = at(A0 + 124 * K, [P, 4, P], F32, "bsp")
        assert 76 + 126 <= 207

        R0 = A0 + 64 * K
        hn = at(R0, [P, TT, D], F32, "hn")
        hT = at(R0 + 16 * K, [P, KD, SEQ], F32, "hT")
        wr = at(R0 + 32 * K, [P, KD, E], F32, "wr")
        frow = at(A0 + 112 * K, [P, D], F32, "frow")
        rt_at = [0]

        def region(offset):
            rt_at[0] = offset

        def rt(shape, dt, name):
            n = 1
            for w in shape[1:]:
                n *= w
            t = at(rt_at[0], shape, dt, name)
            rt_at[0] += -(-n * (2 if dt == BF16 else 4) // 64) * 64
            return t

        region(R0 + 33 * K)
        iota_e = rt([P, 48], F32, "iota_e")
        iota_s = rt([P, P], F32, "iota_s")
        pcol = rt([P, 1], F32, "pcol")
        kcol = rt([P, 16], F32, "kcol")
        before = rt([P, P], BF16, "before")
        onesb = rt([P, P], BF16, "onesb")
        ones_e = rt([P, E], F32, "ones_e")
        own = rt([P, BLOCKS], F32, "own")
        chosen = rt([P, TT, E], BF16, "chosen")
        logits = rt([P, TT, E], F32, "logits")
        assert rt_at[0] <= R0 + 36 * K
        region(A0 + 116 * K)
        lgT = rt([E, SEQ], F32, "lgT")
        spill = rt([P, E], F32, "spill")
        incl = rt([P, E], F32, "incl")
        first = rt([P, E], F32, "first")
        idxf, rpos, rfirst, lap, over, rslot, rblk = (rt([P, 16], F32, n) for n in
                                                      ("idxf", "rpos", "rfirst", "lap", "over", "rslot", "rblk"))
        nbf = rt([P, 1], F32, "nbf")
        assert rt_at[0] <= A0 + 119 * K, rt_at[0] - A0
        region(R0 + 16 * K)
        pick = rt([P, 16, E], F32, "pick")
        prod = rt([P, 16, E], F32, "prod")
        hot_s = rt([P, 16, P], BF16, "hot_s")
        hot_b = rt([P, 16, 48], F32, "hot_b")
        hot_v = rt([P, 16, 96], BF16, "hot_v")
        row = rt([P, 48], F32, "row")
        rnk = rt([P, 48], F32, "rnk")
        skp = rt([P, 48], F32, "skp")
        exf = rt([P, BLOCKS], F32, "exf")
        assert rt_at[0] <= R0 + 32 * K
        ended = at(R0 + 16 * K, [P, BLOCKS, E], F32, "ended")

        raw_b = raw + [at(A0 + 32 * K + 8 * K * s, [P, PIECE], F32, f"raw{3 + s}") for s in range(RAW_B - RAW_A)]
        whi_b = whi + [at(A0 + 8 * K * s, [P, PIECE], F32R, f"whi{2 + s}") for s in range(SPLIT_B - SPLIT_A)]
        wlo_b = wlo + [at(A0 + 16 * K + 8 * K * s, [P, PIECE], F32R, f"wlo{2 + s}") for s in range(SPLIT_B - SPLIT_A)]
        biasr = at(A0 + 119 * K, [2 * E, 3 * D], F32, "biasr")
        selh = at(A0 + 56 * K, [2 * E, P], F32R, "selh")
        seld = at(A0 + 56 * K + 512, [2 * E, P], F32R, "seld")
        selt = at(A0 + 57 * K, [2 * E, BLOCKS], F32, "selt")
        xgat = at(A0 + 60 * K, [P, D], F32, "xgat")
        B0 = A0 + 64 * K
        xth = at(B0, [P, KD, P], F32R, "xth")
        xtl = at(B0 + 4 * K, [P, KD, P], F32R, "xtl")
        hth = at(B0 + 8 * K, [P, KD, P], F32R, "hth")
        htl = at(B0 + 12 * K, [P, KD, P], F32R, "htl")
        hid = at(B0 + 16 * K, [P, D], F32, "hid")
        gm = at(B0 + 20 * K, [P, D], F32, "gm")
        um = at(B0 + 24 * K, [P, D], F32, "um")
        sg = at(B0 + 28 * K, [P, D], F32, "sg")
        yb = at(B0 + 32 * K, [P, D], F32, "yb")
        bias = at(B0 + 36 * K, [2 * E, 3 * D], F32R, "bias")
        gfin = at(A0 + 124 * K, [P, D], F32, "gfin")
        iota_t = at(A0 + 112 * K, [P, SEQ], F32, "iota_t")
        hot_t = at(A0 + 114 * K, [P, SEQ], F32R, "hot_t")
        yh = at(B0, [P, D], F32R, "yh")
        yl = at(B0 + 4 * K, [P, D], F32R, "yl")

        ps = ctx.enter_context(nc.psum_tensor("ps", [P, 8, 512], F32))
        hn_dram = nc.dram_tensor("hn_dram", (SEQ, D), F32).ap()
        y_dram = nc.dram_tensor("y_dram", (SEQ * TOPK, D), F32).ap()

        def sem(name):
            return ctx.enter_context(nc.semaphore(name))

        raw_landed = [sem(f"raw_landed{s}") for s in range(RAW_B)]
        x_loaded = [sem(f"x_loaded{t}") for t in range(TT)]
        gcol_loaded = sem("gcol_loaded")
        consts_loaded = sem("consts_loaded")
        wsp_loaded = sem("wsp_loaded")
        x_again = sem("x_again")
        bias_loaded = sem("bias_loaded")
        wr_loaded, frow_loaded = sem("wr_loaded"), sem("frow_loaded")
        high_made, low_made, piece_used = sem("high_made"), sem("low_made"), sem("piece_used")
        pool_made = sem("pool_made")
        dve_step = sem("dve_step")
        sum_made, root_made, xn_made = sem("sum_made"), sem("root_made"), sem("xn_made")
        xT_turned, xnh_made, xnl_made = sem("xT_turned"), sem("xnh_made"), sem("xnl_made")
        wsp_turned, wspT_made, wsp_masked = sem("wsp_turned"), sem("wspT_made"), sem("wsp_masked")
        task_done, act_evac, dve_evac = sem("task_done"), sem("act_evac"), sem("dve_evac")
        scores_ready, max_made, exp_made, prob_made = sem("scores_ready"), sem("max_made"), sem("exp_made"), sem("prob_made")
        prob_turned, probT_made, head_done, ah_made, al_made = (sem("prob_turned"), sem("probT_made"),
                                                                sem("head_done"), sem("ah_made"), sem("al_made"))
        ln_var, ln_root, ln_made = sem("ln_var"), sem("ln_root"), sem("ln_made")
        sg_sum, sgh_made, sgl_made = sem("sg_sum"), sem("sgh_made"), sem("sgl_made")
        sigm_made, merged, mh_made, ml_made = sem("sigm_made"), sem("merged"), sem("mh_made"), sem("ml_made")
        h2_sum, h2_root, hn_made, hn_stored = sem("h2_sum"), sem("h2_root"), sem("hn_made"), sem("hn_stored")
        h2_turned, hT_made, wr_scaled, lgT_done, lgT_made = (sem("h2_turned"), sem("hT_made"), sem("wr_scaled"),
                                                             sem("lgT_done"), sem("lgT_made"))
        logits_done, chosen_made = sem("logits_done"), sem("chosen_made")
        counted, hot_made, table_done = sem("counted"), sem("hot_made"), sem("table_done")
        xidx_ready, tables_ready = sem("xidx_ready"), sem("tables_ready")
        exps_in, exps_out = sem("exps_in"), sem("exps_out")
        bias_made = sem("bias_made")
        idx_copied, idx_seen, x_landed, y_stored = sem("idx_copied"), sem("idx_seen"), sem("x_landed"), sem("y_stored")
        selh_made, seld_made = sem("selh_made"), sem("seld_made")
        x_turned, xth_made, xtl_made = sem("x_turned"), sem("xth_made"), sem("xtl_made")
        gu_done, gate_made, up_made, sig_made, gu_mult, hid_made = (
            sem("gu_done"), sem("gate_made"), sem("up_made"), sem("sig_made"), sem("gu_mult"), sem("hid_made"))
        hid_turned, hth_made, htl_made = sem("hid_turned"), sem("hth_made"), sem("htl_made")
        y_done, y_made = sem("y_done"), sem("y_made")
        yh_made, yl_made, hot_t_made, late_added = sem("yh_made"), sem("yl_made"), sem("hot_t_made"), sem("late_added")
        late_placed = sem("late_placed")
        y_loaded = [sem(f"y_loaded{s}") for s in range(RAW_B)]
        acc_made, fin_sum, fin_root, fin_made, out_stored = (sem("acc_made"), sem("fin_sum"), sem("fin_root"),
                                                             sem("fin_made"), sem("out_stored"))

        x2 = x[0].rearrange("(t p) d -> t p d", p=P)
        out2 = out[0].rearrange("(t p) d -> t p d", p=P)
        win = w_in[0].rearrange("(k p) (n c) -> n p k c", p=P, c=256)
        wao = w_attn_out[0].rearrange("(k p) (n c) -> n p k c", p=P, c=512)
        wso = w_sgu_out[0].rearrange("(k p) (n c) -> n p k c", p=P, c=512)
        wmo = w_mix_out[0].rearrange("(k p) (n c) -> n p k c", p=P, c=256)
        hn_d = hn_dram.rearrange("(t p) d -> t p d", p=P)
        y_d = y_dram.rearrange("(r t p) d -> t p r d", r=TOPK, p=P)
        slope = [2.0 ** (-8.0 * (h + 1) / HEADS) for h in range(HEADS)]

        def piece_source(n):
            if n < N_IN:
                return win[n], 8
            if n < N_IN + 2:
                return wao[n - N_IN], 4
            if n < N_IN + 4:
                return wso[n - N_IN - 2], 4
            return wmo[n - N_IN - 4], 8

        def mix_slot(n):
            k = piece_source(n)[1]
            return (whi[n % SPLIT_A][:].rearrange("p (k c) -> p k c", k=k),
                    wlo[n % SPLIT_A][:].rearrange("p (k c) -> p k c", k=k))

        M0 = N_MIX
        H2_DONE = 4 + 2 * KD + D // 128
        task_piece = ([n for n in range(N_IN) for _ in range(2)] + [None] * 4
                      + [n for n in range(N_IN, N_IN + 4) for _ in range(4)] + [n for n in range(N_IN + 4, N_MIX) for _ in range(2)])
        ends_piece = [p is not None and (i + 1 == len(task_piece) or task_piece[i + 1] != p) for i, p in enumerate(task_piece)]

        def y_load(i):
            return 2 * (i // 4) + i % 2, i // 2 % 2

        def wait_task(eng, task):
            if ends_piece[task]:
                eng.wait_ge(piece_used, task_piece[task] + 1)
            else:
                eng.wait_ge(task_done, sum(not x for x in ends_piece[:task + 1]))

        sc_ps = {3: (4, 0), 2: (5, 0), 0: (5, 384), 1: (6, 0)}
        sc_sb = {0: 0, 1: 128, 2: 384, 3: 768}
        pt_at = {0: 0, 1: 512, 3: 896, 2: 1024}
        ps46 = ps[:, 4:7, :].rearrange("p b c -> p (b c)")
        gu_ps = ps[:, 0:4, :].rearrange("p b c -> p (b c)").rearrange("p (c two) -> p two c", two=2)
        t_ps = ps[:, 4:6, :].rearrange("p b c -> p (b c)")
        y_ps = ps[:, 6:8, :].rearrange("p b c -> p (b c)")

        block = ctx.enter_context(nc.Block())

        @block.sync
        def _(sp):
            def expert_source(e, j):
                if j < GU_P:
                    return w_gate_up[0][e, j * P:(j + 1) * P, :]
                return w_down[0][e, (j - GU_P) * 256:(j - GU_P + 1) * 256, :].rearrange("(p two) c -> p (two c)", two=2)

            for t in range(TT):
                sp.dma_start(x_in[:, t, :], x2[t]).then_inc(x_loaded[t], 16)
            sp.dma_start(gcol[:], mix_norm_g[0].rearrange("(k p) -> p k", p=P),
                         allow_slow_non_contiguous=True).then_inc(gcol_loaded, 16)
            for n in range(N_MIX):
                src, k = piece_source(n)
                if n >= RAW_A:
                    sp.wait_ge(low_made, n - RAW_A + 1)
                sp.dma_start(raw[n % RAW_A][:].rearrange("p (k c) -> p k c", k=k), src).then_inc(raw_landed[n % RAW_A], 16)
                if n == 2:
                    sp.dma_start(fcol[:], ffn_norm_g[0].rearrange("(k p) -> p k", p=P),
                                 allow_slow_non_contiguous=True).then_inc(consts_loaded, 16)
                    sp.dma_start(wsp[:], w_spatial[0].rearrange("g t s -> t g s")).then_inc(wsp_loaded, 16)
                    sp.dma_start(lng[:], sgu_ln_g[0].rearrange("(o c) -> o c", o=1).broadcast_to((P, SGU_W))).then_inc(consts_loaded, 16)
                    sp.dma_start(lnb[:], sgu_ln_b[0].rearrange("(o c) -> o c", o=1).broadcast_to((P, SGU_W))).then_inc(consts_loaded, 16)
                    for g in range(GROUPS):
                        q = (g % 2) * 64
                        sp.dma_start(bsp[q:q + 64, g // 2, :], b_spatial[0][g:g + 1, :].broadcast_to((64, P))).then_inc(consts_loaded, 16)
                    sp.dma_start(brow[:], b_router[0].rearrange("(o c) -> o c", o=1).broadcast_to((P, E))).then_inc(consts_loaded, 16)
                if n == N_IN + 3:
                    sp.wait_ge(head_done, HEADS)
                    sp.dma_start(h2[:], x[0].rearrange("(t p) d -> p t d", p=P)).then_inc(x_again, 16)

            for m in range(GU_P + 2):
                if m < RAW_A:
                    last = max(i for i in range(N_MIX) if i % RAW_A == m)
                    sp.wait_ge(low_made, last + 1)
                elif m < RAW_B:
                    sp.wait_ge(ml_made, KD)
                else:
                    sp.wait_ge(low_made, M0 + m - RAW_B + 1)
                sp.dma_start(raw_b[m % RAW_B][:], expert_source(m // GU_P, m % GU_P)).then_inc(raw_landed[m % RAW_B], 16)

            def load(turn, j, expert):
                sp.wait_ge(low_made, (turn - 1) * PER_E + (M0 + GU_P + j - RAW_B + 1))
                s = (GU_P + j) % RAW_B
                sp.dma_start(raw_b[s][:], expert_source(expert, j % PER_E)).then_inc(raw_landed[s], 16)

            sp.wait_ge(tables_ready, 1)
            nb = sp.value_load(n_blocks[0:1, 0:1], min_val=E, max_val=E + MAX_OVER)
            with sp.Fori(1, nb - 1) as e:
                past = sp.value_load(expert_of[0:1, bass.ds(e - 1, 1)], min_val=0, max_val=E - 1)
                now = sp.value_load(expert_of[0:1, bass.ds(e, 1)], min_val=0, max_val=E - 1)
                after = sp.value_load(expert_of[0:1, bass.ds(e + 1, 1)], min_val=0, max_val=E - 1)
                for j in range(2, PER_E + 2):
                    load(e, j, now if j < GU_P else past if j < PER_E else after)
            past = sp.value_load(expert_of[0:1, bass.ds(nb - 2, 1)], min_val=0, max_val=E - 1)
            last = sp.value_load(expert_of[0:1, bass.ds(nb - 1, 1)], min_val=0, max_val=E - 1)
            for j in range(2, PER_E):
                load(nb - 1, j, last if j < GU_P else past)
            for j in range(GU_P, PER_E):
                sp.wait_ge(low_made, nb * PER_E + (M0 + j - PER_E - RAW_B + 1))
                sp.dma_start(raw_b[j % RAW_B][:], expert_source(last, j)).then_inc(raw_landed[j % RAW_B], 16)
            sp.wait_ge(y_stored, nb * 16)
            for i in range(2 * TT):
                t, half = y_load(i)
                if 2 <= i < RAW_B:
                    sp.wait_ge(low_made, nb * PER_E + (M0 - 4 + i - 1))
                elif i >= RAW_B:
                    sp.wait_ge(acc_made, 4)
                sp.dma_start(raw_b[i % RAW_B][:].rearrange("p (r d) -> p r d", r=2),
                             y_d[t][:, 2 * half:2 * half + 2, :]).then_inc(y_loaded[i % RAW_B], 16)
            for t in range(TT):
                sp.wait_ge(fin_made, t + 1)
                sp.dma_start(out2[t], h2[:, t, :]).then_inc(out_stored, 16)
            sp.wait_ge(out_stored, 16 * TT)

        @block.gpsimd
        def _(pool):
            made = [0]

            def step(ins, wait=True):
                made[0] += 1
                ins.then_inc(pool_made, 1)
                if wait:
                    pool.wait_ge(pool_made, made[0])

            step(nc.gpsimd.memset(ident[:], 0.0))
            step(nc.gpsimd.affine_select(out=ident[:], in_=ident[:], compare_op=ALU.not_equal, fill=1.0, base=0,
                                         pattern=[[-1, P]], channel_multiplier=1))
            step(nc.gpsimd.iota(dist[:], pattern=[[1, SEQ]], base=-(SEQ - P), channel_multiplier=-1,
                                allow_small_or_imprecise_dtypes=True))
            step(nc.gpsimd.affine_select(out=dist[:], in_=dist[:], compare_op=ALU.is_ge, fill=FAR, base=SEQ - P,
                                         pattern=[[-1, SEQ]], channel_multiplier=1))
            pool.wait_ge(wspT_made, 2)
            nc.gpsimd.affine_select(out=wspT[:], in_=wspT[:], compare_op=ALU.is_ge, fill=0.0, base=0,
                                    pattern=[[0, GROUPS], [1, P]], channel_multiplier=-1).then_inc(wsp_masked, 1)
            pool.wait_ge(piece_used, N_IN + 4)
            pool.dma_start(wr[:], w_router[0].rearrange("(k p) e -> p k e", p=P)).then_inc(wr_loaded, 16)
            for half in range(2):
                pool.dma_start(biasr[half * E:(half + 1) * E, 0:2 * D], b_gate_up[0]).then_inc(bias_loaded, 16)
                pool.dma_start(biasr[half * E:(half + 1) * E, 2 * D:3 * D], b_down[0]).then_inc(bias_loaded, 16)
            pool.dma_start(frow[:], ffn_norm_g[0].rearrange("(o c) -> o c", o=1).broadcast_to((P, D))).then_inc(frow_loaded, 16)
            step(nc.gpsimd.iota(iota_e[:], pattern=[[1, 48]], base=0, channel_multiplier=0,
                                allow_small_or_imprecise_dtypes=True))
            step(nc.gpsimd.iota(iota_s[:], pattern=[[1, P]], base=0, channel_multiplier=0,
                                allow_small_or_imprecise_dtypes=True))
            step(nc.gpsimd.iota(pcol[:], pattern=[[1, 1]], base=0, channel_multiplier=1,
                                allow_small_or_imprecise_dtypes=True))
            step(nc.gpsimd.affine_select(out=own[:], in_=iota_e[:], compare_op=ALU.is_ge, fill=0.0, base=E - 1,
                                         pattern=[[-1, BLOCKS]], channel_multiplier=0))
            step(nc.gpsimd.iota(kcol[:], pattern=[[1, TT], [TT, TOPK]], base=1, channel_multiplier=0,
                                allow_small_or_imprecise_dtypes=True))
            step(nc.gpsimd.memset(onesb[:], 1.0))
            step(nc.gpsimd.memset(ones_e[:], 1.0))
            step(nc.gpsimd.affine_select(out=before[:], in_=onesb[:], compare_op=ALU.is_gt, fill=0.0, base=0,
                                         pattern=[[1, P]], channel_multiplier=-1))
            pool.wait_ge(ml_made, KD)
            step(nc.gpsimd.memset(selt[:], 0.0))
            step(nc.gpsimd.affine_select(out=selt[:], in_=selt[:], compare_op=ALU.not_equal, fill=1.0, base=0,
                                         pattern=[[-1, BLOCKS]], channel_multiplier=1))
            step(nc.gpsimd.affine_select(out=selt[:], in_=selt[:], compare_op=ALU.not_equal, fill=1.0, base=-E,
                                         pattern=[[-1, BLOCKS]], channel_multiplier=1))
            step(nc.gpsimd.memset(xgat[:], 0.0))

            last_token = nc.gpsimd.to_reg(SEQ - 1)
            last_row = nc.gpsimd.to_reg(SEQ * TOPK - 1)

            def gather(b, copies):
                nc.gpsimd.tensor_copy(cur_x[:], xidx[:, bass.ds(b, 1)]).then_inc(idx_copied, 1)
                pool.wait_ge(idx_copied, copies)
                pool.sem_inc(idx_seen, 1)
                pool.indirect_dma_start(out=xgat[:], out_offset=None, in_=hn_dram,
                                        in_offset=bass.IndirectOffsetOnAxis(ap=cur_x[:, 0:1].bitcast(U32), axis=0),
                                        bounds_check=last_token, oob_is_err=False).then_inc(x_landed, 16)

            def scatter(b, copies):
                nc.gpsimd.tensor_copy(cur_y[:], yidx[:, bass.ds(b, 1)]).then_inc(idx_copied, 1)
                pool.wait_ge(idx_copied, copies)
                pool.sem_inc(idx_seen, 1)
                pool.indirect_dma_start(out=y_dram, out_offset=bass.IndirectOffsetOnAxis(ap=cur_y[:, 0:1].bitcast(U32), axis=0),
                                        in_=yb[:], in_offset=None,
                                        bounds_check=last_row, oob_is_err=False).then_inc(y_stored, 16)

            def select(dst, e, signal):
                nc.gpsimd.tensor_copy(dst[:], selt[:, bass.ds(e, 1)].broadcast_to((2 * E, P))).then_inc(signal, 1)

            for t in range(TT):
                pool.wait_ge(hn_made, t + 1)
                pool.dma_start(hn_d[t], hn[:, t, :]).then_inc(hn_stored, 16)
            select(selh, 0, selh_made)
            select(seld, 0, seld_made)
            pool.wait_ge(bias_made, 2)
            pool.dma_start(gfin[:], final_norm_g.rearrange("(o c) -> o c", o=1).broadcast_to((P, D))).then_inc(bias_loaded, 16)
            pool.wait_ge(xidx_ready, 1)
            pool.wait_ge(hn_stored, 16 * TT)
            gather(0, 1)
            pool.wait_ge(x_turned, 1)
            gather(1, 2)
            pool.wait_ge(tables_ready, 1)
            nb = pool.value_load(n_blocks[0:1, 0:1], min_val=E, max_val=E + MAX_OVER)
            step(nc.gpsimd.memset(yb[:], 0.0))
            scatter(nb - 1, 3)
            pool.wait_ge(gu_done, 1)
            select(selh, 1, selh_made)
            nc.gpsimd.tensor_copy(xlast[:], xidx[:, bass.ds(nb - 1, 1)]).then_inc(pool_made, 1)
            nc.gpsimd.iota(iota_t[:], pattern=[[1, SEQ]], base=0, channel_multiplier=0,
                           allow_small_or_imprecise_dtypes=True).then_inc(pool_made, 1)
            with pool.Fori(1, nb) as e:
                now = pool.value_load(expert_of[0:1, bass.ds(e, 1)], min_val=0, max_val=E - 1)
                after = pool.value_load(expert_of[0:1, bass.ds(e + 1, 1)], min_val=0, max_val=E - 1)
                pool.wait_ge(x_turned, e + 1)
                pool.wait_ge(x_landed, e * 16 + 16)
                gather(e + 1, e * 2 + 2)
                pool.wait_ge(gu_done, e + 1)
                select(selh, after, selh_made)
                pool.wait_ge(y_made, e)
                scatter(e - 1, e * 2 + 3)
                select(seld, now, seld_made)
                pool.wait_ge(y_stored, e * 16 + 16)
            pool.wait_ge(x_landed, nb * 16 + 16)

        @block.scalar
        def _(act):
            def mix_high(n):
                act.wait_ge(raw_landed[n % RAW_A], 16 * (n // RAW_A + 1))
                if n >= SPLIT_A:
                    act.wait_ge(piece_used, n - SPLIT_A + 1)
                nc.scalar.activation(whi[n % SPLIT_A][:], raw[n % RAW_A][:], ACT.Copy).then_inc(high_made, 1)

            for t in range(TT):
                act.wait_ge(x_loaded[t], 16)
                nc.scalar.activation(xn[:, t, :], x_in[:, t, :], ACT.Square, accum_out=stat[:, t, 0:1]).then_inc(sum_made, 1)
            act.wait_ge(sum_made, 2 * TT)
            nc.scalar.activation(stat[:, :, 2:3], stat[:, :, 1:2], ACT.Sqrt).then_inc(root_made, 1)
            mix_high(0)
            act.wait_ge(gcol_loaded, 16)
            for k in range(KD):
                act.wait_ge(xT_turned, k + 1)
                nc.scalar.activation(xnh[:, k, :], ps[:, k, :], ACT.Copy, scale=gcol[:, k:k + 1]).then_inc(xnh_made, 1)
            mix_high(1)

            def spatial_weights():
                for c in range(2):
                    act.wait_ge(wsp_turned, c + 1)
                    nc.scalar.activation(wspT[:, 4 * c:4 * c + 4, :], ps[:, 4 + c, :].rearrange("p (g t) -> p g t", g=4),
                                         ACT.Copy).then_inc(wspT_made, 1)

            def evac(task):
                wait_task(act, task)
                n, c = task // 2, task % 2
                src = ps[:, task % 4, :]
                if n < 2:
                    nc.scalar.activation(qT[:, task, :], src, ACT.Copy, scale=HD ** -0.5).then_inc(act_evac, 1)
                elif n < 4:
                    nc.scalar.activation(kT[:, task - 4, :], src, ACT.Copy).then_inc(act_evac, 1)
                elif n < 6:
                    nc.scalar.activation(v[:, 2 * c:2 * c + 2, (n - 4) * 256:(n - 3) * 256],
                                         src.rearrange("p (t d) -> p t d", t=2), ACT.Copy).then_inc(act_evac, 1)
                elif n < 8:
                    nc.scalar.activation(u[:, task - 12, :], src, ACT.Gelu).then_inc(act_evac, 1)
                elif n < 10:
                    nc.scalar.activation(vv[:, 2 * c:2 * c + 2, (n - 8) * 256:(n - 7) * 256],
                                         src.rearrange("p (t d) -> p t d", t=2), ACT.Gelu).then_inc(act_evac, 1)
                else:
                    nc.scalar.activation(gates[:, task - 20, :], src, ACT.Copy).then_inc(act_evac, 1)

            for n in range(N_IN):
                if n >= 1:
                    mix_high(n + 1)
                if n == 1:
                    spatial_weights()
                evac(2 * n)
                ht, hs = n - 10, n - 9
                if ht >= 0:
                    act.wait_ge(prob_turned, ht + 1)
                    if ht >= 1:
                        act.wait_ge(head_done, ht)
                    nc.scalar.activation(probT[:], ps46[:, 0:1280], ACT.Copy).then_inc(probT_made, 1)
                evac(2 * n + 1)
                if n == 10:
                    act.wait_ge(ln_var, TT)
                    nc.scalar.activation(stat[:, :, 5:6], stat[:, :, 4:5], ACT.Sqrt).then_inc(ln_root, 1)
                if ht >= 0:
                    act.wait_ge(head_done, ht + 1)
                    q = (ht % 2) * 64
                    nc.scalar.activation(ah[q:q + 64, ht // 2, :], ps[q:q + 64, 7, :], ACT.Copy).then_inc(ah_made, 1)
                if 0 <= hs < HEADS:
                    for i in range(TT):
                        act.wait_ge(max_made, 4 * hs + i + 1)
                        a = sc_sb[i]
                        nc.scalar.activation(prob[:, a:a + P * (i + 1)], prob[:, a:a + P * (i + 1)], ACT.Exp,
                                             bias=negmax[:, hs % 2, i:i + 1],
                                             accum_out=rowsum[:, hs % 2, i:i + 1]).then_inc(exp_made, 1)
            act.wait_ge(act_evac, 2 * N_IN)
            mix_high(N_IN + 1)
            for c in range(4):
                act.wait_ge(sg_sum, c + 1)
                nc.scalar.activation(sgh[:, c, :], u[:, c, :], ACT.Copy).then_inc(sgh_made, 1)
                nc.scalar.activation(gates[:, 4 * c:4 * c + 4, :], gates[:, 4 * c:4 * c + 4, :], ACT.Sigmoid).then_inc(sigm_made, 1)
            mix_high(N_IN + 2)
            mix_high(N_IN + 3)
            for d in range(KD):
                if d == 4:
                    mix_high(N_IN + 4)
                act.wait_ge(merged, d + 1)
                nc.scalar.activation(xnh[:, d, :], gates[:, d, :], ACT.Copy).then_inc(mh_made, 1)
            mix_high(N_IN + 5)
            mix_high(N_IN + 6)
            act.wait_ge(bias_loaded, 16 * 4)
            nc.scalar.activation(bias[:], biasr[:], ACT.Copy).then_inc(bias_made, 1)
            mix_high(N_IN + 7)

            def high(j, m_or_expr, s_raw, turns, free):
                act.wait_ge(raw_landed[s_raw], turns)
                act.wait_ge(piece_used, free)
                nc.scalar.activation(whi_b[j][:], raw_b[s_raw][:], ACT.Copy).then_inc(high_made, 1)

            mix_turns = [16 * len([i for i in range(N_MIX) if i % RAW_A == s]) if s < RAW_A else 0 for s in range(RAW_B)]

            def first_high(m):
                high(m % SPLIT_B, m, m % RAW_B, mix_turns[m % RAW_B] + 16 * (m // RAW_B + 1),
                     max(M0 - 2 + m + 1 if m < 2 else M0, M0 + m - SPLIT_B + 1))

            def squares(tiles, evacuated):
                act.wait_ge(dve_evac, evacuated)
                for t in tiles:
                    nc.scalar.activation(hn[:, t, :], h2[:, t, :], ACT.Square, accum_out=stat[:, t, 0:1]).then_inc(h2_sum, 1)

            def turned(half):
                for b in range(4):
                    act.wait_ge(h2_turned, 4 * half + b + 1)
                    nc.scalar.activation(hT[:, 2 * b:2 * b + 2, half * 256:(half + 1) * 256],
                                         ps[:, 4 - 4 * half + b, :].rearrange("p (k s) -> p k s", k=2),
                                         ACT.Copy).then_inc(hT_made, 1)

            squares((0, 1), H2_DONE - 1)
            turned(0)
            first_high(0)
            squares((2, 3), H2_DONE)
            act.wait_ge(h2_sum, 2 * TT)
            nc.scalar.activation(stat[:, :, 2:3], stat[:, :, 1:2], ACT.Sqrt).then_inc(h2_root, 1)
            turned(1)
            first_high(1)
            first_high(2)
            first_high(3)
            act.wait_ge(exps_in, 1)
            nc.scalar.activation(topw[:], topw[:], ACT.Exp).then_inc(exps_out, 1)

            def tokens_high(e):
                act.wait_ge(x_turned, e + 1)
                nc.scalar.activation(xth[:], t_ps.rearrange("p (k s) -> p k s", k=KD), ACT.Copy).then_inc(xth_made, 1)

            def hidden_high(e):
                act.wait_ge(hid_turned, e + 1)
                nc.scalar.activation(hth[:], t_ps.rearrange("p (k s) -> p k s", k=KD), ACT.Copy).then_inc(hth_made, 1)

            def sigmoid(e):
                act.wait_ge(gate_made, e + 1)
                nc.scalar.activation(sg[:], gm[:], ACT.Sigmoid, scale=ALPHA).then_inc(sig_made, 1)

            def rows(e):
                act.wait_ge(y_done, e + 1)
                nc.scalar.activation(yb[:], y_ps, ACT.Copy).then_inc(y_made, 1)

            tokens_high(0)
            for m in range(4, GU_P):
                first_high(m)
            def loop_high(e, j):
                s_raw = (GU_P + j) % RAW_B
                m0 = GU_P + j
                turns = mix_turns[s_raw] + 16 * (m0 // RAW_B + 1)
                act.wait_ge(raw_landed[s_raw], (e - 1) * (16 * PER_E // RAW_B) + turns)
                act.wait_ge(piece_used, (e - 1) * PER_E + (M0 + m0 - SPLIT_B + 1))
                nc.scalar.activation(whi_b[(GU_P + j) % SPLIT_B][:], raw_b[s_raw][:], ACT.Copy).then_inc(high_made, 1)

            loop_high(1, 0)
            loop_high(1, 1)
            tokens_high(1)
            sigmoid(0)
            act.wait_ge(tables_ready, 1)
            nb = act.value_load(n_blocks[0:1, 0:1], min_val=E, max_val=E + MAX_OVER)
            act.wait_ge(y_stored, 16)
            with act.Fori(1, nb) as e:
                for j in range(PER_E):
                    loop_high(e, j + 2)
                    if j == 4:
                        hidden_high(e - 1)
                    if j == 8:
                        tokens_high(e + 1)
                    if j == 10:
                        sigmoid(e)
                rows(e - 1)
            loop_high(nb, 2)
            hidden_high(nb - 1)
            loop_high(nb, 3)
            act.wait_ge(y_done, nb)
            nc.scalar.activation(yh[:], y_ps, ACT.Copy).then_inc(yh_made, 1)
            for t in range(TT):
                act.wait_ge(late_added, t + 1)
                nc.scalar.activation(gm[:], h2[:, t, :], ACT.Square, accum_out=stat[:, t, 0:1]).then_inc(fin_sum, 1)
                act.wait_ge(fin_sum, 2 * t + 2)
                nc.scalar.activation(stat[:, t, 2:3], stat[:, t, 1:2], ACT.Sqrt).then_inc(fin_root, 1)

        @block.vector
        def _(dve):
            steps = [0]

            def link(ins):
                steps[0] += 1
                ins.then_inc(dve_step, 1)
                dve.wait_ge(dve_step, steps[0])

            def mix_low(n):
                dve.wait_ge(high_made, n + 1)
                nc.vector.tensor_tensor(wlo[n % SPLIT_A][:], raw[n % RAW_A][:], whi[n % SPLIT_A][:].bitcast(F32),
                                        ALU.subtract).then_inc(low_made, 1)

            for t in range(TT):
                dve.wait_ge(sum_made, TT + t)
                nc.vector.tensor_scalar(stat[:, t, 1:2], stat[:, t, 0:1], 1.0 / D, EPS, ALU.mult, ALU.add).then_inc(sum_made, 1)
            dve.wait_ge(root_made, 1)
            link(nc.vector.reciprocal(stat[:, :, 3:4], stat[:, :, 2:3]))
            for t in range(TT):
                nc.vector.tensor_scalar(xn[:, t, :], x_in[:, t, :], stat[:, t, 3:4], None, ALU.mult).then_inc(xn_made, 1)
            mix_low(0)
            dve.wait_ge(gcol_loaded, 16)
            for k in range(KD):
                dve.wait_ge(xnh_made, k + 1)
                nc.vector.scalar_tensor_tensor(out=xnl[:, k, :], in0=ps[:, k, :], scalar=gcol[:, k:k + 1],
                                               in1=xnh[:, k, :].bitcast(F32), op0=ALU.mult, op1=ALU.subtract).then_inc(xnl_made, 1)
            mix_low(1)
            dve.wait_ge(pool_made, DIST)
            dve.wait_ge(consts_loaded, CONSTS)
            for n in range(N_IN):
                if n >= 1:
                    mix_low(n + 1)
                ht, hs = n - 10, n - 9
                if n == 10:
                    dve.wait_ge(act_evac, 20)
                    for t in range(TT):
                        link(nc.vector.bn_stats(bn[:, t, :], vv[:, t, :]))
                        link(nc.vector.bn_aggr(mv[:, t, :], bn[:, t, :]))
                        nc.vector.tensor_scalar(stat[:, t, 4:5], mv[:, t, 1:2], EPS, None, ALU.add).then_inc(ln_var, 1)
                if n == 11:
                    dve.wait_ge(ln_root, 1)
                    link(nc.vector.reciprocal(stat[:, :, 6:7], stat[:, :, 5:6]))
                    for t in range(TT):
                        link(nc.vector.tensor_scalar(vv[:, t, :], vv[:, t, :], mv[:, t, 0:1], stat[:, t, 6:7],
                                                     ALU.subtract, ALU.mult))
                        link(nc.vector.tensor_tensor(vv[:, t, :], vv[:, t, :], lng[:], ALU.mult))
                        nc.vector.tensor_tensor(vv[:, t, :], vv[:, t, :], lnb[:], ALU.add).then_inc(ln_made, 1)
                if 0 <= hs < HEADS:
                    dve.wait_ge(scores_ready, hs + 1)
                    for i in range(TT):
                        w, a = P * (i + 1), sc_sb[i]
                        bank, col = sc_ps[i]
                        link(nc.vector.scalar_tensor_tensor(out=prob[:, a:a + w], in0=dist[:, SEQ - w:SEQ], scalar=slope[hs],
                                                            in1=ps[:, bank, col:col + w], op0=ALU.mult, op1=ALU.add))
                        nc.vector.tensor_reduce(negmax[:, hs % 2, i:i + 1], prob[:, a:a + w], AX_X, ALU.max,
                                                negate=True).then_inc(max_made, 1)
                if ht >= 0:
                    dve.wait_ge(ah_made, ht + 1)
                    q = (ht % 2) * 64
                    nc.vector.tensor_tensor(al[q:q + 64, ht // 2, :], ps[q:q + 64, 7, :],
                                            ah[q:q + 64, ht // 2, :].bitcast(F32), ALU.subtract).then_inc(al_made, 1)
                if 0 <= hs < HEADS:
                    dve.wait_ge(exp_made, 4 * hs + 4)
                    link(nc.vector.reciprocal(rinv[:, hs % 2, :], rowsum[:, hs % 2, :]))
                    for i in range(TT):
                        w, a = P * (i + 1), sc_sb[i]
                        nc.vector.tensor_scalar(prob[:, a:a + w], prob[:, a:a + w], rinv[:, hs % 2, i:i + 1], None,
                                                ALU.mult).then_inc(prob_made, 1)
            mix_low(N_IN + 1)
            for g in range(4):
                task = 2 * N_IN + g
                wait_task(dve, task)
                m4 = ps[:, task % 4, :].rearrange("p (c t) -> p c t", c=TT)
                nc.vector.tensor_tensor(lng[:].rearrange("p (c t) -> p c t", c=TT), m4, bsp[:, g:g + 1, :].broadcast_to((P, TT, P)),
                                        ALU.add).then_inc(dve_evac, 1)
                dve.wait_ge(dve_evac, g + 1)
                nc.vector.tensor_tensor(u[:, g, :], u[:, g, :], lng[:], ALU.mult).then_inc(sg_sum, 1)
                dve.wait_ge(sgh_made, g + 1)
                nc.vector.tensor_tensor(sgl[:, g, :], u[:, g, :], sgh[:, g, :].bitcast(F32), ALU.subtract).then_inc(sgl_made, 1)
            for d in range(KD):
                task = 2 * N_IN + 4 + d
                dve.wait_ge(sigm_made, d // 4 + 1)
                wait_task(dve, task)
                nc.vector.tensor_tensor(gates[:, d, :], gates[:, d, :], ps[:, task % 4, :], ALU.mult).then_inc(dve_evac, 1)
                if d % 4 == 3:
                    mix_low(N_IN + 2 + d // 4)

            def merged_low(d):
                dve.wait_ge(mh_made, d + 1)
                nc.vector.tensor_tensor(xnl[:, d, :], gates[:, d, :], xnh[:, d, :].bitcast(F32), ALU.subtract).then_inc(ml_made, 1)

            for d in range(KD):
                if d == 4:
                    mix_low(N_IN + 4)
                task = 2 * N_IN + 12 + d
                dve.wait_ge(sigm_made, 2 + d // 4 + 1)
                wait_task(dve, task)
                nc.vector.tensor_tensor(gates[:, KD + d, :], gates[:, KD + d, :], ps[:, task % 4, :], ALU.mult).then_inc(dve_evac, 1)
                dve.wait_ge(dve_evac, 4 + KD + d + 1)
                nc.vector.tensor_tensor(gates[:, d, :], gates[:, d, :], gates[:, KD + d, :], ALU.add).then_inc(merged, 1)
                if d >= 1:
                    merged_low(d - 1)
            merged_low(KD - 1)
            mix_low(N_IN + 5)
            dve.wait_ge(x_again, 16)

            def residual(n, c):
                task = 2 * N_IN + 20 + 2 * n + c
                wait_task(dve, task)
                part = h2[:, 2 * c:2 * c + 2, n * 256:(n + 1) * 256]
                nc.vector.tensor_tensor(part, part, ps[:, task % 4, :].rearrange("p (t d) -> p t d", t=2),
                                        ALU.add).then_inc(dve_evac, 1)

            for n in range(4):
                residual(n, 0)
                if n == 3:
                    break
                residual(n, 1)
                if n < 2:
                    mix_low(N_IN + 6 + n)
                if n == 1:
                    dve.wait_ge(bias_made, 1)
                    nc.vector.tensor_tensor(bias[E:2 * E, :], biasr[E:2 * E, :], bias[E:2 * E, :].bitcast(F32),
                                            ALU.subtract).then_inc(bias_made, 1)
                    dve.wait_ge(wr_loaded, 16)
                    nc.vector.tensor_tensor(wr[:], wr[:], fcol[:].unsqueeze(2).broadcast_to((P, KD, E)), ALU.mult).then_inc(wr_scaled, 1)

            def low(s, s_raw, number):
                dve.wait_ge(high_made, number)
                nc.vector.tensor_tensor(wlo_b[s][:], raw_b[s_raw][:], whi_b[s][:].bitcast(F32), ALU.subtract).then_inc(low_made, 1)

            def first_low(m):
                low(m % SPLIT_B, m % RAW_B, M0 + m + 1)

            first_low(0)
            residual(3, 1)
            for t in range(TT):
                dve.wait_ge(h2_sum, TT + t)
                nc.vector.tensor_scalar(stat[:, t, 1:2], stat[:, t, 0:1], 1.0 / D, EPS, ALU.mult, ALU.add).then_inc(h2_sum, 1)
            dve.wait_ge(h2_root, 1)
            link(nc.vector.reciprocal(stat[:, :, 3:4], stat[:, :, 2:3]))
            dve.wait_ge(frow_loaded, 16)
            for t in range(TT):
                nc.vector.scalar_tensor_tensor(out=hn[:, t, :], in0=h2[:, t, :], scalar=stat[:, t, 3:4], in1=frow[:],
                                               op0=ALU.mult, op1=ALU.mult).then_inc(hn_made, 1)

            for half in range(2):
                dve.wait_ge(lgT_done, half + 1)
                cols = slice(half * 256, (half + 1) * 256)
                nc.vector.tensor_copy(lgT[:, cols], ps[0:E, 4 + 3 * half, cols]).then_inc(lgT_made, 1)
            first_low(1)
            dve.wait_ge(logits_done, 1)
            dve.wait_ge(pool_made, ROUTE_CONSTS)
            for t in range(TT):
                ins = nc.vector.scalar_tensor_tensor(out=logits[:, t, :], in0=ps[:, 5, t * E:(t + 1) * E], scalar=stat[:, t, 3:4],
                                                     in1=brow[:], op0=ALU.mult, op1=ALU.add)
            link(ins)
            for t in range(TT):
                ins = nc.vector.max(top8[:, t, :], logits[:, t, :])
            link(ins)
            for t in range(TT):
                ins = nc.vector.max_index(idx8[:, t, :], top8[:, t, :], logits[:, t, :])
            link(ins)
            idxf3 = idxf[:].rearrange("p (t r) -> p t r", t=TT)
            link(nc.vector.tensor_copy(idxf3, idx8[:, :, 0:TOPK]))
            nc.vector.tensor_tensor(topw[:], top8[:, :, 0:TOPK], top8[:, :, 0:1].broadcast_to((P, TT, TOPK)),
                                    ALU.subtract).then_inc(exps_in, 1)
            link(nc.vector.tensor_tensor(pick[:], idxf[:].unsqueeze(2).broadcast_to((P, 16, E)),
                                         iota_e[:, 0:E].unsqueeze(1).broadcast_to((P, 16, E)), ALU.is_equal))
            with nc.allow_low_precision("zeros and ones are exact in bfloat16"):
                nc.vector.tensor_reduce(chosen[:], pick[:].rearrange("p (t r) e -> p t e r", t=TT), AX_X, ALU.add).then_inc(chosen_made, 1)
            dve.wait_ge(counted, 1)
            link(nc.vector.tensor_tensor(prod[:].rearrange("p (t r) e -> p t r e", t=TT), pick[:].rearrange("p (t r) e -> p t r e", t=TT),
                                         ps[:, 6, 0:TT * E].rearrange("p (t e) -> p t e", t=TT).unsqueeze(2).broadcast_to((P, TT, TOPK, E)),
                                         ALU.mult))
            nc.vector.tensor_reduce(rpos[:], prod[:], AX_X, ALU.add)
            cnt = ps[:, 6, TT * E:TT * E + E]
            link(nc.vector.tensor_scalar(spill[:], cnt, float(P), None, ALU.is_gt))
            for q in (2, 3):
                link(nc.vector.scalar_tensor_tensor(out=spill[:], in0=cnt, scalar=float(P * q), in1=spill[:],
                                                    op0=ALU.is_gt, op1=ALU.add))
            link(nc.vector.tensor_tensor_scan(incl[:], ones_e[:], spill[:], 0.0, ALU.mult, ALU.add))
            link(nc.vector.scalar_tensor_tensor(out=first[:], in0=incl[:], scalar=float(E - 1), in1=spill[:],
                                                op0=ALU.add, op1=ALU.subtract))
            link(nc.vector.tensor_tensor(prod[:], pick[:], first[:].unsqueeze(1).broadcast_to((P, 16, E)), ALU.mult))
            nc.vector.tensor_reduce(rfirst[:], prod[:], AX_X, ALU.add)
            link(nc.vector.tensor_scalar(over[:], rpos[:], float(P), None, ALU.is_ge))
            link(nc.vector.scalar_tensor_tensor(out=lap[:], in0=rpos[:], scalar=float(P * 2), in1=over[:], op0=ALU.is_ge, op1=ALU.add))
            link(nc.vector.scalar_tensor_tensor(out=lap[:], in0=rpos[:], scalar=float(P * 3), in1=lap[:], op0=ALU.is_ge, op1=ALU.add))
            nc.vector.scalar_tensor_tensor(out=rslot[:], in0=lap[:], scalar=-float(P), in1=rpos[:], op0=ALU.mult, op1=ALU.add)
            link(nc.vector.tensor_tensor(rblk[:], lap[:], rfirst[:], ALU.add))
            link(nc.vector.tensor_tensor(rblk[:], rblk[:], idxf[:], ALU.subtract))
            link(nc.vector.tensor_tensor(rblk[:], rblk[:], over[:], ALU.mult))
            link(nc.vector.tensor_tensor(rblk[:], rblk[:], idxf[:], ALU.add))
            nc.vector.tensor_tensor(hot_s[:], rslot[:].unsqueeze(2).broadcast_to((P, 16, P)),
                                    iota_s[:].unsqueeze(1).broadcast_to((P, 16, P)), ALU.is_equal)
            link(nc.vector.tensor_tensor(hot_b[:], rblk[:].unsqueeze(2).broadcast_to((P, 16, 48)),
                                         iota_e[:].unsqueeze(1).broadcast_to((P, 16, 48)), ALU.is_equal))
            nc.vector.tensor_scalar(hot_v[:, :, 0:48], hot_b[:], pcol[:, 0:1], None, ALU.mult)
            nc.vector.tensor_tensor(hot_v[:, :, 48:96], hot_b[:], kcol[:].unsqueeze(2).broadcast_to((P, 16, 48)),
                                    ALU.mult).then_inc(hot_made, 1)
            dve.wait_ge(exps_out, 1)
            link(nc.vector.tensor_reduce(wsum[:], topw[:], AX_X, ALU.add))
            link(nc.vector.reciprocal(wsum[:], wsum[:]))
            link(nc.vector.tensor_tensor(topw[:], topw[:], wsum[:].unsqueeze(2).broadcast_to((P, TT, TOPK)), ALU.mult))
            dve.wait_ge(table_done, 1)
            a_, b_ = ps[:, 7, 0:48], ps[:, 7, 48:96]
            nc.vector.tensor_scalar(skp[:], b_, 0.5, SKIP, ALU.is_lt, ALU.mult)
            link(nc.vector.tensor_scalar(rnk[:], b_, 4.5, None, ALU.is_gt))
            link(nc.vector.scalar_tensor_tensor(out=rnk[:], in0=b_, scalar=8.5, in1=rnk[:], op0=ALU.is_gt, op1=ALU.add))
            link(nc.vector.scalar_tensor_tensor(out=rnk[:], in0=b_, scalar=12.5, in1=rnk[:], op0=ALU.is_gt, op1=ALU.add))
            link(nc.vector.scalar_tensor_tensor(out=row[:], in0=b_, scalar=float(P), in1=skp[:], op0=ALU.mult, op1=ALU.add))
            link(nc.vector.scalar_tensor_tensor(out=row[:], in0=row[:], scalar=-float(P), in1=a_, op0=ALU.add, op1=ALU.add))
            nc.vector.scalar_tensor_tensor(out=xidx[:], in0=rnk[:], scalar=-float(SEQ), in1=row[:], op0=ALU.mult,
                                           op1=ALU.add).then_inc(xidx_ready, 1)
            nc.vector.tensor_copy(yidx[:], row[:])
            link(nc.vector.tensor_scalar(exf[:], iota_e[:], -float(E), None, ALU.add))
            link(nc.vector.tensor_tensor(ended[:], incl[:].unsqueeze(1).broadcast_to((P, BLOCKS, E)),
                                         exf[:].unsqueeze(2).broadcast_to((P, BLOCKS, E)), ALU.is_le))
            link(nc.vector.tensor_reduce(exf[:], ended[:], AX_X, ALU.add))
            link(nc.vector.scalar_tensor_tensor(out=exf[:], in0=exf[:], scalar=float(E - 1), in1=own[:], op0=ALU.min, op1=ALU.add))
            nc.vector.tensor_copy(expert_of[:], exf[:])
            link(nc.vector.tensor_scalar(nbf[:], incl[:, E - 1:E], float(E), None, ALU.add))
            nc.vector.tensor_copy(n_blocks[:], nbf[:]).then_inc(tables_ready, 1)
            link(nc.vector.tensor_scalar(late[:], rblk[:], nbf[:, 0:1], -1.0, ALU.subtract, ALU.is_equal))
            topw16 = topw[:].rearrange("p t r -> p (t r)")
            link(nc.vector.tensor_tensor(late[:], late[:], topw16, ALU.mult))
            nc.vector.tensor_reduce(wlate[:], late[:].rearrange("p (t r) -> p t r", t=TT), AX_X, ALU.add)
            link(nc.vector.tensor_tensor(topw16, topw16, late[:], ALU.subtract))
            first_low(2)
            first_low(3)

            def tokens_low(e):
                dve.wait_ge(xth_made, e + 1)
                nc.vector.tensor_tensor(xtl[:], t_ps.rearrange("p (k s) -> p k s", k=KD), xth[:].bitcast(F32),
                                        ALU.subtract).then_inc(xtl_made, 1)

            def hidden_low(e):
                dve.wait_ge(hth_made, e + 1)
                nc.vector.tensor_tensor(htl[:], t_ps.rearrange("p (k s) -> p k s", k=KD), hth[:].bitcast(F32),
                                        ALU.subtract).then_inc(htl_made, 1)

            def gate(e):
                dve.wait_ge(gu_done, e + 1)
                nc.vector.tensor_scalar(gm[:], gu_ps[:, 0, :], LIMIT, None, ALU.min).then_inc(gate_made, 1)

            def up(e):
                nc.vector.tensor_scalar(um[:], gu_ps[:, 1, :], LIMIT, -LIMIT, ALU.min, ALU.max).then_inc(up_made, 1)

            def product(e):
                dve.wait_ge(up_made, e + 1)
                nc.vector.scalar_tensor_tensor(out=um[:], in0=um[:], scalar=1.0, in1=gm[:], op0=ALU.add,
                                               op1=ALU.mult).then_inc(gu_mult, 1)

            def hidden(e):
                dve.wait_ge(gu_mult, e + 1)
                dve.wait_ge(sig_made, e + 1)
                nc.vector.tensor_tensor(hid[:], um[:], sg[:], ALU.mult).then_inc(hid_made, 1)

            tokens_low(0)
            for m in range(4, 8):
                first_low(m)

            def loop_low(e, j):
                s, s_raw = (GU_P + j) % SPLIT_B, (GU_P + j) % RAW_B
                dve.wait_ge(high_made, (e - 1) * PER_E + (M0 + GU_P + j + 1))
                nc.vector.tensor_tensor(wlo_b[s][:], raw_b[s_raw][:], whi_b[s][:].bitcast(F32), ALU.subtract).then_inc(low_made, 1)

            loop_low(1, 0)
            loop_low(1, 1)
            tokens_low(1)
            gate(0)
            up(0)
            nb = dve.value_load(n_blocks[0:1, 0:1], min_val=E, max_val=E + MAX_OVER)
            with dve.Fori(1, nb) as e:
                for j in range(PER_E):
                    loop_low(e, j + 2)
                    if j == 0:
                        product(e - 1)
                    if j == 1:
                        hidden(e - 1)
                    if j == 4:
                        hidden_low(e - 1)
                    if j == 8:
                        tokens_low(e + 1)
                    if j == 9:
                        gate(e)
                    if j == 10:
                        up(e)
            product(nb - 1)
            hidden(nb - 1)
            loop_low(nb, 2)
            hidden_low(nb - 1)
            loop_low(nb, 3)
            dve.wait_ge(pool_made, LATE_CONSTS)
            nc.vector.tensor_scalar(hot_t[:], iota_t[:], xlast[:, 0:1], None, ALU.is_equal).then_inc(hot_t_made, 1)

            def halves_of_last():
                dve.wait_ge(yh_made, 1)
                nc.vector.tensor_tensor(yl[:], y_ps, yh[:].bitcast(F32), ALU.subtract).then_inc(yl_made, 1)

            def final_norm(t):
                dve.wait_ge(fin_sum, 2 * t + 1)
                nc.vector.tensor_scalar(stat[:, t, 1:2], stat[:, t, 0:1], 1.0 / D, EPS, ALU.mult, ALU.add).then_inc(fin_sum, 1)
                dve.wait_ge(fin_root, t + 1)
                link(nc.vector.reciprocal(stat[:, t, 3:4], stat[:, t, 2:3]))
                nc.vector.scalar_tensor_tensor(out=h2[:, t, :], in0=h2[:, t, :], scalar=stat[:, t, 3:4], in1=gfin[:],
                                               op0=ALU.mult, op1=ALU.mult).then_inc(fin_made, 1)

            def add_last(t):
                dve.wait_ge(late_placed, t + 1)
                dve.wait_ge(acc_made, 8 * (t // 2) + 8)
                nc.vector.scalar_tensor_tensor(out=h2[:, t, :], in0=ps[:, 2 * t:2 * t + 2, :].rearrange("p b c -> p (b c)"),
                                               scalar=wlate[:, t:t + 1], in1=h2[:, t, :], op0=ALU.mult,
                                               op1=ALU.add).then_inc(late_added, 1)

            dve.wait_ge(bias_loaded, 16 * 5)
            for pair in range(TT // 2):
                for i in range(4 * pair, 4 * pair + 4, 2):
                    for r2 in range(2):
                        for n in (i, i + 1):
                            t, half = y_load(n)
                            if r2 == 0:
                                dve.wait_ge(y_loaded[n % RAW_B], 16 * (n // RAW_B + 1))
                            number = 2 * i + 2 * r2 + n - i
                            if number >= 8 * pair + 2:
                                dve.wait_ge(acc_made, number - 1)
                            rank = 2 * half + r2
                            nc.vector.scalar_tensor_tensor(out=h2[:, t, :], in0=raw_b[n % RAW_B][:, r2 * D:(r2 + 1) * D],
                                                           scalar=topw[:, t, rank:rank + 1], in1=h2[:, t, :], op0=ALU.mult,
                                                           op1=ALU.add).then_inc(acc_made, 1)
                if pair == 0:
                    halves_of_last()
                add_last(2 * pair)
                add_last(2 * pair + 1)
                final_norm(2 * pair)
                final_norm(2 * pair + 1)

        @block.tensor
        def _(pe):
            def three(out_ap, sta, mov, first, last):
                nc.tensor.matmul(out_ap, sta[0], mov[0], start=first, stop=False)
                nc.tensor.matmul(out_ap, sta[0], mov[1], start=False, stop=False)
                return nc.tensor.matmul(out_ap, sta[1], mov[0], start=False, stop=last)

            def wait_bank(task):
                if task < 4:
                    return
                if task - 4 < 2 * N_IN:
                    pe.wait_ge(act_evac, task - 3)
                else:
                    pe.wait_ge(dve_evac, task - 4 - 2 * N_IN + 1)

            def turned_task(n, c, task, mov, kt, col):
                wait_bank(task)
                hi, lo = mix_slot(n)
                for k in range(kt):
                    if task == 0:
                        pe.wait_ge(xnl_made, k + 1)
                    ins = three(ps[:, task % 4, :], (hi[:, k, col:col + P], lo[:, k, col:col + P]),
                                (mov[0][:, k, :], mov[1][:, k, :]), k == 0, k == kt - 1)
                ins.then_inc(piece_used if ends_piece[task] else task_done, 1)

            def token_task(n, c, task):
                wait_bank(task)
                hi, lo = mix_slot(n)
                for i in range(2):
                    if task == len(task_piece) - 1 and i == 1:
                        turn_h2(0)
                    tok = slice((2 * c + i) * P, (2 * c + i + 1) * P)
                    for k in range(KD):
                        ins = three(ps[:, task % 4, i * 256:(i + 1) * 256], (xnh[:, k, tok], xnl[:, k, tok]),
                                    (hi[:, k, :], lo[:, k, :]), k == 0, k == KD - 1)
                ins.then_inc(piece_used if ends_piece[task] else task_done, 1)

            def turn_h2(half):
                pe.wait_ge(dve_evac, H2_DONE - 1 + half)
                for b in range(4):
                    for k in (2 * b, 2 * b + 1):
                        for i in range(2):
                            a = (k % 2) * 256 + i * P
                            ins = nc.tensor.transpose(ps[:, 4 - 4 * half + b, a:a + P], h2[:, 2 * half + i, k * P:(k + 1) * P], ident[:])
                    ins.then_inc(h2_turned, 1)

            pe.wait_ge(pool_made, IDENT)
            for k in range(KD):
                for t in range(TT):
                    if k == 0:
                        pe.wait_ge(xn_made, t + 1)
                    ins = nc.tensor.transpose(ps[:, k, t * P:(t + 1) * P], xn[:, t, k * P:(k + 1) * P], ident[:])
                ins.then_inc(xT_turned, 1)

            def turn_spatial():
                pe.wait_ge(wsp_loaded, 16)
                for c in range(2):
                    for g in range(4):
                        ins = nc.tensor.transpose(ps[:, 4 + c, g * P:(g + 1) * P], wsp[:, 4 * c + g, :], ident[:])
                    ins.then_inc(wsp_turned, 1)

            def scores(h):
                pe.wait_ge(act_evac, 8)
                if h == 0:
                    pe.wait_ge(wspT_made, 2)
                else:
                    pe.wait_ge(probT_made, h)
                q, pair = (h % 2) * 64, h // 2
                for i in (3, 2, 0, 1):
                    bank, col = sc_ps[i]
                    w = P * (i + 1)
                    ins = nc.tensor.matmul(ps[:, bank, col:col + w], qT[q:q + 64, pair, i * P:(i + 1) * P],
                                           kT[q:q + 64, pair, 0:w], start=True, stop=True)
                ins.then_inc(scores_ready, 1)

            def turn_prob(h):
                pe.wait_ge(prob_made, 4 * h + 4)
                for i in range(TT):
                    for j in range(i + 1):
                        a = pt_at[j] + (i - j) * P
                        ins = nc.tensor.transpose(ps46[:, a:a + P], prob[:, sc_sb[i] + j * P:sc_sb[i] + (j + 1) * P], ident[:])
                ins.then_inc(prob_turned, 1)

            def weigh(h):
                pe.wait_ge(probT_made, h + 1)
                pe.wait_ge(act_evac, 12)
                if h >= 1:
                    pe.wait_ge(al_made, h)
                q = (h % 2) * 64
                for j in range(TT):
                    ins = nc.tensor.matmul(ps[q:q + 64, 7, j * P:SEQ], v[:, j, h * HD:(h + 1) * HD],
                                           probT[:, pt_at[j]:pt_at[j] + SEQ - j * P], start=(j == 0), stop=(j == TT - 1))
                ins.then_inc(head_done, 1)

            xT = (xnh, xnl)
            for n in range(N_IN):
                pe.wait_ge(low_made, n + 1)
                by_token = 4 <= n < 6 or 8 <= n < 10
                for c in range(2):
                    if by_token:
                        token_task(n, c, 2 * n + c)
                    else:
                        turned_task(n, c, 2 * n + c, xT, KD, c * P)
                    if c == 0 and n >= 10:
                        turn_prob(n - 10)
                if n == 0:
                    turn_spatial()
                if 0 <= n - 9 < HEADS:
                    scores(n - 9)
                if n >= 10:
                    weigh(n - 10)
            pe.wait_ge(ln_made, TT)
            pe.wait_ge(wsp_masked, 1)
            for g in range(4):
                task = 2 * N_IN + g
                wait_bank(task)
                for c in range(TT):
                    for half in range(2):
                        q = half * 64
                        ins = nc.tensor.matmul(ps[q:q + 64, task % 4, c * P:(c + 1) * P],
                                               vv[:, c, (2 * g + half) * 64:(2 * g + half + 1) * 64],
                                               wspT[:, 2 * g + half, :], start=True, stop=True)
                ins.then_inc(task_done, 1)
            for n in range(N_IN, N_IN + 4):
                attn = n < N_IN + 2
                pe.wait_ge(low_made, n + 1)
                if n == N_IN:
                    pe.wait_ge(al_made, HEADS)
                if n == N_IN + 2:
                    pe.wait_ge(sgl_made, 4)
                for c in range(4):
                    turned_task(n, c, 2 * N_IN + 4 + 4 * (n - N_IN) + c, (ah, al) if attn else (sgh, sgl), 4, c * P)
            for n in range(N_IN + 4, N_MIX):
                pe.wait_ge(low_made, n + 1)
                pe.wait_ge(ml_made, KD)
                for c in range(2):
                    token_task(n, c, 2 * N_IN + 20 + 2 * (n - N_IN - 4) + c)

            pe.wait_ge(wr_scaled, 1)
            for half in range(2):
                if half == 1:
                    turn_h2(1)
                for k in range(KD):
                    pe.wait_ge(hT_made, 4 * half + k // 2 + 1)
                    cols = slice(half * 256, (half + 1) * 256)
                    ins = nc.tensor.matmul(ps[0:E, 4 + 3 * half, cols], wr[:, k, :], hT[:, k, cols], start=(k == 0), stop=(k == KD - 1))
                ins.then_inc(lgT_done, 1)
            for t in range(TT):
                pe.wait_ge(lgT_made, t // 2 + 1)
                ins = nc.tensor.transpose(ps[:, 5, t * E:(t + 1) * E], lgT[:, t * P:(t + 1) * P], ident[0:E, 0:E])
            ins.then_inc(logits_done, 1)
            pe.wait_ge(chosen_made, 1)
            for t in range(TT):
                dst = ps[:, 6, t * E:(t + 1) * E]
                for s in range(t):
                    nc.tensor.matmul(dst, onesb[:], chosen[:, s, :], start=(s == 0), stop=False)
                nc.tensor.matmul(dst, before[:], chosen[:, t, :], start=(t == 0), stop=True)
            for s in range(TT):
                ins = nc.tensor.matmul(ps[:, 6, TT * E:TT * E + E], onesb[:], chosen[:, s, :], start=(s == 0), stop=(s == TT - 1))
            ins.then_inc(counted, 1)
            pe.wait_ge(hot_made, 1)
            for i in range(16):
                ins = nc.tensor.matmul(ps[:, 7, 0:96], hot_s[:, i, :], hot_v[:, i, :], start=(i == 0), stop=(i == 15))
            ins.then_inc(table_done, 1)

            def turn_tokens(landed, used):
                pe.wait_ge(x_landed, landed)
                pe.wait_ge(htl_made, used) if used is not None else None
                for k in range(KD):
                    ins = nc.tensor.transpose(t_ps[:, k * P:(k + 1) * P], xgat[:, k * P:(k + 1) * P], ident[:])
                ins.then_inc(x_turned, 1)

            def turn_hidden(e, tokens):
                pe.wait_ge(hid_made, e + 1)
                pe.wait_ge(xtl_made, tokens)
                for k in range(KD):
                    a = (k // 2) * 256 + k % 2
                    ins = nc.tensor.transpose(t_ps[:, k * P:(k + 1) * P], hid[:, a:a + 255:2], ident[:])
                ins.then_inc(hid_turned, 1)

            def gate_up_ready(e, tokens):
                pe.wait_ge(xtl_made, tokens)
                if e is not None:
                    pe.wait_ge(gate_made, e)
                    pe.wait_ge(up_made, e)

            def gate_up_bias(sel):
                pe.wait_ge(selh_made, sel)
                for q in range(4):
                    ins = nc.tensor.matmul(ps[:, q, :], selh[:], bias[:, q * 512:(q + 1) * 512], start=False, stop=True)
                ins.then_inc(gu_done, 1)

            def gate_up_piece(j, s, number):
                pe.wait_ge(low_made, number)
                for q in range(4):
                    cols = slice(q * 512, (q + 1) * 512)
                    ins = three(ps[:, q, :], (xth[:, j, :], xtl[:, j, :]), (whi_b[s][:, cols], wlo_b[s][:, cols]),
                                j == 0, False)
                ins.then_inc(piece_used, 1)

            def down_ready(halves):
                pe.wait_ge(htl_made, halves)

            def down_bias(sel):
                pe.wait_ge(seld_made, sel)
                for q in range(2):
                    ins = nc.tensor.matmul(ps[:, 6 + q, :], seld[:], bias[:, 2 * D + q * 512:2 * D + (q + 1) * 512],
                                           start=False, stop=True)
                ins.then_inc(y_done, 1)

            def down_piece(i, s, number):
                pe.wait_ge(low_made, number)
                for two in range(2):
                    k = 2 * i + two
                    for q in range(2):
                        cols = slice(two * D + q * 512, two * D + (q + 1) * 512)
                        ins = three(ps[:, 6 + q, :], (hth[:, k, :], htl[:, k, :]), (whi_b[s][:, cols], wlo_b[s][:, cols]),
                                    k == 0, False)
                ins.then_inc(piece_used, 1)

            pe.wait_ge(bias_made, 2)
            turn_tokens(16, None)
            gate_up_ready(None, 1)
            for j in range(GU_P):
                gate_up_piece(j, j % SPLIT_B, M0 + j + 1)
            gate_up_bias(1)
            turn_tokens(32, None)
            pe.wait_ge(tables_ready, 1)
            nb = pe.value_load(n_blocks[0:1, 0:1], min_val=E, max_val=E + MAX_OVER)
            with pe.Fori(1, nb) as e:
                gate_up_ready(e, e + 1)
                for j in range(PER_E):
                    number = (e - 1) * PER_E + (M0 + GU_P + j + 1)
                    if j == 4:
                        turn_hidden(e - 1, e + 1)
                    if j == GU_P:
                        gate_up_bias(e + 1)
                        turn_tokens(e * 16 + 32, e)
                        down_ready(e)
                    if j < GU_P:
                        gate_up_piece(j, (GU_P + j) % SPLIT_B, number)
                    else:
                        down_piece(j - GU_P, (GU_P + j) % SPLIT_B, number)
                down_bias(e)
            turn_hidden(nb - 1, nb + 1)
            down_ready(nb)
            for i in range(4):
                down_piece(i, (GU_P + i) % SPLIT_B, nb * PER_E + (M0 + GU_P - PER_E + i + 1))
            down_bias(nb)
            pe.wait_ge(hot_t_made, 1)
            pe.wait_ge(up_made, nb)
            pe.wait_ge(yl_made, 1)
            for t in range(TT):
                for q in range(2):
                    cols = slice(q * 512, (q + 1) * 512)
                    nc.tensor.matmul(ps[:, 2 * t + q, :], hot_t[:, t * P:(t + 1) * P], yh[:, cols], start=True, stop=False)
                    ins = nc.tensor.matmul(ps[:, 2 * t + q, :], hot_t[:, t * P:(t + 1) * P], yl[:, cols], start=False, stop=True)
                ins.then_inc(late_placed, 1)


_INS = ["x", "mix_norm_g", "w_in", "w_attn_out", "sgu_ln_g", "sgu_ln_b", "w_spatial", "b_spatial", "w_sgu_out", "w_mix_out",
        "ffn_norm_g", "w_router", "b_router", "w_gate_up", "b_gate_up", "w_down", "b_down", "final_norm_g"]


def kernel(**inputs):
    import numpy as np
    import concourse.bacc as bacc
    from concourse.bass_utils import run_bass_kernel_spmd

    nc = bacc.Bacc("TRN2", target_bir_lowering=False, num_devices=1)
    arrays, args = {}, []
    for name in _INS:
        a = np.ascontiguousarray(inputs[name])
        arrays[f"in_{name}"] = a
        args.append(nc.dram_tensor(f"in_{name}", a.shape, mybir.dt.from_np(a.dtype), kind="ExternalInput").ap())
    args.append(nc.dram_tensor("out_0", (1, SEQ, D), F32, kind="ExternalOutput").ap())
    build(nc, *args)
    r = run_bass_kernel_spmd(nc, [arrays], core_ids=[0])
    return r.results[0]["out_0"]
```

```python
from contextlib import ExitStack

import concourse.bass as bass
from concourse import mybir

F32 = mybir.dt.float32
F32R = mybir.dt.float32r
BF16 = mybir.dt.bfloat16
I32 = mybir.dt.int32
U32 = mybir.dt.uint32
ALU = mybir.AluOpType
ACT = mybir.ActivationFunctionType
AX_X = mybir.AxisListType.X

P = 128
D = 1024
KD = D // P
SEQ = 512
TT = SEQ // P
HEADS, HD = 8, 64
ATTN_W = HEADS * HD
SGU_W = D // 2
GROUPS = 8
E = 32
TOPK = 4
EPS = 1e-5
LIMIT, ALPHA = 7.0, 1.702
FAR = -1.0e30
SKIP = 65536.0

PIECE = 2048
N_IN = (3 * ATTN_W + 2 * SGU_W + 2 * D) // 256
N_MIX = N_IN + 2 + 2 + D // 256
RAW_A, SPLIT_A = 3, 2
RAW_B, SPLIT_B = 6, 4
EARLY = RAW_B + 2
PER_E = 12
GU_P = 8
MAX_OVER = (SEQ * TOPK) // (P + 1)
BLOCKS = 48
IDENT, DIST, ROUTE_CONSTS, LATE_CONSTS = 2, 4, 11, 19
CONSTS = 16 * (3 + GROUPS + 1)
assert E + MAX_OVER < BLOCKS and PER_E % RAW_B == 0 and PER_E % SPLIT_B == 0


def build(nc, x, mix_norm_g, w_in, w_attn_out, sgu_ln_g, sgu_ln_b, w_spatial, b_spatial, w_sgu_out, w_mix_out,
          ffn_norm_g, w_router, b_router, w_gate_up, b_gate_up, w_down, b_down, final_norm_g, out):
    ctx = ExitStack()
    with ctx:
        base = -(-nc.sbuf_base // 64) * 64

        def at(offset, shape, dt, name):
            return nc.alloc_sbuf_tensor_at(name, shape, dt, offset=base + offset)

        K = 1024
        raw = [at(8 * K * s, [P, PIECE], F32, f"raw{s}") for s in range(RAW_A)]
        whi = [at(24 * K + 8 * K * s, [P, PIECE], F32R, f"whi{s}") for s in range(SPLIT_A)]
        wlo = [at(40 * K + 8 * K * s, [P, PIECE], F32R, f"wlo{s}") for s in range(SPLIT_A)]
        h2 = at(56 * K, [P, TT, D], F32, "h2")
        qT = at(56 * K, [P, HEADS // 2, SEQ], F32, "qT")
        kT = at(64 * K, [P, HEADS // 2, SEQ], F32, "kT")
        S0 = 72 * K
        small_at = [S0]

        def small(shape, dt, name):
            n = 1
            for v in shape[1:]:
                n *= v
            size = -(-n * (2 if dt == BF16 else 4) // 64) * 64
            t = at(small_at[0], shape, dt, name)
            small_at[0] += size
            return t

        ident = small([P, P], F32, "ident")
        gcol = small([P, KD], F32, "gcol")
        fcol = small([P, KD], F32, "fcol")
        stat = small([P, 4, 8], F32, "stat")
        bn = small([P, TT, 6], F32, "bn")
        mv = small([P, TT, 2], F32, "mv")
        negmax = small([P, 2, 4], F32, "negmax")
        rowsum = small([P, 2, 4], F32, "rowsum")
        rinv = small([P, 2, 4], F32, "rinv")
        top8 = small([P, TT, 8], F32, "top8")
        idx8 = small([P, TT, 8], U32, "idx8")
        topw = small([P, TT, TOPK], F32, "topw")
        wsum = small([P, TT], F32, "wsum")
        xidx = small([P, BLOCKS + 1], I32, "xidx")
        yidx = small([P, BLOCKS], I32, "yidx")
        expert_of = small([P, BLOCKS], I32, "expert_of")
        n_blocks = small([P, 1], I32, "n_blocks")
        cur_x = small([P, 1], I32, "cur_x")
        cur_y = small([P, 1], I32, "cur_y")
        late = small([P, 16], F32, "late")
        wlate = small([P, TT], F32, "wlate")
        xlast = small([P, 1], F32, "xlast")
        brow = small([P, E], F32, "brow")
        assert small_at[0] <= 76 * K, small_at[0]

        A0 = 76 * K
        xnh = at(A0, [P, KD, SEQ], F32R, "xnh")
        xnl = at(A0 + 16 * K, [P, KD, SEQ], F32R, "xnl")
        gates = at(A0 + 32 * K, [P, 2 * KD, SEQ], F32, "gates")
        x_in = at(A0 + 32 * K, [P, TT, D], F32, "x_in")
        xn = at(A0 + 48 * K, [P, TT, D], F32, "xn")
        v = at(A0 + 64 * K, [P, TT, ATTN_W], F32, "v")
        sgh = at(A0 + 64 * K, [P, 4, SEQ], F32R, "sgh")
        prob = at(A0 + 72 * K, [P, 1280], F32, "prob")
        probT = at(A0 + 77 * K, [P, 1280], F32, "probT")
        sgl = at(A0 + 72 * K, [P, 4, SEQ], F32R, "sgl")
        u = at(A0 + 82 * K, [P, 4, SEQ], F32, "u")
        vv = at(A0 + 90 * K, [P, TT, SGU_W], F32, "vv")
        wsp = at(A0 + 90 * K, [P, GROUPS, P], F32, "wsp")
        ah = at(A0 + 98 * K, [P, HEADS // 2, SEQ], F32R, "ah")
        al = at(A0 + 106 * K, [P, HEADS // 2, SEQ], F32R, "al")
        wspT = at(A0 + 114 * K, [P, GROUPS, P], F32, "wspT")
        dist = at(A0 + 118 * K, [P, SEQ], F32, "dist")
        lng = at(A0 + 120 * K, [P, SGU_W], F32, "lng")
        lnb = at(A0 + 122 * K, [P, SGU_W], F32, "lnb")
        bsp = at(A0 + 124 * K, [P, 4, P], F32, "bsp")
        assert 76 + 126 <= 207

        R0 = A0 + 64 * K
        hn = at(R0, [P, TT, D], F32, "hn")
        hT = at(R0 + 16 * K, [P, KD, SEQ], F32, "hT")
        wr = at(R0 + 32 * K, [P, KD, E], F32, "wr")
        frow = at(A0 + 60 * K, [P, D], F32, "frow")
        rt_at = [0]

        def region(offset):
            rt_at[0] = offset

        def rt(shape, dt, name):
            n = 1
            for w in shape[1:]:
                n *= w
            t = at(rt_at[0], shape, dt, name)
            rt_at[0] += -(-n * (2 if dt == BF16 else 4) // 64) * 64
            return t

        region(R0 + 33 * K)
        iota_e = rt([P, 48], F32, "iota_e")
        iota_s = rt([P, P], F32, "iota_s")
        pcol = rt([P, 1], F32, "pcol")
        kcol = rt([P, 16], F32, "kcol")
        before = rt([P, P], BF16, "before")
        onesb = rt([P, P], BF16, "onesb")
        ones_e = rt([P, E], F32, "ones_e")
        chosen = rt([P, TT, E], BF16, "chosen")
        logits = rt([P, TT, E], F32, "logits")
        assert rt_at[0] <= R0 + 36 * K
        region(A0 + 128 * K)
        lgT = rt([E, SEQ], F32, "lgT")
        spill = rt([P, E], F32, "spill")
        incl = rt([P, E], F32, "incl")
        first = rt([P, E], F32, "first")
        idxf, rpos, rfirst, lap, over, rslot, rblk = (rt([P, 16], F32, n) for n in
                                                      ("idxf", "rpos", "rfirst", "lap", "over", "rslot", "rblk"))
        nbf = rt([P, 1], F32, "nbf")
        assert rt_at[0] <= A0 + 131 * K, rt_at[0] - A0
        region(R0 + 16 * K)
        pick = rt([P, 16, E], F32, "pick")
        prod = rt([P, 16, E], F32, "prod")
        hot_s = rt([P, 16, P], BF16, "hot_s")
        hot_b = rt([P, 16, 48], F32, "hot_b")
        hot_v = rt([P, 16, 96], BF16, "hot_v")
        row = rt([P, 48], F32, "row")
        rnk = rt([P, 48], F32, "rnk")
        skp = rt([P, 48], F32, "skp")
        exf = rt([P, 16], F32, "exf")
        assert rt_at[0] <= R0 + 32 * K
        ended = at(R0 + 16 * K, [P, 16, E], F32, "ended")

        raw_b = raw + [at(A0 + 32 * K + 8 * K * s, [P, PIECE], F32, f"raw{3 + s}") for s in range(RAW_B - RAW_A)]
        raw_b += [at(A0 + 120 * K, [P, PIECE], F32, "raw6"), at(A0 + 112 * K, [P, PIECE], F32, "raw7")]
        whi_b = whi + [at(A0 + 8 * K * s, [P, PIECE], F32R, f"whi{2 + s}") for s in range(SPLIT_B - SPLIT_A)]
        wlo_b = wlo + [at(A0 + 16 * K + 8 * K * s, [P, PIECE], F32R, f"wlo{2 + s}") for s in range(SPLIT_B - SPLIT_A)]
        biasr = at(A0 + 119 * K, [2 * E, 3 * D], F32, "biasr")
        selh = at(A0 + 56 * K, [2 * E, P], F32R, "selh")
        seld = at(A0 + 56 * K + 512, [2 * E, P], F32R, "seld")
        selt = at(A0 + 57 * K, [2 * E, BLOCKS], F32, "selt")
        xgat = at(A0 + 60 * K, [P, D], F32, "xgat")
        B0 = A0 + 64 * K
        xth = at(B0, [P, KD, P], F32R, "xth")
        xtl = at(B0 + 4 * K, [P, KD, P], F32R, "xtl")
        hth = at(B0 + 8 * K, [P, KD, P], F32R, "hth")
        htl = at(B0 + 12 * K, [P, KD, P], F32R, "htl")
        hid = at(B0 + 16 * K, [P, D], F32, "hid")
        gm = at(B0 + 20 * K, [P, D], F32, "gm")
        um = at(B0 + 24 * K, [P, D], F32, "um")
        sg = at(B0 + 28 * K, [P, D], F32, "sg")
        yb = at(B0 + 32 * K, [P, D], F32, "yb")
        bias = at(B0 + 36 * K, [2 * E, 3 * D], F32R, "bias")
        gfin = at(A0 + 116 * K, [P, D], F32, "gfin")
        iota_t = at(A0 + 112 * K, [P, SEQ], F32, "iota_t")
        hot_t = at(A0 + 114 * K, [P, SEQ], F32R, "hot_t")
        yh = at(B0, [P, D], F32R, "yh")
        yl = at(B0 + 4 * K, [P, D], F32R, "yl")

        ps = ctx.enter_context(nc.psum_tensor("ps", [P, 8, 512], F32))
        hn_dram = nc.dram_tensor("hn_dram", (SEQ, D), F32).ap()
        y_dram = nc.dram_tensor("y_dram", (SEQ * TOPK, D), F32).ap()

        def sem(name):
            return ctx.enter_context(nc.semaphore(name))

        raw_landed = [sem(f"raw_landed{s}") for s in range(EARLY)]
        x_loaded = [sem(f"x_loaded{t}") for t in range(TT)]
        gcol_loaded = sem("gcol_loaded")
        consts_loaded = sem("consts_loaded")
        wsp_loaded = sem("wsp_loaded")
        x_again = sem("x_again")
        bias_loaded = sem("bias_loaded")
        wr_loaded, frow_loaded = sem("wr_loaded"), sem("frow_loaded")
        high_made, low_made, piece_used = sem("high_made"), sem("low_made"), sem("piece_used")
        pool_made = sem("pool_made")
        dve_step = sem("dve_step")
        mean_made = sem("mean_made")
        sum_made, root_made, xn_made = sem("sum_made"), sem("root_made"), sem("xn_made")
        xT_turned, xnh_made, xnl_made = sem("xT_turned"), sem("xnh_made"), sem("xnl_made")
        wsp_turned, wspT_made, wsp_masked = sem("wsp_turned"), sem("wspT_made"), sem("wsp_masked")
        task_done, act_evac, dve_evac = sem("task_done"), sem("act_evac"), sem("dve_evac")
        scores_ready, max_made, exp_made, prob_made = sem("scores_ready"), sem("max_made"), sem("exp_made"), sem("prob_made")
        prob_turned, probT_made, head_done, ah_made, al_made = (sem("prob_turned"), sem("probT_made"),
                                                                sem("head_done"), sem("ah_made"), sem("al_made"))
        ln_var, ln_root, ln_made = sem("ln_var"), sem("ln_root"), sem("ln_made")
        sg_sum, sgh_made, sgl_made = sem("sg_sum"), sem("sgh_made"), sem("sgl_made")
        sigm_made, merged, mh_made, ml_made = sem("sigm_made"), sem("merged"), sem("mh_made"), sem("ml_made")
        hg_made, rinv_made = sem("hg_made"), sem("rinv_made")
        h2_sum, h2_root, hn_made, hn_stored = sem("h2_sum"), sem("h2_root"), sem("hn_made"), sem("hn_stored")
        h2_turned, hT_made, wr_scaled, lgT_done, lgT_made = (sem("h2_turned"), sem("hT_made"), sem("wr_scaled"),
                                                             sem("lgT_done"), sem("lgT_made"))
        logits_done, chosen_made = sem("logits_done"), sem("chosen_made")
        counted, hot_s_made, table_done = sem("counted"), sem("hot_s_made"), sem("table_done")
        xidx_ready, tables_ready = sem("xidx_ready"), sem("tables_ready")
        exps_in, exps_out = sem("exps_in"), sem("exps_out")
        bias_made = sem("bias_made")
        idx_copied, idx_seen, x_landed, y_stored = sem("idx_copied"), sem("idx_seen"), sem("x_landed"), sem("y_stored")
        half_turned, half_high, half_low = sem("half_turned"), sem("half_high"), sem("half_low")
        hot_b_made, hot_a_made, hot_k_made = sem("hot_b_made"), sem("hot_a_made"), sem("hot_k_made")
        selh_made, seld_made = sem("selh_made"), sem("seld_made")
        x_turned, xth_made, xtl_made = sem("x_turned"), sem("xth_made"), sem("xtl_made")
        gu_done, gate_made, up_made, sig_made, gu_mult, hid_made = (
            sem("gu_done"), sem("gate_made"), sem("up_made"), sem("sig_made"), sem("gu_mult"), sem("hid_made"))
        hid_turned, hth_made, htl_made = sem("hid_turned"), sem("hth_made"), sem("htl_made")
        y_done, y_made = sem("y_done"), sem("y_made")
        yh_made, yl_made, hot_t_made, late_added = sem("yh_made"), sem("yl_made"), sem("hot_t_made"), sem("late_added")
        late_placed = sem("late_placed")
        y_loaded = [sem(f"y_loaded{s}") for s in range(RAW_B)]
        acc_made, fin_sum, fin_root, fin_made, out_stored = (sem("acc_made"), sem("fin_sum"), sem("fin_root"),
                                                             sem("fin_made"), sem("out_stored"))

        x2 = x[0].rearrange("(t p) d -> t p d", p=P)
        out2 = out[0].rearrange("(t p) d -> t p d", p=P)
        win = w_in[0].rearrange("(k p) (n c) -> n p k c", p=P, c=256)
        wao = w_attn_out[0].rearrange("(k p) (n c) -> n p k c", p=P, c=512)
        wso = w_sgu_out[0].rearrange("(k p) (n c) -> n p k c", p=P, c=512)
        wmo = w_mix_out[0].rearrange("(k p) (n c) -> n p k c", p=P, c=256)
        hn_d = hn_dram.rearrange("(t p) d -> t p d", p=P)
        y_d = y_dram.rearrange("(r t p) d -> t p r d", r=TOPK, p=P)
        slope = [2.0 ** (-8.0 * (h + 1) / HEADS) for h in range(HEADS)]

        def piece_source(n):
            if n < N_IN:
                return win[n], 8
            if n < N_IN + 2:
                return wao[n - N_IN], 4
            if n < N_IN + 4:
                return wso[n - N_IN - 2], 4
            return wmo[n - N_IN - 4], 8

        def mix_slot(n):
            k = piece_source(n)[1]
            return (whi[n % SPLIT_A][:].rearrange("p (k c) -> p k c", k=k),
                    wlo[n % SPLIT_A][:].rearrange("p (k c) -> p k c", k=k))

        M0 = N_MIX
        H2_DONE = 4 + 2 * KD + D // 128
        task_piece = ([n for n in range(N_IN) for _ in range(2)] + [None] * 4
                      + [n for n in range(N_IN, N_IN + 4) for _ in range(4)]
                      + [n for n in range(N_IN + 4, N_MIX) for _ in range(2)])
        ends_piece = [p is not None and (i + 1 == len(task_piece) or task_piece[i + 1] != p) for i, p in enumerate(task_piece)]

        def y_load(i):
            return 2 * (i // 4) + i % 2, i // 2 % 2

        def y_slot(i):
            return (i + 4) % RAW_B

        def wait_task(eng, task):
            if ends_piece[task]:
                eng.wait_ge(piece_used, task_piece[task] + 1)
            else:
                eng.wait_ge(task_done, sum(not x for x in ends_piece[:task + 1]))

        sc_ps = {3: (4, 0), 2: (5, 0), 0: (5, 384), 1: (6, 0)}
        sc_sb = {0: 0, 1: 128, 2: 384, 3: 768}
        pt_at = {0: 0, 1: 512, 3: 896, 2: 1024}
        ps46 = ps[:, 4:7, :].rearrange("p b c -> p (b c)")
        gu_ps = ps[:, 0:4, :].rearrange("p b c -> p (b c)").rearrange("p (c two) -> p two c", two=2)
        t_ps = ps[:, 4:6, :].rearrange("p b c -> p (b c)")
        y_ps = ps[:, 6:8, :].rearrange("p b c -> p (b c)")

        block = ctx.enter_context(nc.Block())

        @block.sync
        def _(sp):
            def expert_source(e, j):
                if j < GU_P:
                    return w_gate_up[0][e, j * P:(j + 1) * P, :]
                return w_down[0][e, (j - GU_P) * 256:(j - GU_P + 1) * 256, :].rearrange("(p two) c -> p (two c)", two=2)

            for t in range(TT):
                sp.dma_start(x_in[:, t, :], x2[t]).then_inc(x_loaded[t], 16)
            sp.dma_start(gcol[:], mix_norm_g[0].rearrange("(k p) -> p k", p=P),
                         allow_slow_non_contiguous=True).then_inc(gcol_loaded, 16)
            for n in range(N_MIX):
                src, k = piece_source(n)
                if n >= RAW_A:
                    sp.wait_ge(low_made, n - RAW_A + 1)
                sp.dma_start(raw[n % RAW_A][:].rearrange("p (k c) -> p k c", k=k), src).then_inc(raw_landed[n % RAW_A], 16)
                if n == 2:
                    sp.dma_start(fcol[:], ffn_norm_g[0].rearrange("(k p) -> p k", p=P),
                                 allow_slow_non_contiguous=True).then_inc(consts_loaded, 16)
                    sp.dma_start(wsp[:], w_spatial[0].rearrange("g t s -> t g s")).then_inc(wsp_loaded, 16)
                    sp.dma_start(lng[:], sgu_ln_g[0].rearrange("(o c) -> o c", o=1)
                                 .broadcast_to((P, SGU_W))).then_inc(consts_loaded, 16)
                    sp.dma_start(lnb[:], sgu_ln_b[0].rearrange("(o c) -> o c", o=1)
                                 .broadcast_to((P, SGU_W))).then_inc(consts_loaded, 16)
                    for g in range(GROUPS):
                        q = (g % 2) * 64
                        sp.dma_start(bsp[q:q + 64, g // 2, :],
                                     b_spatial[0][g:g + 1, :].broadcast_to((64, P))).then_inc(consts_loaded, 16)
                    sp.dma_start(brow[:], b_router[0].rearrange("(o c) -> o c", o=1)
                                 .broadcast_to((P, E))).then_inc(consts_loaded, 16)
                if n == N_IN + 3:
                    sp.wait_ge(head_done, HEADS)
                    sp.dma_start(h2[:], x[0].rearrange("(t p) d -> p t d", p=P)).then_inc(x_again, 16)

            for m in range(EARLY + RAW_B):
                if m < RAW_A:
                    last = max(i for i in range(N_MIX) if i % RAW_A == m)
                    sp.wait_ge(low_made, last + 1)
                elif m < RAW_B:
                    sp.wait_ge(ml_made, KD)
                elif m < EARLY:
                    sp.wait_ge(bias_made, 2)
                else:
                    sp.wait_ge(low_made, M0 + m - EARLY + 1)
                s = m if m < EARLY else m % EARLY
                sp.dma_start(raw_b[s][:], expert_source(m // GU_P, m % GU_P)).then_inc(raw_landed[s], 16)

            def load(turn, j, expert):
                sp.wait_ge(low_made, (turn - 1) * PER_E + (M0 + GU_P + j - RAW_B + 1))
                sp.dma_start(raw_b[j % RAW_B][:], expert_source(expert, j % PER_E)).then_inc(raw_landed[j % RAW_B], 16)

            sp.wait_ge(tables_ready, 1)
            nb = sp.value_load(n_blocks[0:1, 0:1], min_val=E, max_val=E + MAX_OVER)
            with sp.Fori(1, nb - 1) as e:
                past = sp.value_load(expert_of[0:1, bass.ds(e - 1, 1)], min_val=0, max_val=E - 1)
                now = sp.value_load(expert_of[0:1, bass.ds(e, 1)], min_val=0, max_val=E - 1)
                after = sp.value_load(expert_of[0:1, bass.ds(e + 1, 1)], min_val=0, max_val=E - 1)
                for j in range(RAW_B, PER_E + RAW_B):
                    load(e, j, now if j < GU_P else past if j < PER_E else after)
            past = sp.value_load(expert_of[0:1, bass.ds(nb - 2, 1)], min_val=0, max_val=E - 1)
            last = sp.value_load(expert_of[0:1, bass.ds(nb - 1, 1)], min_val=0, max_val=E - 1)
            for j in range(RAW_B, PER_E):
                load(nb - 1, j, last if j < GU_P else past)
            for i in range(4):
                sp.wait_ge(low_made, nb * PER_E + (M0 + GU_P + i - PER_E - RAW_B + 1))
                sp.dma_start(raw_b[i][:], expert_source(last, GU_P + i)).then_inc(raw_landed[i], 16)
            sp.wait_ge(y_stored, nb * 16)
            for i in range(2 * TT):
                t, half = y_load(i)
                s = y_slot(i)
                if 2 <= i < RAW_B:
                    sp.wait_ge(low_made, nb * PER_E + (M0 - 4 + i - 1))
                elif i >= RAW_B:
                    sp.wait_ge(acc_made, 4)
                sp.dma_start(raw_b[s][:].rearrange("p (r d) -> p r d", r=2),
                             y_d[t][:, 2 * half:2 * half + 2, :]).then_inc(y_loaded[s], 16)
            for t in range(TT):
                sp.wait_ge(fin_made, t + 1)
                sp.dma_start(out2[t], h2[:, t, :]).then_inc(out_stored, 16)
            sp.wait_ge(out_stored, 16 * TT)

        @block.gpsimd
        def _(pool):
            made = [0]

            def step(ins, wait=True):
                made[0] += 1
                ins.then_inc(pool_made, 1)
                if wait:
                    pool.wait_ge(pool_made, made[0])

            step(nc.gpsimd.memset(ident[:], 0.0))
            step(nc.gpsimd.affine_select(out=ident[:], in_=ident[:], compare_op=ALU.not_equal, fill=1.0, base=0,
                                         pattern=[[-1, P]], channel_multiplier=1))
            step(nc.gpsimd.iota(dist[:], pattern=[[1, SEQ]], base=-(SEQ - P), channel_multiplier=-1,
                                allow_small_or_imprecise_dtypes=True))
            step(nc.gpsimd.affine_select(out=dist[:], in_=dist[:], compare_op=ALU.is_ge, fill=FAR, base=SEQ - P,
                                         pattern=[[-1, SEQ]], channel_multiplier=1))
            pool.wait_ge(wspT_made, 2)
            nc.gpsimd.affine_select(out=wspT[:], in_=wspT[:], compare_op=ALU.is_ge, fill=0.0, base=0,
                                    pattern=[[0, GROUPS], [1, P]], channel_multiplier=-1).then_inc(wsp_masked, 1)
            pool.wait_ge(piece_used, N_IN + 4)
            pool.dma_start(wr[:], w_router[0].rearrange("(k p) e -> p k e", p=P)).then_inc(wr_loaded, 16)
            for half in range(2):
                pool.dma_start(biasr[half * E:(half + 1) * E, 0:2 * D], b_gate_up[0]).then_inc(bias_loaded, 16)
                pool.dma_start(biasr[half * E:(half + 1) * E, 2 * D:3 * D], b_down[0]).then_inc(bias_loaded, 16)
            step(nc.gpsimd.iota(iota_e[:], pattern=[[1, 48]], base=0, channel_multiplier=0,
                                allow_small_or_imprecise_dtypes=True))
            step(nc.gpsimd.iota(iota_s[:], pattern=[[1, P]], base=0, channel_multiplier=0,
                                allow_small_or_imprecise_dtypes=True))
            step(nc.gpsimd.iota(pcol[:], pattern=[[1, 1]], base=0, channel_multiplier=1,
                                allow_small_or_imprecise_dtypes=True))
            step(nc.gpsimd.iota(kcol[:], pattern=[[1, TT], [TT, TOPK]], base=1, channel_multiplier=0,
                                allow_small_or_imprecise_dtypes=True))
            step(nc.gpsimd.memset(onesb[:], 1.0))
            step(nc.gpsimd.memset(ones_e[:], 1.0))
            step(nc.gpsimd.affine_select(out=before[:], in_=onesb[:], compare_op=ALU.is_gt, fill=0.0, base=0,
                                         pattern=[[1, P]], channel_multiplier=-1))
            pool.wait_ge(ml_made, KD)
            pool.dma_start(frow[:], ffn_norm_g[0].rearrange("(o c) -> o c", o=1).broadcast_to((P, D))).then_inc(frow_loaded, 16)
            step(nc.gpsimd.memset(selt[:], 0.0))
            step(nc.gpsimd.affine_select(out=selt[:], in_=selt[:], compare_op=ALU.not_equal, fill=1.0, base=0,
                                         pattern=[[-1, BLOCKS]], channel_multiplier=1))
            step(nc.gpsimd.affine_select(out=selt[:], in_=selt[:], compare_op=ALU.not_equal, fill=1.0, base=-E,
                                         pattern=[[-1, BLOCKS]], channel_multiplier=1))

            last_token = nc.gpsimd.to_reg(SEQ - 1)
            last_row = nc.gpsimd.to_reg(SEQ * TOPK - 1)

            def gather(b, copies):
                nc.gpsimd.tensor_copy(cur_x[:], xidx[:, bass.ds(b, 1)]).then_inc(idx_copied, 1)
                pool.wait_ge(idx_copied, copies)
                pool.sem_inc(idx_seen, 1)
                pool.indirect_dma_start(out=xgat[:], out_offset=None, in_=hn_dram,
                                        in_offset=bass.IndirectOffsetOnAxis(ap=cur_x[:, 0:1].bitcast(U32), axis=0),
                                        bounds_check=last_token, oob_is_err=False).then_inc(x_landed, 16)

            def scatter(b, copies):
                nc.gpsimd.tensor_copy(cur_y[:], yidx[:, bass.ds(b, 1)]).then_inc(idx_copied, 1)
                pool.wait_ge(idx_copied, copies)
                pool.sem_inc(idx_seen, 1)
                pool.indirect_dma_start(out=y_dram, out_offset=bass.IndirectOffsetOnAxis(ap=cur_y[:, 0:1].bitcast(U32), axis=0),
                                        in_=yb[:], in_offset=None,
                                        bounds_check=last_row, oob_is_err=False).then_inc(y_stored, 16)

            def select(dst, e, signal):
                nc.gpsimd.tensor_copy(dst[:], selt[:, bass.ds(e, 1)].broadcast_to((2 * E, P))).then_inc(signal, 1)

            select(selh, 0, selh_made)
            select(seld, 0, seld_made)
            for t in range(TT):
                pool.wait_ge(hn_made, t + 1)
                pool.dma_start(hn_d[t], hn[:, t, :]).then_inc(hn_stored, 16)
            step(nc.gpsimd.memset(xidx[:, BLOCKS:BLOCKS + 1], int(SKIP)))
            step(nc.gpsimd.memset(xgat[:], 0.0))
            pool.wait_ge(low_made, M0 + 1)

            def pool_low(m):
                pool.wait_ge(high_made, M0 + m + 1)
                nc.gpsimd.tensor_tensor(wlo_b[m][:], raw_b[m][:], whi_b[m][:].bitcast(F32), ALU.subtract).then_inc(low_made, 1)

            pool_low(1)
            pool.wait_ge(hot_b_made, 1)
            nc.gpsimd.tensor_tensor(hot_v[:, :, 48:96], hot_b[:], kcol[:].unsqueeze(2).broadcast_to((P, 16, 48)),
                                    ALU.mult).then_inc(hot_k_made, 1)
            pool.wait_ge(xidx_ready, 1)
            pool.wait_ge(hn_stored, 16 * TT)
            pool.indirect_dma_start(out=xgat[:], out_offset=None, in_=hn_dram,
                                    in_offset=bass.IndirectOffsetOnAxis(ap=xidx[:, 0:1].bitcast(U32), axis=0),
                                    bounds_check=last_token, oob_is_err=False).then_inc(x_landed, 16)
            pool_low(2)
            pool.wait_ge(x_turned, 1)
            gather(1, 1)
            pool.wait_ge(tables_ready, 1)
            nb = pool.value_load(n_blocks[0:1, 0:1], min_val=E, max_val=E + MAX_OVER)
            step(nc.gpsimd.memset(yb[:], 0.0))
            scatter(nb - 1, 2)
            pool.wait_ge(gu_done, 1)
            select(selh, 1, selh_made)
            pool.dma_start(gfin[:], final_norm_g.rearrange("(o c) -> o c", o=1).broadcast_to((P, D))).then_inc(bias_loaded, 16)
            nc.gpsimd.tensor_copy(xlast[:], xidx[:, bass.ds(nb - 1, 1)]).then_inc(pool_made, 1)
            nc.gpsimd.iota(iota_t[:], pattern=[[1, SEQ]], base=0, channel_multiplier=0,
                           allow_small_or_imprecise_dtypes=True).then_inc(pool_made, 1)
            pool.wait_ge(x_turned, 2)
            gather(2, 3)
            with pool.Fori(1, nb) as e:
                now = pool.value_load(expert_of[0:1, bass.ds(e, 1)], min_val=0, max_val=E - 1)
                after = pool.value_load(expert_of[0:1, bass.ds(e + 1, 1)], min_val=0, max_val=E - 1)
                pool.wait_ge(gu_done, e + 1)
                select(selh, after, selh_made)
                pool.wait_ge(x_turned, e + 2)
                pool.wait_ge(x_landed, e * 16 + 32)
                gather(e + 2, e * 2 + 2)
                pool.wait_ge(y_made, e)
                pool.wait_ge(y_stored, e * 16)
                scatter(e - 1, e * 2 + 3)
                select(seld, now, seld_made)
            pool.wait_ge(x_landed, nb * 16 + 32)

        @block.scalar
        def _(act):
            def mix_high(n):
                act.wait_ge(raw_landed[n % RAW_A], 16 * (n // RAW_A + 1))
                if n >= SPLIT_A:
                    act.wait_ge(piece_used, n - SPLIT_A + 1)
                nc.scalar.activation(whi[n % SPLIT_A][:], raw[n % RAW_A][:], ACT.Copy).then_inc(high_made, 1)

            for t in range(TT + 1):
                if t < TT:
                    act.wait_ge(x_loaded[t], 16)
                    nc.scalar.activation(xn[:, t, :], x_in[:, t, :], ACT.Square, accum_out=stat[:, t, 0:1]).then_inc(sum_made, 1)
                if t >= 1:
                    act.wait_ge(mean_made, t)
                    nc.scalar.activation(stat[:, t - 1, 2:3], stat[:, t - 1, 1:2], ACT.Sqrt).then_inc(root_made, 1)
            act.wait_ge(gcol_loaded, 16)
            mix_high(0)
            for k in range(KD):
                act.wait_ge(xT_turned, k + 1)
                nc.scalar.activation(xnh[:, k, :], ps[:, k, :], ACT.Copy, scale=gcol[:, k:k + 1]).then_inc(xnh_made, 1)
            mix_high(1)

            def spatial_weights():
                for c in range(2):
                    act.wait_ge(wsp_turned, c + 1)
                    nc.scalar.activation(wspT[:, 4 * c:4 * c + 4, :], ps[:, 4 + c, :].rearrange("p (g t) -> p g t", g=4),
                                         ACT.Copy).then_inc(wspT_made, 1)

            def evac(task):
                wait_task(act, task)
                n, c = task // 2, task % 2
                src = ps[:, task % 4, :]
                if n < 2:
                    nc.scalar.activation(qT[:, task, :], src, ACT.Copy, scale=HD ** -0.5).then_inc(act_evac, 1)
                elif n < 4:
                    nc.scalar.activation(kT[:, task - 4, :], src, ACT.Copy).then_inc(act_evac, 1)
                elif n < 6:
                    nc.scalar.activation(v[:, 2 * c:2 * c + 2, (n - 4) * 256:(n - 3) * 256],
                                         src.rearrange("p (t d) -> p t d", t=2), ACT.Copy).then_inc(act_evac, 1)
                elif n < 8:
                    nc.scalar.activation(u[:, task - 12, :], src, ACT.Gelu).then_inc(act_evac, 1)
                elif n < 10:
                    nc.scalar.activation(vv[:, 2 * c:2 * c + 2, (n - 8) * 256:(n - 7) * 256],
                                         src.rearrange("p (t d) -> p t d", t=2), ACT.Gelu).then_inc(act_evac, 1)
                else:
                    nc.scalar.activation(gates[:, task - 20, :], src, ACT.Copy).then_inc(act_evac, 1)

            for n in range(N_IN):
                if n >= 1:
                    mix_high(n + 1)
                if n == 1:
                    spatial_weights()
                evac(2 * n)
                ht, hs = n - 10, n - 9
                if ht >= 0:
                    act.wait_ge(prob_turned, ht + 1)
                    if ht >= 1:
                        act.wait_ge(head_done, ht)
                    nc.scalar.activation(probT[:], ps46[:, 0:1280], ACT.Copy).then_inc(probT_made, 1)
                evac(2 * n + 1)
                if n == 10:
                    act.wait_ge(ln_var, TT)
                    nc.scalar.activation(stat[:, :, 5:6], stat[:, :, 4:5], ACT.Sqrt).then_inc(ln_root, 1)
                if ht >= 0:
                    act.wait_ge(head_done, ht + 1)
                    q = (ht % 2) * 64
                    nc.scalar.activation(ah[q:q + 64, ht // 2, :], ps[q:q + 64, 7, :], ACT.Copy).then_inc(ah_made, 1)
                if 0 <= hs < HEADS:
                    for i in range(TT):
                        act.wait_ge(max_made, 4 * hs + i + 1)
                        a = sc_sb[i]
                        nc.scalar.activation(prob[:, a:a + P * (i + 1)], prob[:, a:a + P * (i + 1)], ACT.Exp,
                                             bias=negmax[:, hs % 2, i:i + 1],
                                             accum_out=rowsum[:, hs % 2, i:i + 1]).then_inc(exp_made, 1)
            act.wait_ge(act_evac, 2 * N_IN)
            mix_high(N_IN + 1)
            for c in range(4):
                act.wait_ge(sg_sum, c + 1)
                nc.scalar.activation(sgh[:, c, :], u[:, c, :], ACT.Copy).then_inc(sgh_made, 1)
                nc.scalar.activation(gates[:, 4 * c:4 * c + 4, :], gates[:, 4 * c:4 * c + 4, :], ACT.Sigmoid).then_inc(sigm_made, 1)
            mix_high(N_IN + 2)
            mix_high(N_IN + 3)
            for d in range(KD):
                if d == 4:
                    mix_high(N_IN + 4)
                act.wait_ge(merged, d + 1)
                nc.scalar.activation(xnh[:, d, :], gates[:, d, :], ACT.Copy).then_inc(mh_made, 1)
            mix_high(N_IN + 5)
            mix_high(N_IN + 6)
            act.wait_ge(bias_loaded, 16 * 4)
            nc.scalar.activation(bias[:], biasr[:], ACT.Copy).then_inc(bias_made, 1)
            mix_high(N_IN + 7)

            def high(j, s_raw, turns, free):
                act.wait_ge(raw_landed[s_raw], turns)
                act.wait_ge(piece_used, free)
                nc.scalar.activation(whi_b[j][:], raw_b[s_raw][:], ACT.Copy).then_inc(high_made, 1)

            mix_turns = [16 * len([i for i in range(N_MIX) if i % RAW_A == s]) if s < RAW_A else 0 for s in range(EARLY)]

            def first_high(m):
                high(m % SPLIT_B, m, mix_turns[m] + 16,
                     max(M0 - 2 + m + 1 if m < 2 else M0, M0 + m - SPLIT_B + 1))

            def square(t):
                nc.scalar.activation(hn[:, t, :], h2[:, t, :], ACT.Square, accum_out=stat[:, t, 0:1]).then_inc(h2_sum, 1)

            def turned(half):
                for b in range(4):
                    act.wait_ge(h2_turned, 4 * half + b + 1)
                    nc.scalar.activation(hT[:, 2 * b:2 * b + 2, half * 256:(half + 1) * 256],
                                         ps[:, 4 - 4 * half + b, :].rearrange("p (k s) -> p k s", k=2),
                                         ACT.Copy).then_inc(hT_made, 1)

            act.wait_ge(dve_evac, H2_DONE - 1)
            square(0)
            square(1)
            turned(0)
            first_high(0)
            act.wait_ge(dve_evac, H2_DONE)
            square(2)
            square(3)
            turned(1)
            act.wait_ge(h2_sum, 2 * TT)
            nc.scalar.activation(stat[:, :, 2:3], stat[:, :, 1:2], ACT.Sqrt).then_inc(h2_root, 1)
            act.wait_ge(rinv_made, 1)
            for t in range(TT):
                act.wait_ge(hg_made, t + 1)
                nc.scalar.activation(hn[:, t, :], hn[:, t, :], ACT.Copy, scale=stat[:, t, 3:4]).then_inc(hn_made, 1)
            first_high(1)
            first_high(2)
            first_high(3)
            act.wait_ge(exps_in, 1)
            nc.scalar.activation(topw[:], topw[:], ACT.Exp).then_inc(exps_out, 1)
            act.wait_ge(hot_b_made, 1)
            nc.scalar.activation(hot_v[:, :, 0:48], hot_b[:], ACT.Copy, scale=pcol[:, 0:1]).then_inc(hot_a_made, 1)

            def tokens_high(e):
                act.wait_ge(x_turned, e + 1)
                nc.scalar.activation(xth[:], t_ps.rearrange("p (k s) -> p k s", k=KD), ACT.Copy).then_inc(xth_made, 1)

            def hidden_high(e):
                act.wait_ge(hid_turned, e + 1)
                nc.scalar.activation(hth[:], t_ps.rearrange("p (k s) -> p k s", k=KD), ACT.Copy).then_inc(hth_made, 1)

            def sigmoid(e):
                act.wait_ge(gate_made, e + 1)
                nc.scalar.activation(sg[:], gm[:], ACT.Sigmoid, scale=ALPHA).then_inc(sig_made, 1)

            def rows(e, stored):
                act.wait_ge(y_done, e + 1)
                act.wait_ge(y_stored, stored)
                nc.scalar.activation(yb[:], y_ps, ACT.Copy).then_inc(y_made, 1)

            half = KD // 2
            act.wait_ge(half_turned, 1)
            nc.scalar.activation(xth[:, 0:half, :], t_ps[:, 0:half * P].rearrange("p (k s) -> p k s", k=half),
                                 ACT.Copy).then_inc(half_high, 1)
            act.wait_ge(x_turned, 1)
            nc.scalar.activation(xth[:, half:KD, :], t_ps[:, half * P:KD * P].rearrange("p (k s) -> p k s", k=half),
                                 ACT.Copy).then_inc(xth_made, 1)
            for m in range(4, GU_P):
                first_high(m)

            def loop_high(e, j):
                s_raw = j % RAW_B
                turns = mix_turns[s_raw] + 16 * (j // RAW_B + 2)
                act.wait_ge(raw_landed[s_raw], (e - 1) * (16 * PER_E // RAW_B) + turns)
                act.wait_ge(piece_used, (e - 1) * PER_E + (M0 + GU_P + j - SPLIT_B + 1))
                nc.scalar.activation(whi_b[(GU_P + j) % SPLIT_B][:], raw_b[s_raw][:], ACT.Copy).then_inc(high_made, 1)

            loop_high(1, 0)
            loop_high(1, 1)
            tokens_high(1)
            sigmoid(0)
            act.wait_ge(tables_ready, 1)
            nb = act.value_load(n_blocks[0:1, 0:1], min_val=E, max_val=E + MAX_OVER)
            with act.Fori(1, nb) as e:
                for j in range(PER_E):
                    loop_high(e, j + 2)
                    if j == 4:
                        hidden_high(e - 1)
                    if j == 8:
                        tokens_high(e + 1)
                    if j == 10:
                        sigmoid(e)
                rows(e - 1, e * 16)
            loop_high(nb, 2)
            hidden_high(nb - 1)
            loop_high(nb, 3)
            act.wait_ge(y_done, nb)
            nc.scalar.activation(yh[:], y_ps, ACT.Copy).then_inc(yh_made, 1)
            for t in range(TT):
                act.wait_ge(late_added, t + 1)
                nc.scalar.activation(gm[:], h2[:, t, :], ACT.Square, accum_out=stat[:, t, 0:1]).then_inc(fin_sum, 1)
                act.wait_ge(fin_sum, 2 * t + 2)
                nc.scalar.activation(stat[:, t, 2:3], stat[:, t, 1:2], ACT.Sqrt).then_inc(fin_root, 1)

        @block.vector
        def _(dve):
            steps = [0]

            def link(ins):
                steps[0] += 1
                ins.then_inc(dve_step, 1)
                dve.wait_ge(dve_step, steps[0])

            def mix_low(n):
                dve.wait_ge(high_made, n + 1)
                nc.vector.tensor_tensor(wlo[n % SPLIT_A][:], raw[n % RAW_A][:], whi[n % SPLIT_A][:].bitcast(F32),
                                        ALU.subtract).then_inc(low_made, 1)

            for t in range(TT + 1):
                if t < TT:
                    dve.wait_ge(sum_made, t + 1)
                    nc.vector.tensor_scalar(stat[:, t, 1:2], stat[:, t, 0:1], 1.0 / D, EPS,
                                            ALU.mult, ALU.add).then_inc(mean_made, 1)
                if t >= 1:
                    dve.wait_ge(root_made, t)
                    link(nc.vector.reciprocal(stat[:, t - 1, 3:4], stat[:, t - 1, 2:3]))
                    nc.vector.tensor_scalar(xn[:, t - 1, :], x_in[:, t - 1, :], stat[:, t - 1, 3:4], None,
                                            ALU.mult).then_inc(xn_made, 1)
            dve.wait_ge(gcol_loaded, 16)
            mix_low(0)
            for k in range(KD):
                dve.wait_ge(xnh_made, k + 1)
                nc.vector.scalar_tensor_tensor(out=xnl[:, k, :], in0=ps[:, k, :], scalar=gcol[:, k:k + 1],
                                               in1=xnh[:, k, :].bitcast(F32), op0=ALU.mult, op1=ALU.subtract).then_inc(xnl_made, 1)
            mix_low(1)
            dve.wait_ge(pool_made, DIST)
            dve.wait_ge(consts_loaded, CONSTS)
            for n in range(N_IN):
                if n >= 1:
                    mix_low(n + 1)
                ht, hs = n - 10, n - 9
                if n == 10:
                    dve.wait_ge(act_evac, 20)
                    for t in range(TT):
                        link(nc.vector.bn_stats(bn[:, t, :], vv[:, t, :]))
                        link(nc.vector.bn_aggr(mv[:, t, :], bn[:, t, :]))
                        nc.vector.tensor_scalar(stat[:, t, 4:5], mv[:, t, 1:2], EPS, None, ALU.add).then_inc(ln_var, 1)
                if n == 11:
                    dve.wait_ge(ln_root, 1)
                    link(nc.vector.reciprocal(stat[:, :, 6:7], stat[:, :, 5:6]))
                if 11 <= n < 11 + TT:
                    t = n - 11
                    link(nc.vector.tensor_scalar(vv[:, t, :], vv[:, t, :], mv[:, t, 0:1], stat[:, t, 6:7],
                                                 ALU.subtract, ALU.mult))
                    link(nc.vector.tensor_tensor(vv[:, t, :], vv[:, t, :], lng[:], ALU.mult))
                    nc.vector.tensor_tensor(vv[:, t, :], vv[:, t, :], lnb[:], ALU.add).then_inc(ln_made, 1)
                if 0 <= hs < HEADS:
                    dve.wait_ge(scores_ready, hs + 1)
                    for i in range(TT):
                        w, a = P * (i + 1), sc_sb[i]
                        bank, col = sc_ps[i]
                        link(nc.vector.scalar_tensor_tensor(out=prob[:, a:a + w], in0=dist[:, SEQ - w:SEQ], scalar=slope[hs],
                                                            in1=ps[:, bank, col:col + w], op0=ALU.mult, op1=ALU.add))
                        nc.vector.tensor_reduce(negmax[:, hs % 2, i:i + 1], prob[:, a:a + w], AX_X, ALU.max,
                                                negate=True).then_inc(max_made, 1)
                if ht >= 0:
                    dve.wait_ge(ah_made, ht + 1)
                    q = (ht % 2) * 64
                    nc.vector.tensor_tensor(al[q:q + 64, ht // 2, :], ps[q:q + 64, 7, :],
                                            ah[q:q + 64, ht // 2, :].bitcast(F32), ALU.subtract).then_inc(al_made, 1)
                if 0 <= hs < HEADS:
                    dve.wait_ge(exp_made, 4 * hs + 4)
                    link(nc.vector.reciprocal(rinv[:, hs % 2, :], rowsum[:, hs % 2, :]))
                    for i in range(TT):
                        w, a = P * (i + 1), sc_sb[i]
                        nc.vector.tensor_scalar(prob[:, a:a + w], prob[:, a:a + w], rinv[:, hs % 2, i:i + 1], None,
                                                ALU.mult).then_inc(prob_made, 1)
            def gated_low(g):
                dve.wait_ge(sgh_made, g + 1)
                nc.vector.tensor_tensor(sgl[:, g, :], u[:, g, :], sgh[:, g, :].bitcast(F32), ALU.subtract).then_inc(sgl_made, 1)

            for g in range(4):
                task = 2 * N_IN + g
                wait_task(dve, task)
                m4 = ps[:, task % 4, :].rearrange("p (c t) -> p c t", c=TT)
                mixed = (lng, lnb)[g % 2]
                nc.vector.tensor_tensor(mixed[:].rearrange("p (c t) -> p c t", c=TT), m4,
                                        bsp[:, g:g + 1, :].broadcast_to((P, TT, P)), ALU.add).then_inc(dve_evac, 1)
                dve.wait_ge(dve_evac, g + 1)
                nc.vector.tensor_tensor(u[:, g, :], u[:, g, :], mixed[:], ALU.mult).then_inc(sg_sum, 1)
                if g == 1:
                    mix_low(N_IN + 1)
                if g >= 1:
                    gated_low(g - 1)
            gated_low(3)
            for d in range(KD):
                task = 2 * N_IN + 4 + d
                dve.wait_ge(sigm_made, d // 4 + 1)
                wait_task(dve, task)
                nc.vector.tensor_tensor(gates[:, d, :], gates[:, d, :], ps[:, task % 4, :], ALU.mult).then_inc(dve_evac, 1)
                if d % 4 == 3:
                    mix_low(N_IN + 2 + d // 4)

            def merged_low(d):
                dve.wait_ge(mh_made, d + 1)
                nc.vector.tensor_tensor(xnl[:, d, :], gates[:, d, :], xnh[:, d, :].bitcast(F32), ALU.subtract).then_inc(ml_made, 1)

            for d in range(KD):
                if d == 4:
                    mix_low(N_IN + 4)
                task = 2 * N_IN + 12 + d
                dve.wait_ge(sigm_made, 2 + d // 4 + 1)
                wait_task(dve, task)
                nc.vector.tensor_tensor(gates[:, KD + d, :], gates[:, KD + d, :], ps[:, task % 4, :],
                                        ALU.mult).then_inc(dve_evac, 1)
                dve.wait_ge(dve_evac, 4 + KD + d + 1)
                nc.vector.tensor_tensor(gates[:, d, :], gates[:, d, :], gates[:, KD + d, :], ALU.add).then_inc(merged, 1)
                if d >= 1:
                    merged_low(d - 1)
            merged_low(KD - 1)
            mix_low(N_IN + 5)
            dve.wait_ge(x_again, 16)

            def residual(n, c):
                task = 2 * N_IN + 20 + 2 * n + c
                wait_task(dve, task)
                part = h2[:, 2 * c:2 * c + 2, n * 256:(n + 1) * 256]
                nc.vector.tensor_tensor(part, part, ps[:, task % 4, :].rearrange("p (t d) -> p t d", t=2),
                                        ALU.add).then_inc(dve_evac, 1)

            for n in range(4):
                residual(n, 0)
                if n == 3:
                    break
                residual(n, 1)
                if n < 2:
                    mix_low(N_IN + 6 + n)
                if n == 1:
                    dve.wait_ge(bias_made, 1)
                    nc.vector.tensor_tensor(bias[E:2 * E, :], biasr[E:2 * E, :], bias[E:2 * E, :].bitcast(F32),
                                            ALU.subtract).then_inc(bias_made, 1)
                    dve.wait_ge(wr_loaded, 16)
                    nc.vector.tensor_tensor(wr[:], wr[:], fcol[:].unsqueeze(2).broadcast_to((P, KD, E)),
                                            ALU.mult).then_inc(wr_scaled, 1)

            def low(s, s_raw, number):
                dve.wait_ge(high_made, number)
                nc.vector.tensor_tensor(wlo_b[s][:], raw_b[s_raw][:], whi_b[s][:].bitcast(F32), ALU.subtract).then_inc(low_made, 1)

            def first_low(m, before=0):
                if before:
                    dve.wait_ge(low_made, before)
                low(m % SPLIT_B, m, M0 + m + 1)

            def weighted(t):
                dve.wait_ge(h2_sum, t + 1)
                nc.vector.tensor_tensor(hn[:, t, :], h2[:, t, :], frow[:], ALU.mult).then_inc(hg_made, 1)

            def logits_turned(half):
                dve.wait_ge(lgT_done, half + 1)
                cols = slice(half * 256, (half + 1) * 256)
                nc.vector.tensor_copy(lgT[:, cols], ps[0:E, 4 + 3 * half, cols]).then_inc(lgT_made, 1)

            dve.wait_ge(frow_loaded, 16)
            weighted(0)
            weighted(1)
            first_low(0)
            residual(3, 1)
            for t in range(TT):
                dve.wait_ge(h2_sum, TT + t)
                nc.vector.tensor_scalar(stat[:, t, 1:2], stat[:, t, 0:1], 1.0 / D, EPS, ALU.mult, ALU.add).then_inc(h2_sum, 1)
            weighted(2)
            weighted(3)
            logits_turned(0)

            dve.wait_ge(h2_root, 1)
            nc.vector.reciprocal(stat[:, :, 3:4], stat[:, :, 2:3]).then_inc(rinv_made, 1)
            logits_turned(1)
            dve.wait_ge(rinv_made, 1)
            dve.wait_ge(logits_done, 1)
            dve.wait_ge(pool_made, ROUTE_CONSTS)
            for t in range(TT):
                ins = nc.vector.scalar_tensor_tensor(out=logits[:, t, :], in0=ps[:, 5, t * E:(t + 1) * E], scalar=stat[:, t, 3:4],
                                                     in1=brow[:], op0=ALU.mult, op1=ALU.add)
            link(ins)
            for t in range(TT):
                ins = nc.vector.max(top8[:, t, :], logits[:, t, :])
            link(ins)
            for t in range(TT):
                ins = nc.vector.max_index(idx8[:, t, :], top8[:, t, :], logits[:, t, :])
            link(ins)
            idxf3 = idxf[:].rearrange("p (t r) -> p t r", t=TT)
            link(nc.vector.tensor_copy(idxf3, idx8[:, :, 0:TOPK]))
            nc.vector.tensor_tensor(topw[:], top8[:, :, 0:TOPK], top8[:, :, 0:1].broadcast_to((P, TT, TOPK)),
                                    ALU.subtract).then_inc(exps_in, 1)
            link(nc.vector.tensor_tensor(pick[:], idxf[:].unsqueeze(2).broadcast_to((P, 16, E)),
                                         iota_e[:, 0:E].unsqueeze(1).broadcast_to((P, 16, E)), ALU.is_equal))
            with nc.allow_low_precision("zeros and ones are exact in bfloat16"):
                nc.vector.tensor_reduce(chosen[:], pick[:].rearrange("p (t r) e -> p t e r", t=TT),
                                        AX_X, ALU.add).then_inc(chosen_made, 1)
            dve.wait_ge(counted, 1)
            link(nc.vector.tensor_tensor(prod[:].rearrange("p (t r) e -> p t r e", t=TT),
                                         pick[:].rearrange("p (t r) e -> p t r e", t=TT),
                                         ps[:, 6, 0:TT * E].rearrange("p (t e) -> p t e", t=TT)
                                         .unsqueeze(2).broadcast_to((P, TT, TOPK, E)),
                                         ALU.mult))
            nc.vector.tensor_reduce(rpos[:], prod[:], AX_X, ALU.add)
            cnt = ps[:, 6, TT * E:TT * E + E]
            link(nc.vector.tensor_scalar(spill[:], cnt, float(P), None, ALU.is_gt))
            for q in (2, 3):
                link(nc.vector.scalar_tensor_tensor(out=spill[:], in0=cnt, scalar=float(P * q), in1=spill[:],
                                                    op0=ALU.is_gt, op1=ALU.add))
            link(nc.vector.tensor_tensor_scan(incl[:], ones_e[:], spill[:], 0.0, ALU.mult, ALU.add))
            link(nc.vector.scalar_tensor_tensor(out=first[:], in0=incl[:], scalar=float(E - 1), in1=spill[:],
                                                op0=ALU.add, op1=ALU.subtract))
            link(nc.vector.tensor_tensor(prod[:], pick[:], first[:].unsqueeze(1).broadcast_to((P, 16, E)), ALU.mult))
            nc.vector.tensor_reduce(rfirst[:], prod[:], AX_X, ALU.add)
            link(nc.vector.tensor_scalar(over[:], rpos[:], float(P), None, ALU.is_ge))
            link(nc.vector.scalar_tensor_tensor(out=lap[:], in0=rpos[:], scalar=float(P * 2), in1=over[:],
                                                    op0=ALU.is_ge, op1=ALU.add))
            link(nc.vector.scalar_tensor_tensor(out=lap[:], in0=rpos[:], scalar=float(P * 3), in1=lap[:],
                                                    op0=ALU.is_ge, op1=ALU.add))
            nc.vector.scalar_tensor_tensor(out=rslot[:], in0=lap[:], scalar=-float(P), in1=rpos[:], op0=ALU.mult, op1=ALU.add)
            link(nc.vector.tensor_tensor(rblk[:], lap[:], rfirst[:], ALU.add))
            link(nc.vector.tensor_tensor(rblk[:], rblk[:], idxf[:], ALU.subtract))
            link(nc.vector.tensor_tensor(rblk[:], rblk[:], over[:], ALU.mult))
            link(nc.vector.tensor_tensor(rblk[:], rblk[:], idxf[:], ALU.add))
            nc.vector.tensor_tensor(hot_b[:], rblk[:].unsqueeze(2).broadcast_to((P, 16, 48)),
                                    iota_e[:].unsqueeze(1).broadcast_to((P, 16, 48)), ALU.is_equal).then_inc(hot_b_made, 1)
            nc.vector.tensor_tensor(hot_s[:], rslot[:].unsqueeze(2).broadcast_to((P, 16, P)),
                                    iota_s[:].unsqueeze(1).broadcast_to((P, 16, P)), ALU.is_equal).then_inc(hot_s_made, 1)
            dve.wait_ge(exps_out, 1)
            link(nc.vector.tensor_reduce(wsum[:], topw[:], AX_X, ALU.add))
            link(nc.vector.reciprocal(wsum[:], wsum[:]))
            link(nc.vector.tensor_tensor(topw[:], topw[:], wsum[:].unsqueeze(2).broadcast_to((P, TT, TOPK)), ALU.mult))
            dve.wait_ge(table_done, 1)
            a_, b_ = ps[:, 7, 0:48], ps[:, 7, 48:96]
            nc.vector.tensor_scalar(skp[:], b_, 0.5, SKIP, ALU.is_lt, ALU.mult)
            link(nc.vector.tensor_scalar(rnk[:], b_, 4.5, None, ALU.is_gt))
            link(nc.vector.scalar_tensor_tensor(out=rnk[:], in0=b_, scalar=8.5, in1=rnk[:], op0=ALU.is_gt, op1=ALU.add))
            link(nc.vector.scalar_tensor_tensor(out=rnk[:], in0=b_, scalar=12.5, in1=rnk[:], op0=ALU.is_gt, op1=ALU.add))
            link(nc.vector.scalar_tensor_tensor(out=row[:], in0=b_, scalar=float(P), in1=skp[:], op0=ALU.mult, op1=ALU.add))
            link(nc.vector.scalar_tensor_tensor(out=row[:], in0=row[:], scalar=-float(P), in1=a_, op0=ALU.add, op1=ALU.add))
            nc.vector.scalar_tensor_tensor(out=xidx[:, 0:BLOCKS], in0=rnk[:], scalar=-float(SEQ), in1=row[:], op0=ALU.mult,
                                           op1=ALU.add).then_inc(xidx_ready, 1)
            nc.vector.tensor_copy(yidx[:], row[:])
            link(nc.vector.tensor_tensor(ended[:], incl[:].unsqueeze(1).broadcast_to((P, 16, E)),
                                         iota_e[:, 0:16].unsqueeze(2).broadcast_to((P, 16, E)), ALU.is_le))
            link(nc.vector.tensor_reduce(exf[:], ended[:], AX_X, ALU.add))
            nc.vector.tensor_scalar(expert_of[:, E:BLOCKS], exf[:], float(E - 1), None, ALU.min)
            nc.vector.tensor_copy(expert_of[:, 0:E], iota_e[:, 0:E])
            link(nc.vector.tensor_scalar(nbf[:], incl[:, E - 1:E], float(E), None, ALU.add))
            nc.vector.tensor_copy(n_blocks[:], nbf[:]).then_inc(tables_ready, 1)
            link(nc.vector.tensor_scalar(late[:], rblk[:], nbf[:, 0:1], -1.0, ALU.subtract, ALU.is_equal))
            topw16 = topw[:].rearrange("p t r -> p (t r)")
            link(nc.vector.tensor_tensor(late[:], late[:], topw16, ALU.mult))
            nc.vector.tensor_reduce(wlate[:], late[:].rearrange("p (t r) -> p t r", t=TT), AX_X, ALU.add)
            link(nc.vector.tensor_tensor(topw16, topw16, late[:], ALU.subtract))

            def tokens_low(e):
                dve.wait_ge(xth_made, e + 1)
                nc.vector.tensor_tensor(xtl[:], t_ps.rearrange("p (k s) -> p k s", k=KD), xth[:].bitcast(F32),
                                        ALU.subtract).then_inc(xtl_made, 1)

            def hidden_low(e):
                dve.wait_ge(hth_made, e + 1)
                nc.vector.tensor_tensor(htl[:], t_ps.rearrange("p (k s) -> p k s", k=KD), hth[:].bitcast(F32),
                                        ALU.subtract).then_inc(htl_made, 1)

            def gate(e):
                dve.wait_ge(gu_done, e + 1)
                nc.vector.tensor_scalar(gm[:], gu_ps[:, 0, :], LIMIT, None, ALU.min).then_inc(gate_made, 1)

            def up(e):
                nc.vector.tensor_scalar(um[:], gu_ps[:, 1, :], LIMIT, -LIMIT, ALU.min, ALU.max).then_inc(up_made, 1)

            def product(e):
                dve.wait_ge(up_made, e + 1)
                nc.vector.scalar_tensor_tensor(out=um[:], in0=um[:], scalar=1.0, in1=gm[:], op0=ALU.add,
                                               op1=ALU.mult).then_inc(gu_mult, 1)

            def hidden(e):
                dve.wait_ge(gu_mult, e + 1)
                dve.wait_ge(sig_made, e + 1)
                nc.vector.tensor_tensor(hid[:], um[:], sg[:], ALU.mult).then_inc(hid_made, 1)

            half = KD // 2
            dve.wait_ge(half_high, 1)
            nc.vector.tensor_tensor(xtl[:, 0:half, :], t_ps[:, 0:half * P].rearrange("p (k s) -> p k s", k=half),
                                    xth[:, 0:half, :].bitcast(F32), ALU.subtract).then_inc(half_low, 1)
            dve.wait_ge(xth_made, 1)
            nc.vector.tensor_tensor(xtl[:, half:KD, :], t_ps[:, half * P:KD * P].rearrange("p (k s) -> p k s", k=half),
                                    xth[:, half:KD, :].bitcast(F32), ALU.subtract).then_inc(xtl_made, 1)
            first_low(3, M0 + 3)
            for m in range(4, 8):
                first_low(m)

            def loop_low(e, j):
                s, s_raw = (GU_P + j) % SPLIT_B, j % RAW_B
                dve.wait_ge(high_made, (e - 1) * PER_E + (M0 + GU_P + j + 1))
                nc.vector.tensor_tensor(wlo_b[s][:], raw_b[s_raw][:], whi_b[s][:].bitcast(F32), ALU.subtract).then_inc(low_made, 1)

            loop_low(1, 0)
            loop_low(1, 1)
            gate(0)
            up(0)
            tokens_low(1)
            nb = dve.value_load(n_blocks[0:1, 0:1], min_val=E, max_val=E + MAX_OVER)
            with dve.Fori(1, nb) as e:
                for j in range(PER_E):
                    loop_low(e, j + 2)
                    if j == 0:
                        product(e - 1)
                    if j == 1:
                        hidden(e - 1)
                    if j == 4:
                        hidden_low(e - 1)
                    if j == 8:
                        tokens_low(e + 1)
                    if j == 9:
                        gate(e)
                    if j == 10:
                        up(e)
            product(nb - 1)
            hidden(nb - 1)
            loop_low(nb, 2)
            hidden_low(nb - 1)
            loop_low(nb, 3)
            dve.wait_ge(pool_made, LATE_CONSTS)
            nc.vector.tensor_scalar(hot_t[:], iota_t[:], xlast[:, 0:1], None, ALU.is_equal).then_inc(hot_t_made, 1)

            def halves_of_last():
                dve.wait_ge(yh_made, 1)
                nc.vector.tensor_tensor(yl[:], y_ps, yh[:].bitcast(F32), ALU.subtract).then_inc(yl_made, 1)

            def final_norm(t):
                dve.wait_ge(fin_sum, 2 * t + 1)
                nc.vector.tensor_scalar(stat[:, t, 1:2], stat[:, t, 0:1], 1.0 / D, EPS, ALU.mult, ALU.add).then_inc(fin_sum, 1)
                dve.wait_ge(fin_root, t + 1)
                link(nc.vector.reciprocal(stat[:, t, 3:4], stat[:, t, 2:3]))
                nc.vector.scalar_tensor_tensor(out=h2[:, t, :], in0=h2[:, t, :], scalar=stat[:, t, 3:4], in1=gfin[:],
                                               op0=ALU.mult, op1=ALU.mult).then_inc(fin_made, 1)

            def add_last(t):
                dve.wait_ge(late_placed, t + 1)
                dve.wait_ge(acc_made, 8 * (t // 2) + 8)
                nc.vector.scalar_tensor_tensor(out=h2[:, t, :], in0=ps[:, 2 * t:2 * t + 2, :].rearrange("p b c -> p (b c)"),
                                               scalar=wlate[:, t:t + 1], in1=h2[:, t, :], op0=ALU.mult,
                                               op1=ALU.add).then_inc(late_added, 1)

            dve.wait_ge(bias_loaded, 16 * 5)
            for pair in range(TT // 2):
                for i in range(4 * pair, 4 * pair + 4, 2):
                    for r2 in range(2):
                        for n in (i, i + 1):
                            t, half = y_load(n)
                            if r2 == 0:
                                dve.wait_ge(y_loaded[y_slot(n)], 16 * (n // RAW_B + 1))
                            number = 2 * i + 2 * r2 + n - i
                            if number >= 8 * pair + 2:
                                dve.wait_ge(acc_made, number - 1)
                            rank = 2 * half + r2
                            nc.vector.scalar_tensor_tensor(out=h2[:, t, :], in0=raw_b[y_slot(n)][:, r2 * D:(r2 + 1) * D],
                                                           scalar=topw[:, t, rank:rank + 1], in1=h2[:, t, :], op0=ALU.mult,
                                                           op1=ALU.add).then_inc(acc_made, 1)
                if pair == 0:
                    halves_of_last()
                add_last(2 * pair)
                add_last(2 * pair + 1)
                final_norm(2 * pair)
                final_norm(2 * pair + 1)

        @block.tensor
        def _(pe):
            def three(out_ap, sta, mov, first, last):
                nc.tensor.matmul(out_ap, sta[0], mov[0], start=first, stop=False)
                nc.tensor.matmul(out_ap, sta[0], mov[1], start=False, stop=False)
                return nc.tensor.matmul(out_ap, sta[1], mov[0], start=False, stop=last)

            def wait_bank(task):
                if task < 4:
                    return
                if task - 4 < 2 * N_IN:
                    pe.wait_ge(act_evac, task - 3)
                else:
                    pe.wait_ge(dve_evac, task - 4 - 2 * N_IN + 1)

            def turned_task(n, c, task, mov, kt, col):
                wait_bank(task)
                hi, lo = mix_slot(n)
                for k in range(kt):
                    if task == 0:
                        pe.wait_ge(xnl_made, k + 1)
                    ins = three(ps[:, task % 4, :], (hi[:, k, col:col + P], lo[:, k, col:col + P]),
                                (mov[0][:, k, :], mov[1][:, k, :]), k == 0, k == kt - 1)
                ins.then_inc(piece_used if ends_piece[task] else task_done, 1)

            def token_task(n, c, task):
                wait_bank(task)
                hi, lo = mix_slot(n)
                for i in range(2):
                    if task == len(task_piece) - 1 and i == 1:
                        turn_h2(0)
                    tok = slice((2 * c + i) * P, (2 * c + i + 1) * P)
                    for k in range(KD):
                        if n == N_IN + 4 and c == 0 and i == 0:
                            pe.wait_ge(ml_made, k + 1)
                        ins = three(ps[:, task % 4, i * 256:(i + 1) * 256], (xnh[:, k, tok], xnl[:, k, tok]),
                                    (hi[:, k, :], lo[:, k, :]), k == 0, k == KD - 1)
                ins.then_inc(piece_used if ends_piece[task] else task_done, 1)

            def turn_h2(half):
                pe.wait_ge(dve_evac, H2_DONE - 1 + half)
                for b in range(4):
                    for k in (2 * b, 2 * b + 1):
                        for i in range(2):
                            a = (k % 2) * 256 + i * P
                            ins = nc.tensor.transpose(ps[:, 4 - 4 * half + b, a:a + P],
                                                      h2[:, 2 * half + i, k * P:(k + 1) * P], ident[:])
                    ins.then_inc(h2_turned, 1)

            pe.wait_ge(pool_made, IDENT)
            for t in range(TT):
                pe.wait_ge(xn_made, t + 1)
                for k in range(KD):
                    ins = nc.tensor.transpose(ps[:, k, t * P:(t + 1) * P], xn[:, t, k * P:(k + 1) * P], ident[:])
                    if t == TT - 1:
                        ins.then_inc(xT_turned, 1)

            def turn_spatial():
                pe.wait_ge(wsp_loaded, 16)
                for c in range(2):
                    for g in range(4):
                        ins = nc.tensor.transpose(ps[:, 4 + c, g * P:(g + 1) * P], wsp[:, 4 * c + g, :], ident[:])
                    ins.then_inc(wsp_turned, 1)

            def scores(h):
                pe.wait_ge(act_evac, 8)
                if h == 0:
                    pe.wait_ge(wspT_made, 2)
                else:
                    pe.wait_ge(probT_made, h)
                q, pair = (h % 2) * 64, h // 2
                for i in (3, 2, 0, 1):
                    bank, col = sc_ps[i]
                    w = P * (i + 1)
                    ins = nc.tensor.matmul(ps[:, bank, col:col + w], qT[q:q + 64, pair, i * P:(i + 1) * P],
                                           kT[q:q + 64, pair, 0:w], start=True, stop=True)
                ins.then_inc(scores_ready, 1)

            def turn_prob(h):
                for i in range(TT):
                    pe.wait_ge(prob_made, 4 * h + i + 1)
                    for j in range(i + 1):
                        a = pt_at[j] + (i - j) * P
                        ins = nc.tensor.transpose(ps46[:, a:a + P], prob[:, sc_sb[i] + j * P:sc_sb[i] + (j + 1) * P], ident[:])
                ins.then_inc(prob_turned, 1)

            def weigh(h):
                pe.wait_ge(probT_made, h + 1)
                pe.wait_ge(act_evac, 12)
                if h >= 1:
                    pe.wait_ge(al_made, h)
                q = (h % 2) * 64
                for j in range(TT):
                    ins = nc.tensor.matmul(ps[q:q + 64, 7, j * P:SEQ], v[:, j, h * HD:(h + 1) * HD],
                                           probT[:, pt_at[j]:pt_at[j] + SEQ - j * P], start=(j == 0), stop=(j == TT - 1))
                ins.then_inc(head_done, 1)

            xT = (xnh, xnl)
            for n in range(N_IN):
                pe.wait_ge(low_made, n + 1)
                by_token = 4 <= n < 6 or 8 <= n < 10
                for c in range(2):
                    if by_token:
                        token_task(n, c, 2 * n + c)
                    else:
                        turned_task(n, c, 2 * n + c, xT, KD, c * P)
                    if c == 0 and n >= 10:
                        turn_prob(n - 10)
                if n == 0:
                    turn_spatial()
                if 0 <= n - 9 < HEADS:
                    scores(n - 9)
                if n >= 10:
                    weigh(n - 10)
            pe.wait_ge(ln_made, TT)
            pe.wait_ge(wsp_masked, 1)
            for g in range(4):
                task = 2 * N_IN + g
                wait_bank(task)
                for c in range(TT):
                    for half in range(2):
                        q = half * 64
                        ins = nc.tensor.matmul(ps[q:q + 64, task % 4, c * P:(c + 1) * P],
                                               vv[:, c, (2 * g + half) * 64:(2 * g + half + 1) * 64],
                                               wspT[:, 2 * g + half, :], start=True, stop=True)
                ins.then_inc(task_done, 1)
            for n in range(N_IN, N_IN + 4):
                attn = n < N_IN + 2
                pe.wait_ge(low_made, n + 1)
                if n == N_IN:
                    pe.wait_ge(al_made, HEADS)
                if n == N_IN + 2:
                    pe.wait_ge(sgl_made, 4)
                for c in range(4):
                    turned_task(n, c, 2 * N_IN + 4 + 4 * (n - N_IN) + c, (ah, al) if attn else (sgh, sgl), 4, c * P)
            for n in range(N_IN + 4, N_MIX):
                pe.wait_ge(low_made, n + 1)
                for c in range(2):
                    token_task(n, c, 2 * N_IN + 20 + 2 * (n - N_IN - 4) + c)

            pe.wait_ge(wr_scaled, 1)
            for half in range(2):
                if half == 1:
                    turn_h2(1)
                for k in range(KD):
                    pe.wait_ge(hT_made, 4 * half + k // 2 + 1)
                    cols = slice(half * 256, (half + 1) * 256)
                    ins = nc.tensor.matmul(ps[0:E, 4 + 3 * half, cols], wr[:, k, :], hT[:, k, cols],
                                           start=(k == 0), stop=(k == KD - 1))
                ins.then_inc(lgT_done, 1)
            for t in range(TT):
                pe.wait_ge(lgT_made, t // 2 + 1)
                ins = nc.tensor.transpose(ps[:, 5, t * E:(t + 1) * E], lgT[:, t * P:(t + 1) * P], ident[0:E, 0:E])
            ins.then_inc(logits_done, 1)
            pe.wait_ge(chosen_made, 1)
            for t in range(TT):
                dst = ps[:, 6, t * E:(t + 1) * E]
                for s in range(t):
                    nc.tensor.matmul(dst, onesb[:], chosen[:, s, :], start=(s == 0), stop=False)
                nc.tensor.matmul(dst, before[:], chosen[:, t, :], start=(t == 0), stop=True)
            for s in range(TT):
                ins = nc.tensor.matmul(ps[:, 6, TT * E:TT * E + E], onesb[:], chosen[:, s, :], start=(s == 0), stop=(s == TT - 1))
            ins.then_inc(counted, 1)
            pe.wait_ge(hot_s_made, 1)
            pe.wait_ge(hot_a_made, 1)
            pe.wait_ge(hot_k_made, 1)
            for i in range(16):
                ins = nc.tensor.matmul(ps[:, 7, 0:96], hot_s[:, i, :], hot_v[:, i, :], start=(i == 0), stop=(i == 15))
            ins.then_inc(table_done, 1)

            def turn_tokens(landed, used):
                pe.wait_ge(x_landed, landed)
                if used is not None:
                    pe.wait_ge(htl_made, used)
                for k in range(KD):
                    ins = nc.tensor.transpose(t_ps[:, k * P:(k + 1) * P], xgat[:, k * P:(k + 1) * P], ident[:])
                ins.then_inc(x_turned, 1)

            def turn_hidden(e, tokens):
                pe.wait_ge(hid_made, e + 1)
                pe.wait_ge(xtl_made, tokens)
                for k in range(KD):
                    a = (k // 2) * 256 + k % 2
                    ins = nc.tensor.transpose(t_ps[:, k * P:(k + 1) * P], hid[:, a:a + 255:2], ident[:])
                ins.then_inc(hid_turned, 1)

            def gate_up_ready(e, tokens):
                pe.wait_ge(xtl_made, tokens)
                pe.wait_ge(gate_made, e)
                pe.wait_ge(up_made, e)

            def gate_up_bias(sel):
                pe.wait_ge(selh_made, sel)
                for q in range(4):
                    ins = nc.tensor.matmul(ps[:, q, :], selh[:], bias[:, q * 512:(q + 1) * 512], start=False, stop=True)
                ins.then_inc(gu_done, 1)

            def gate_up_piece(j, s, number):
                pe.wait_ge(low_made, number)
                for q in range(4):
                    cols = slice(q * 512, (q + 1) * 512)
                    ins = three(ps[:, q, :], (xth[:, j, :], xtl[:, j, :]), (whi_b[s][:, cols], wlo_b[s][:, cols]),
                                j == 0, False)
                ins.then_inc(piece_used, 1)

            def down_ready(halves):
                pe.wait_ge(htl_made, halves)

            def down_bias(sel):
                pe.wait_ge(seld_made, sel)
                for q in range(2):
                    ins = nc.tensor.matmul(ps[:, 6 + q, :], seld[:], bias[:, 2 * D + q * 512:2 * D + (q + 1) * 512],
                                           start=False, stop=True)
                ins.then_inc(y_done, 1)

            def down_piece(i, s, number):
                pe.wait_ge(low_made, number)
                for two in range(2):
                    k = 2 * i + two
                    for q in range(2):
                        cols = slice(two * D + q * 512, two * D + (q + 1) * 512)
                        ins = three(ps[:, 6 + q, :], (hth[:, k, :], htl[:, k, :]), (whi_b[s][:, cols], wlo_b[s][:, cols]),
                                    k == 0, False)
                ins.then_inc(piece_used, 1)

            pe.wait_ge(bias_made, 2)
            pe.wait_ge(x_landed, 16)
            for k in range(KD):
                ins = nc.tensor.transpose(t_ps[:, k * P:(k + 1) * P], xgat[:, k * P:(k + 1) * P], ident[:])
                if k == KD // 2 - 1:
                    ins.then_inc(half_turned, 1)
            ins.then_inc(x_turned, 1)
            for j in range(GU_P):
                if j == 0:
                    pe.wait_ge(half_low, 1)
                if j == KD // 2:
                    pe.wait_ge(xtl_made, 1)
                gate_up_piece(j, j % SPLIT_B, M0 + j + 1)
            gate_up_bias(1)
            turn_tokens(32, None)
            pe.wait_ge(tables_ready, 1)
            nb = pe.value_load(n_blocks[0:1, 0:1], min_val=E, max_val=E + MAX_OVER)
            with pe.Fori(1, nb) as e:
                gate_up_ready(e, e + 1)
                for j in range(PER_E):
                    number = (e - 1) * PER_E + (M0 + GU_P + j + 1)
                    if j == 4:
                        turn_hidden(e - 1, e + 1)
                    if j == GU_P:
                        gate_up_bias(e + 1)
                        turn_tokens(e * 16 + 32, e)
                        down_ready(e)
                    if j < GU_P:
                        gate_up_piece(j, (GU_P + j) % SPLIT_B, number)
                    else:
                        down_piece(j - GU_P, (GU_P + j) % SPLIT_B, number)
                down_bias(e)
            turn_hidden(nb - 1, nb + 1)
            down_ready(nb)
            for i in range(4):
                down_piece(i, (GU_P + i) % SPLIT_B, nb * PER_E + (M0 + GU_P - PER_E + i + 1))
            down_bias(nb)
            pe.wait_ge(hot_t_made, 1)
            pe.wait_ge(up_made, nb)
            pe.wait_ge(yl_made, 1)
            for t in range(TT):
                for q in range(2):
                    cols = slice(q * 512, (q + 1) * 512)
                    nc.tensor.matmul(ps[:, 2 * t + q, :], hot_t[:, t * P:(t + 1) * P], yh[:, cols], start=True, stop=False)
                    ins = nc.tensor.matmul(ps[:, 2 * t + q, :], hot_t[:, t * P:(t + 1) * P], yl[:, cols], start=False, stop=True)
                ins.then_inc(late_placed, 1)


_INS = ["x", "mix_norm_g", "w_in", "w_attn_out", "sgu_ln_g", "sgu_ln_b", "w_spatial", "b_spatial", "w_sgu_out", "w_mix_out",
        "ffn_norm_g", "w_router", "b_router", "w_gate_up", "b_gate_up", "w_down", "b_down", "final_norm_g"]


def kernel(**inputs):
    import numpy as np
    import concourse.bacc as bacc
    from concourse.bass_utils import run_bass_kernel_spmd

    nc = bacc.Bacc("TRN2", target_bir_lowering=False, num_devices=1)
    arrays, args = {}, []
    for name in _INS:
        a = np.ascontiguousarray(inputs[name])
        arrays[f"in_{name}"] = a
        args.append(nc.dram_tensor(f"in_{name}", a.shape, mybir.dt.from_np(a.dtype), kind="ExternalInput").ap())
    args.append(nc.dram_tensor("out_0", (1, SEQ, D), F32, kind="ExternalOutput").ap())
    build(nc, *args)
    r = run_bass_kernel_spmd(nc, [arrays], core_ids=[0])
    return r.results[0]["out_0"]
```
